# Optimizing a Trainium2 kernel written in Bass

```python
import math
import jax
import jax.numpy as jnp
from jax import lax
import numpy as np

D_MODEL = 1024
BATCH = 1
SEQ = 256
DEPTH = 2

EPS = 1e-6
M_HEADS = 4
M_DH = D_MODEL // 8
M_W = M_HEADS * M_DH
M_CHUNK = 128
CONV_K = 4
B_HEADS = 8
B_DH = D_MODEL // 16
B_W = B_HEADS * B_DH
MOBA_BLOCK = 256
MOBA_TOPK = 3
MOBA_QCHUNK = 64
C_HEADS = 8
C_DH = D_MODEL // 16
C_VDH = 2 * C_DH
C_W = C_HEADS * C_VDH
C_QBLOCK = 128
PEER_HEADS = 8
PEER_NKEYS = 128
PEER_N = PEER_NKEYS * PEER_NKEYS
PEER_DK = 256
PEER_TOPK = 16
PEER_TOK_CHUNK = 128

IN_EVEN = 4 * M_W + 2 * M_HEADS + 3 * B_W
MIX_EVEN = M_W + B_W
IN_ODD = 4 * C_HEADS * C_DH + C_HEADS * C_VDH
N_EVEN = (DEPTH + 1) // 2
N_ODD = DEPTH // 2


def rms_norm(x, g):
    xf = x.astype(jnp.float32)
    y = xf * lax.rsqrt(jnp.mean(xf * xf, axis=-1, keepdims=True) + EPS)
    return (y * g.astype(jnp.float32)).astype(x.dtype)

def alibi_slopes(n_heads):
    return jnp.asarray([2.0 ** (-8.0 * (h + 1) / n_heads) for h in range(n_heads)], dtype=jnp.float32)

def causal_depthwise_conv(x, w):
    ch = x.shape[-1]
    return lax.conv_general_dilated(x, w.astype(x.dtype)[:, None, :], window_strides=(1,),
                                    padding=[(CONV_K - 1, 0)],
                                    dimension_numbers=('NWC', 'WIO', 'NWC'),
                                    feature_group_count=ch)

def to_heads(t, n_heads):
    bn, s, _ = t.shape
    return t.reshape(bn, s, n_heads, -1).transpose(0, 2, 1, 3)

def from_heads(t):
    bn, h, s, dh = t.shape
    return t.transpose(0, 2, 1, 3).reshape(bn, s, h * dh)

def mlstm_chunkwise(q, k, v, i_pre, f_pre):
    f32 = jnp.float32
    bn, nh, s, dh = q.shape
    L = M_CHUNK
    nc = s // L
    q = q.astype(f32).reshape(bn, nh, nc, L, dh)
    k = (k.astype(f32) * dh ** -0.5).reshape(bn, nh, nc, L, dh)
    v = v.astype(f32).reshape(bn, nh, nc, L, dh)
    ig = i_pre.astype(f32).reshape(bn, nh, nc, L)
    b = jnp.cumsum(jax.nn.log_sigmoid(f_pre.astype(f32)).reshape(bn, nh, nc, L), axis=-1)
    b_end = b[..., -1]
    w_end = b_end[..., None] - b + ig
    m_loc = jnp.max(w_end, axis=-1)
    e_end = jnp.exp(w_end - m_loc[..., None])
    c_loc = jnp.einsum('bhcl,bhcld,bhcle->bhcde', e_end, k, v)
    n_loc = jnp.einsum('bhcl,bhcld->bhcd', e_end, k)

    def step(carry, inp):
        c_st, n_st, m_st = carry
        be, cl, nl, ml = inp
        m_new = jnp.maximum(be + m_st, ml)
        a = jnp.exp(be + m_st - m_new)
        sc = jnp.exp(ml - m_new)
        c_new = a[..., None, None] * c_st + sc[..., None, None] * cl
        n_new = a[..., None] * n_st + sc[..., None] * nl
        return (c_new, n_new, m_new), (c_st, n_st, m_st)

    init = (jnp.zeros((bn, nh, dh, dh), f32), jnp.zeros((bn, nh, dh), f32), jnp.zeros((bn, nh), f32))
    xs = tuple(jnp.moveaxis(t, 2, 0) for t in (b_end, c_loc, n_loc, m_loc))
    _, (c_prev, n_prev, m_prev) = lax.scan(step, init, xs)
    c_prev = jnp.moveaxis(c_prev, 0, 2)
    n_prev = jnp.moveaxis(n_prev, 0, 2)
    m_prev = jnp.moveaxis(m_prev, 0, 2)
    causal = jnp.tril(jnp.ones((L, L), dtype=bool))
    log_d = jnp.where(causal, b[..., :, None] - b[..., None, :] + ig[..., None, :], -jnp.inf)
    a_inter = b + m_prev[..., None]
    m_t = jnp.maximum(a_inter, jnp.max(log_d, axis=-1))
    w_inter = jnp.exp(a_inter - m_t)
    s_intra = jnp.einsum('bhcld,bhcsd->bhcls', q, k) * jnp.exp(log_d - m_t[..., None])
    num = (w_inter[..., None] * jnp.einsum('bhcld,bhcde->bhcle', q, c_prev)
           + jnp.einsum('bhcls,bhcse->bhcle', s_intra, v))
    den = w_inter * jnp.einsum('bhcld,bhcd->bhcl', q, n_prev) + jnp.sum(s_intra, axis=-1)
    h = num / jnp.maximum(jnp.abs(den), jnp.exp(-m_t))[..., None]
    return h.reshape(bn, nh, s, dh)

def moba_attention(q, k, v, slopes):
    f32 = jnp.float32
    bn, nh, s, dh = q.shape
    bs = MOBA_BLOCK
    nb = -(-s // bs)
    pad = nb * bs - s
    scale = dh ** -0.5
    q = q.astype(f32)
    k_blk = jnp.pad(k.astype(f32), ((0, 0), (0, 0), (0, pad), (0, 0))).reshape(bn, nh, nb, bs, dh)
    v_blk = jnp.pad(v.astype(f32), ((0, 0), (0, 0), (0, pad), (0, 0))).reshape(bn, nh, nb, bs, dh)
    k_sel_n = min(MOBA_TOPK, nb - 1)
    if k_sel_n > 0:
        gate = jnp.einsum('bhsd,bhnd->bhsn', q, jnp.mean(k_blk, axis=3))
        fully_past = jnp.arange(nb)[None, :] < (jnp.arange(s) // bs)[:, None]
        gate = jnp.where(fully_past, gate, -jnp.inf)
        gate_val, sel = lax.top_k(gate, k_sel_n)
        sel_ok = jnp.isfinite(gate_val)
    b_idx = jnp.arange(bn)[:, None, None, None]
    h_idx = jnp.arange(nh)[None, :, None, None]
    qc_n = MOBA_QCHUNK

    def one_chunk(ci):
        t0 = ci * qc_n
        qc = lax.dynamic_slice_in_dim(q, t0, qc_n, axis=2)
        tq = t0 + jnp.arange(qc_n)
        j = t0 // bs
        k_own = lax.dynamic_index_in_dim(k_blk, j, axis=2, keepdims=False)
        v_own = lax.dynamic_index_in_dim(v_blk, j, axis=2, keepdims=False)
        dist_own = (tq[:, None] - (j * bs + jnp.arange(bs))[None, :]).astype(f32)
        logit_own = jnp.einsum('bhqd,bhkd->bhqk', qc, k_own) * scale - slopes[:, None, None] * dist_own
        logit_own = jnp.where(dist_own >= 0, logit_own, -jnp.inf)
        if k_sel_n == 0:
            p = jax.nn.softmax(logit_own, axis=-1)
            return jnp.einsum('bhqk,bhkd->bhqd', p, v_own)
        sc = lax.dynamic_slice_in_dim(sel, t0, qc_n, axis=2)
        ok = lax.dynamic_slice_in_dim(sel_ok, t0, qc_n, axis=2)
        k_g = k_blk[b_idx, h_idx, sc]
        v_g = v_blk[b_idx, h_idx, sc]
        dist_g = (tq[:, None, None] - (sc[..., None] * bs + jnp.arange(bs))).astype(f32)
        logit_g = jnp.einsum('bhqd,bhqnkd->bhqnk', qc, k_g) * scale - slopes[:, None, None, None] * dist_g
        logit_g = jnp.where(ok[..., None], logit_g, -jnp.inf)
        logits = jnp.concatenate([logit_g.reshape(bn, nh, qc_n, k_sel_n * bs), logit_own], axis=-1)
        p = jax.nn.softmax(logits, axis=-1)
        p_g = p[..., :k_sel_n * bs].reshape(bn, nh, qc_n, k_sel_n, bs)
        p_own = p[..., k_sel_n * bs:]
        return jnp.einsum('bhqnk,bhqnkd->bhqd', p_g, v_g) + jnp.einsum('bhqk,bhkd->bhqd', p_own, v_own)

    out = lax.map(one_chunk, jnp.arange(s // qc_n))
    return out.transpose(1, 2, 0, 3, 4).reshape(bn, nh, s, dh)

def diff_attention(q, k, v, lam, slopes):
    f32 = jnp.float32
    bn, nh, _, s, dh = q.shape
    scale = dh ** -0.5
    qf = q.astype(f32)
    kf = k.astype(f32)
    vf = v.astype(f32)
    kpos = jnp.arange(s)
    qb_n = C_QBLOCK

    def one_block(ci):
        t0 = ci * qb_n
        qb = lax.dynamic_slice_in_dim(qf, t0, qb_n, axis=3)
        dist = ((t0 + jnp.arange(qb_n))[:, None] - kpos[None, :]).astype(f32)
        logits = jnp.einsum('bhcqd,bhckd->bhcqk', qb, kf) * scale - slopes[:, None, None, None] * dist
        logits = jnp.where(dist >= 0, logits, -jnp.inf)
        p = jax.nn.softmax(logits, axis=-1)
        return jnp.einsum('bhqk,bhkd->bhqd', p[:, :, 0] - lam * p[:, :, 1], vf)

    out = lax.map(one_block, jnp.arange(s // qb_n))
    return out.transpose(1, 2, 0, 3, 4).reshape(bn, nh, s, v.shape[-1])

def mlstm_moba_mixer(h, w_in, conv_w, igate_b, fgate_b, mnorm_g, qn_g, kn_g, w_out):
    f32 = jnp.float32
    z = h @ w_in
    offs = np.cumsum([M_W, M_W, M_W, M_W, M_HEADS, M_HEADS, B_W, B_W]).tolist()
    mq, mk, mv, mo, mi, mf, bq, bk, bv = jnp.split(z, offs, axis=-1)
    qk = jax.nn.silu(causal_depthwise_conv(jnp.concatenate([mq, mk], axis=-1), conv_w))
    mq, mk = qk[..., :M_W], qk[..., M_W:]
    i_pre = (mi + igate_b).transpose(0, 2, 1)
    f_pre = (mf + fgate_b).transpose(0, 2, 1)
    hm = mlstm_chunkwise(to_heads(mq, M_HEADS), to_heads(mk, M_HEADS), to_heads(mv, M_HEADS), i_pre, f_pre)
    hm = rms_norm(hm, mnorm_g[:, None, :]) * jax.nn.sigmoid(to_heads(mo, M_HEADS).astype(f32))
    qb = rms_norm(to_heads(bq, B_HEADS), qn_g)
    kb = rms_norm(to_heads(bk, B_HEADS), kn_g)
    hb = moba_attention(qb, kb, to_heads(bv, B_HEADS), alibi_slopes(B_HEADS))
    y = jnp.concatenate([from_heads(hm), from_heads(hb)], axis=-1).astype(h.dtype)
    return y @ w_out

def diff_attention_mixer(h, w_in, qn_g, kn_g, lam_p, onorm_g, w_out, lam_init):
    f32 = jnp.float32
    bn, s, _ = h.shape
    z = h @ w_in
    qk_w = 2 * C_HEADS * C_DH
    q = z[..., :qk_w].reshape(bn, s, C_HEADS, 2, C_DH).transpose(0, 2, 3, 1, 4)
    k = z[..., qk_w:2 * qk_w].reshape(bn, s, C_HEADS, 2, C_DH).transpose(0, 2, 3, 1, 4)
    v = to_heads(z[..., 2 * qk_w:], C_HEADS)
    q = rms_norm(q, qn_g)
    k = rms_norm(k, kn_g)
    lp = lam_p.astype(f32)
    lam = jnp.exp(jnp.sum(lp[0] * lp[1])) - jnp.exp(jnp.sum(lp[2] * lp[3])) + lam_init
    o = diff_attention(q, k, v, lam, alibi_slopes(C_HEADS))
    o = rms_norm(o, onorm_g) * (1.0 - lam_init)
    return from_heads(o).astype(h.dtype) @ w_out

def peer_ffn(x, wq, keys, u, v):
    f32 = jnp.float32
    bn, s, d = x.shape
    t = bn * s
    xt = x.reshape(t, d)
    qry = (xt @ wq).astype(f32).reshape(t, PEER_HEADS, 2, PEER_DK // 2)
    sub = jnp.einsum('thpd,pnd->thpn', qry, keys.astype(f32))
    s_top, i_top = lax.top_k(sub, PEER_TOPK)
    cand_s = (s_top[:, :, 0, :, None] + s_top[:, :, 1, None, :]).reshape(t, PEER_HEADS, PEER_TOPK * PEER_TOPK)
    cand_i = (i_top[:, :, 0, :, None] * PEER_NKEYS + i_top[:, :, 1, None, :]).reshape(t, PEER_HEADS, PEER_TOPK * PEER_TOPK)
    score, pos = lax.top_k(cand_s, PEER_TOPK)
    idx = jnp.take_along_axis(cand_i, pos, axis=-1)
    gate = jax.nn.softmax(score, axis=-1)
    tc = PEER_TOK_CHUNK
    nt = t // tc

    def one_chunk(args):
        xb, ib, gb = args
        act = jax.nn.gelu(jnp.einsum('td,thkd->thk', xb, u[ib]).astype(f32), approximate=False) * gb
        return jnp.einsum('thk,thkd->td', act, v[ib].astype(f32))

    out = lax.map(one_chunk, (xt.reshape(nt, tc, d),
                              idx.reshape(nt, tc, PEER_HEADS, PEER_TOPK),
                              gate.reshape(nt, tc, PEER_HEADS, PEER_TOPK)))
    return out.reshape(bn, s, d).astype(x.dtype)

def first_inputs(seed: int = 0) -> dict:
    key = jax.random.key(seed)
    ks = jax.random.split(key, 24)
    f32 = jnp.float32
    D = D_MODEL

    def nrm(k, shape, sc):
        return jax.random.normal(k, shape, f32) * sc

    return {
        'x': nrm(ks[0], (BATCH, SEQ, D), 1.0),
        'c': nrm(ks[1], (BATCH, D), 1.0),
        'ada_w': nrm(ks[2], (DEPTH, D, 6 * D), 0.5 * D ** -0.5),
        'ada_b': nrm(ks[3], (DEPTH, 6 * D), 0.01),
        'norm_mix_g': 1.0 + nrm(ks[4], (DEPTH, D), 0.02),
        'norm_ffn_g': 1.0 + nrm(ks[5], (DEPTH, D), 0.02),
        'ev_w_in': nrm(ks[6], (N_EVEN, D, IN_EVEN), D ** -0.5),
        'ev_conv_w': nrm(ks[7], (N_EVEN, CONV_K, 2 * M_W), CONV_K ** -0.5),
        'ev_igate_b': -1.0 + nrm(ks[8], (N_EVEN, M_HEADS), 0.1),
        'ev_fgate_b': jnp.linspace(3.0, 6.0, M_HEADS, dtype=f32) + nrm(ks[9], (N_EVEN, M_HEADS), 0.1),
        'ev_mnorm_g': 1.0 + nrm(ks[10], (N_EVEN, M_HEADS, M_DH), 0.02),
        'ev_qn_g': 1.0 + nrm(ks[11], (N_EVEN, B_DH), 0.02),
        'ev_kn_g': 1.0 + nrm(ks[12], (N_EVEN, B_DH), 0.02),
        'ev_w_out': nrm(ks[13], (N_EVEN, MIX_EVEN, D), MIX_EVEN ** -0.5),
        'od_w_in': nrm(ks[14], (N_ODD, D, IN_ODD), D ** -0.5),
        'od_qn_g': 1.0 + nrm(ks[15], (N_ODD, C_DH), 0.02),
        'od_kn_g': 1.0 + nrm(ks[16], (N_ODD, C_DH), 0.02),
        'od_lam': nrm(ks[17], (N_ODD, 4, C_DH), 0.1),
        'od_onorm_g': 1.0 + nrm(ks[18], (N_ODD, C_VDH), 0.02),
        'od_w_out': nrm(ks[19], (N_ODD, C_W, D), C_W ** -0.5),
        'peer_wq': nrm(ks[20], (DEPTH, D, PEER_HEADS * PEER_DK), D ** -0.5),
        'peer_keys': nrm(ks[21], (DEPTH, 2, PEER_NKEYS, PEER_DK // 2), (PEER_DK // 2) ** -0.5),
        'peer_u': nrm(ks[22], (DEPTH, PEER_N, D), D ** -0.5),
        'peer_v': nrm(ks[23], (DEPTH, PEER_N, D), PEER_HEADS ** -0.5),
    }

def first_block(x, c, ada_w, ada_b, norm_mix_g, norm_ffn_g, ev_w_in, ev_conv_w, ev_igate_b, ev_fgate_b,
              ev_mnorm_g, ev_qn_g, ev_kn_g, ev_w_out, od_w_in, od_qn_g, od_kn_g, od_lam, od_onorm_g,
              od_w_out, peer_wq, peer_keys, peer_u, peer_v):
    c_act = jax.nn.silu(c.astype(jnp.float32))
    for layer in range(DEPTH):
        mod = (c_act @ ada_w[layer].astype(jnp.float32) + ada_b[layer].astype(jnp.float32)).astype(x.dtype)
        sh1, sc1, g1, sh2, sc2, g2 = [m[:, None, :] for m in jnp.split(mod, 6, axis=-1)]
        h = rms_norm(x, norm_mix_g[layer]) * (1.0 + sc1) + sh1
        if layer % 2 == 0:
            e = layer // 2
            y = mlstm_moba_mixer(h, ev_w_in[e], ev_conv_w[e], ev_igate_b[e], ev_fgate_b[e],
                                 ev_mnorm_g[e], ev_qn_g[e], ev_kn_g[e], ev_w_out[e])
        else:
            o = layer // 2
            lam_init = 0.8 - 0.6 * math.exp(-0.3 * layer)
            y = diff_attention_mixer(h, od_w_in[o], od_qn_g[o], od_kn_g[o], od_lam[o],
                                     od_onorm_g[o], od_w_out[o], lam_init)
        x = x + g1 * y.astype(x.dtype)
        h = rms_norm(x, norm_ffn_g[layer]) * (1.0 + sc2) + sh2
        x = x + g2 * peer_ffn(h, peer_wq[layer], peer_keys[layer], peer_u[layer], peer_v[layer])
    return x


DEPTH_2 = 1

HEAD_DIM = 64
MEM_LEN = 256
GRID_W = 64
NA_HEADS = D_MODEL // (2 * HEAD_DIM)
NA_WIN_ROWS = 8
NA_WIN_COLS = 16
DIL_PAIRS = ((128, 1), (512, 4), (2048, 16))
DIL_GROUPS = len(DIL_PAIRS)
DIL_HEADS_PER_GROUP = D_MODEL // (4 * HEAD_DIM)
DIL_HEADS = DIL_GROUPS * DIL_HEADS_PER_GROUP
DIL_BLOCK = 128
MEM_HEADS = 4
T5_BUCKETS = 32
T5_MAX_DIST = 1024
N_GROUPS = 4
EXPERTS_PER_GROUP = 8
N_EXPERTS = N_GROUPS * EXPERTS_PER_GROUP
TOP_K = 2
D_EXPERT = D_MODEL // 2
MOE_BLOCK = 256
NEG_INF = -1e30

NA_W = NA_HEADS * HEAD_DIM
DIL_W = DIL_HEADS * HEAD_DIM
DIL_OUT_W = DIL_HEADS_PER_GROUP * HEAD_DIM
MEM_W = MEM_HEADS * HEAD_DIM
IN_COLS = 3 * NA_W + 3 * DIL_W + MEM_W
MIX_W = NA_W + DIL_OUT_W + MEM_W
IN_SPLITS = (NA_W, 2 * NA_W, 3 * NA_W, 3 * NA_W + DIL_W, 3 * NA_W + 2 * DIL_W, 3 * NA_W + 3 * DIL_W)


def rms_norm_2(x, g):
    xf = x.astype(jnp.float32)
    y = xf * lax.rsqrt(jnp.mean(xf * xf, axis=-1, keepdims=True) + EPS)
    return (y * g.astype(jnp.float32)).astype(x.dtype)

def t5_bucket(rel):
    nb = T5_BUCKETS // 2
    max_exact = nb // 2
    n = jnp.abs(rel)
    upper = (rel > 0).astype(jnp.int32) * nb
    nf = jnp.maximum(n, 1).astype(jnp.float32)
    large = max_exact + (jnp.log(nf / max_exact) / math.log(T5_MAX_DIST / max_exact) * (nb - max_exact)).astype(jnp.int32)
    large = jnp.minimum(large, nb - 1)
    return upper + jnp.where(n < max_exact, n, large)

def neighborhood_attention(q, k, v, rpb):
    b, s, h, dh = q.shape
    rows = s // GRID_W
    kh = min(NA_WIN_ROWS, rows)
    kw = NA_WIN_COLS
    kg = k.reshape(b, rows, GRID_W, h, dh).transpose(0, 3, 1, 2, 4)
    vg = v.reshape(b, rows, GRID_W, h, dh).transpose(0, 3, 1, 2, 4)
    qg = q.reshape(b, rows, GRID_W, h, dh).transpose(1, 0, 3, 2, 4)
    cols = jnp.arange(GRID_W)
    c0 = jnp.clip(cols - kw // 2, 0, GRID_W - kw)
    col_idx = c0[:, None] + jnp.arange(kw)[None, :]
    dc = col_idx - cols[:, None] + (NA_WIN_COLS - 1)
    scale = HEAD_DIM ** -0.5

    def row_fn(args):
        q_r, r = args
        r0 = jnp.clip(r - kh // 2, 0, rows - kh)
        k_rows = lax.dynamic_slice_in_dim(kg, r0, kh, axis=2)
        v_rows = lax.dynamic_slice_in_dim(vg, r0, kh, axis=2)
        k_win = k_rows[:, :, :, col_idx]
        v_win = v_rows[:, :, :, col_idx]
        dr = r0 + jnp.arange(kh) - r + (NA_WIN_ROWS - 1)
        bias = rpb[:, dr[:, None, None], dc[None]].transpose(0, 2, 1, 3)
        logits = jnp.einsum('bhcd,bhacjd->bhcaj', q_r, k_win).astype(jnp.float32) * scale + bias.astype(jnp.float32)[None]
        p = jax.nn.softmax(logits, axis=(-2, -1)).astype(v.dtype)
        return jnp.einsum('bhcaj,bhacjd->bhcd', p, v_win)

    out = lax.map(row_fn, (qg, jnp.arange(rows)))
    return out.transpose(1, 0, 3, 2, 4).reshape(b, s, h * dh)

def dilated_window_attention(q, k, v, offs, bias, half):
    b, s, h, dh = q.shape
    scale = HEAD_DIM ** -0.5
    kp = jnp.pad(k, ((0, 0), (half, half), (0, 0), (0, 0)))
    vp = jnp.pad(v, ((0, 0), (half, half), (0, 0), (0, 0)))
    local = jnp.arange(DIL_BLOCK)[:, None] + offs[None, :] + half
    bias32 = bias.astype(jnp.float32)
    n_blk = s // DIL_BLOCK

    def block_fn(i):
        s0 = i * DIL_BLOCK
        qb = lax.dynamic_slice_in_dim(q, s0, DIL_BLOCK, axis=1)
        kb = lax.dynamic_slice_in_dim(kp, s0, DIL_BLOCK + 2 * half, axis=1)
        vb = lax.dynamic_slice_in_dim(vp, s0, DIL_BLOCK + 2 * half, axis=1)
        kgat = kb[:, local]
        vgat = vb[:, local]
        key_pos = s0 + local - half
        valid = (key_pos >= 0) & (key_pos < s)
        logits = jnp.einsum('bqhd,bqjhd->bqhj', qb, kgat).astype(jnp.float32) * scale + bias32[None, None]
        logits = jnp.where(valid[None, :, None, :], logits, NEG_INF)
        m = jnp.max(logits, axis=-1)
        e = jnp.exp(logits - m[..., None])
        den = jnp.sum(e, axis=-1)
        o = jnp.einsum('bqhj,bqjhd->bqhd', e, vgat.astype(jnp.float32)) / den[..., None]
        return o, m, den

    o, m, den = lax.map(block_fn, jnp.arange(n_blk))
    o = o.transpose(1, 0, 2, 3, 4).reshape(b, s, h, dh)
    m = m.transpose(1, 0, 2, 3).reshape(b, s, h)
    den = den.transpose(1, 0, 2, 3).reshape(b, s, h)
    return o, m, den

def hierarchical_moe(h, w_r1, b_r1, w_r2, b_r2, w1, w3, w2):
    b, s, d = h.shape
    n = b * s
    t = h.reshape(n, d)
    grp_logits = (t @ w_r1).astype(jnp.float32) + b_r1.astype(jnp.float32)
    grp_prob = jax.nn.softmax(grp_logits, axis=-1)
    grp_idx = jnp.argmax(grp_logits, axis=-1)
    grp_gate = jnp.take_along_axis(grp_prob, grp_idx[:, None], axis=-1)
    fine_logits = ((t @ w_r2).astype(jnp.float32) + b_r2.astype(jnp.float32)).reshape(n, N_GROUPS, EXPERTS_PER_GROUP)
    fine_sel = jnp.take_along_axis(fine_logits, grp_idx[:, None, None], axis=1)[:, 0]
    top_val, top_idx = lax.top_k(fine_sel, TOP_K)
    gate = grp_gate * jax.nn.softmax(top_val, axis=-1)
    exp_idx = grp_idx[:, None] * EXPERTS_PER_GROUP + top_idx
    n_rows = n * TOP_K
    e_flat = exp_idx.reshape(-1)
    g_flat = gate.reshape(-1)
    tok_flat = jnp.repeat(jnp.arange(n), TOP_K)
    order = jnp.argsort(e_flat)
    e_sorted = e_flat[order]
    counts = jnp.bincount(e_flat, length=N_EXPERTS)
    cnt_start = jnp.cumsum(counts) - counts
    padded = (counts + MOE_BLOCK - 1) // MOE_BLOCK * MOE_BLOCK
    pad_end = jnp.cumsum(padded)
    pad_start = pad_end - padded
    dest = pad_start[e_sorted] + jnp.arange(n_rows) - cnt_start[e_sorted]
    cap = n_rows + N_EXPERTS * MOE_BLOCK
    row_tok = jnp.full((cap,), n, jnp.int32).at[dest].set(tok_flat[order])
    row_gate = jnp.zeros((cap,), jnp.float32).at[dest].set(g_flat[order])
    n_blk = cap // MOE_BLOCK
    blk_exp = jnp.minimum(jnp.searchsorted(pad_end, jnp.arange(n_blk) * MOE_BLOCK, side='right'), N_EXPERTS - 1)
    t_pad = jnp.concatenate([t, jnp.zeros((1, d), t.dtype)], axis=0)
    xs = t_pad[row_tok].reshape(n_blk, MOE_BLOCK, d)

    def expert_block(args):
        xb, e = args
        a = jax.nn.silu(xb @ w1[e]) * (xb @ w3[e])
        return a @ w2[e]

    yb = lax.map(expert_block, (xs, blk_exp)).reshape(cap, d)
    y = jnp.zeros((n + 1, d), h.dtype).at[row_tok].add(yb * row_gate[:, None].astype(h.dtype))
    return y[:n].reshape(b, s, d)

def second_inputs(seed: int = 0) -> dict:
    key = jax.random.key(seed)
    ks = jax.random.split(key, 18)
    f32 = jnp.float32

    def nrm(k, shape, sc):
        return jax.random.normal(k, shape, f32) * sc

    L = DEPTH_2
    return {
        'x': nrm(ks[0], (BATCH, SEQ, D_MODEL), 1.0),
        'mem': nrm(ks[1], (BATCH, MEM_LEN, D_MODEL), 1.0),
        'g_mix': 1.0 + nrm(ks[2], (L, D_MODEL), 0.02),
        'w_in': nrm(ks[3], (L, D_MODEL, IN_COLS), D_MODEL ** -0.5),
        'qk_gain': 1.0 + nrm(ks[4], (L, 3, 2, HEAD_DIM), 0.02),
        'na_rpb': nrm(ks[5], (L, NA_HEADS, 2 * NA_WIN_ROWS - 1, 2 * NA_WIN_COLS - 1), 0.1),
        't5_table': nrm(ks[6], (T5_BUCKETS, DIL_HEADS), 0.1),
        'g_mem': 1.0 + nrm(ks[7], (L, D_MODEL), 0.02),
        'w_mem_kv': nrm(ks[8], (L, D_MODEL, 2 * MEM_W), D_MODEL ** -0.5),
        'w_out': nrm(ks[9], (L, MIX_W, D_MODEL), MIX_W ** -0.5),
        'g_ffn': 1.0 + nrm(ks[10], (L, D_MODEL), 0.02),
        'w_r1': nrm(ks[11], (L, D_MODEL, N_GROUPS), D_MODEL ** -0.5),
        'b_r1': nrm(ks[12], (L, N_GROUPS), 0.01),
        'w_r2': nrm(ks[13], (L, D_MODEL, N_EXPERTS), D_MODEL ** -0.5),
        'b_r2': nrm(ks[14], (L, N_EXPERTS), 0.01),
        'w1': nrm(ks[15], (L, N_EXPERTS, D_MODEL, D_EXPERT), D_MODEL ** -0.5),
        'w3': nrm(ks[16], (L, N_EXPERTS, D_MODEL, D_EXPERT), D_MODEL ** -0.5),
        'w2': nrm(ks[17], (L, N_EXPERTS, D_EXPERT, D_MODEL), D_EXPERT ** -0.5),
    }

def second_block(x, mem, g_mix, w_in, qk_gain, na_rpb, t5_table, g_mem, w_mem_kv, w_out, g_ffn, w_r1, b_r1, w_r2, b_r2, w1, w3, w2):
    b, s, _ = x.shape
    hd = HEAD_DIM
    scale = HEAD_DIM ** -0.5
    t5 = t5_table.reshape(T5_BUCKETS, DIL_GROUPS, DIL_HEADS_PER_GROUP)
    for l in range(DEPTH_2):
        h = rms_norm_2(x, g_mix[l])
        qa, ka, va, qd, kd, vd, qm = jnp.split(h @ w_in[l], IN_SPLITS, axis=-1)

        qa = rms_norm_2(qa.reshape(b, s, NA_HEADS, hd), qk_gain[l, 0, 0])
        ka = rms_norm_2(ka.reshape(b, s, NA_HEADS, hd), qk_gain[l, 0, 1])
        va = va.reshape(b, s, NA_HEADS, hd)
        out_na = neighborhood_attention(qa, ka, va, na_rpb[l])

        dshape = (b, s, DIL_GROUPS, DIL_HEADS_PER_GROUP, hd)
        qd = rms_norm_2(qd.reshape(dshape), qk_gain[l, 1, 0])
        kd = rms_norm_2(kd.reshape(dshape), qk_gain[l, 1, 1])
        vd = vd.reshape(dshape)
        o_list, m_list, d_list = [], [], []
        for g, (win, dil) in enumerate(DIL_PAIRS):
            half = win // 2
            n_side = half // dil
            offs = jnp.arange(-n_side, n_side + 1) * dil
            bias = t5[t5_bucket(offs), g].T
            o, m, den = dilated_window_attention(qd[:, :, g], kd[:, :, g], vd[:, :, g], offs, bias, half)
            o_list.append(o)
            m_list.append(m)
            d_list.append(den)
        m_all = jnp.stack(m_list)
        wts = jnp.stack(d_list) * jnp.exp(m_all - jnp.max(m_all, axis=0, keepdims=True))
        out_dil = jnp.sum(wts[..., None] * jnp.stack(o_list), axis=0) / jnp.sum(wts, axis=0)[..., None]
        out_dil = out_dil.astype(x.dtype).reshape(b, s, DIL_OUT_W)

        kvm = rms_norm_2(mem, g_mem[l]) @ w_mem_kv[l]
        km, vm = jnp.split(kvm, 2, axis=-1)
        km = rms_norm_2(km.reshape(b, -1, MEM_HEADS, hd), qk_gain[l, 2, 1])
        vm = vm.reshape(b, -1, MEM_HEADS, hd)
        qm = rms_norm_2(qm.reshape(b, s, MEM_HEADS, hd), qk_gain[l, 2, 0])
        logits_m = jnp.einsum('bshd,bmhd->bhsm', qm, km).astype(jnp.float32) * scale
        p_m = jax.nn.softmax(logits_m, axis=-1).astype(vm.dtype)
        out_mem = jnp.einsum('bhsm,bmhd->bshd', p_m, vm).reshape(b, s, MEM_W)

        x = x + jnp.concatenate([out_na, out_dil, out_mem], axis=-1) @ w_out[l]
        x = x + hierarchical_moe(rms_norm_2(x, g_ffn[l]), w_r1[l], b_r1[l], w_r2[l], b_r2[l], w1[l], w3[l], w2[l])
    return x


def setup_inputs(seed=0):
    out = dict(first_inputs(seed))
    for name, value in second_inputs(seed + 1).items():
        if name != "x":
            out[name + "_2"] = value
    return out


def reference(
    x, c, ada_w, ada_b, norm_mix_g, norm_ffn_g, ev_w_in, ev_conv_w, ev_igate_b, ev_fgate_b,
    ev_mnorm_g, ev_qn_g, ev_kn_g, ev_w_out, od_w_in, od_qn_g, od_kn_g, od_lam, od_onorm_g,
    od_w_out, peer_wq, peer_keys, peer_u, peer_v, mem_2, g_mix_2, w_in_2, qk_gain_2, na_rpb_2,
    t5_table_2, g_mem_2, w_mem_kv_2, w_out_2, g_ffn_2, w_r1_2, b_r1_2, w_r2_2, b_r2_2, w1_2,
    w3_2, w2_2,
):
    x = first_block(
        x, c, ada_w, ada_b, norm_mix_g, norm_ffn_g, ev_w_in, ev_conv_w, ev_igate_b, ev_fgate_b,
        ev_mnorm_g, ev_qn_g, ev_kn_g, ev_w_out, od_w_in, od_qn_g, od_kn_g, od_lam, od_onorm_g,
        od_w_out, peer_wq, peer_keys, peer_u, peer_v,
    )
    return second_block(
        x, mem_2, g_mix_2, w_in_2, qk_gain_2, na_rpb_2, t5_table_2, g_mem_2, w_mem_kv_2,
        w_out_2, g_ffn_2, w_r1_2, b_r1_2, w_r2_2, b_r2_2, w1_2, w3_2, w2_2,
    )


_drawn_inputs = setup_inputs


def setup_inputs(seed=0):
    import zlib

    import numpy as np

    out = dict(_drawn_inputs(seed))
    spreads = {}
    factors = {'norm_mix_g': 2.987,
     'ev_igate_b': 8.0,
     'ev_mnorm_g': 2.896,
     'ev_qn_g': 3.937,
     'ev_kn_g': 5.23,
     'od_qn_g': 4.071,
     'od_kn_g': 3.066,
     'g_mix_2': 2.908,
     'qk_gain_2': 3.791,
     't5_table_2': 3.173,
     'g_mem_2': 8.0,
     'b_r1_2': 50.44,
     'b_r2_2': 27.112,
     'od_onorm_g': 3.363,
     'na_rpb_2': 5.596,
     'g_ffn_2': 8.0}
    for name, (base, spread) in spreads.items():
        noise = np.random.default_rng([zlib.crc32(name.encode()), seed]).standard_normal(out[name].shape)
        drawn = base * np.exp(spread * noise) if base else spread * noise
        out[name] = jnp.asarray(drawn.astype(out[name].dtype))
    for name, factor in factors.items():
        out[name] = (out[name] * factor).astype(out[name].dtype)
    return out
```

```python
import math
from contextlib import ExitStack

import numpy as np

import concourse.bass as bass
from concourse import mybir

F32 = mybir.dt.float32
U32 = mybir.dt.uint32
ALU = mybir.AluOpType
ACT = mybir.ActivationFunctionType
AX = mybir.AxisListType

P = 128
D = 1024
S = 256
T = S // P
KT = D // P
EPS = 1e-6
NEG = -1e30
RING = 4
CH = 512

M_HEADS, M_DH = 4, 128
B_HEADS, C_HEADS, NA_HEADS, MEM_HEADS = 8, 8, 8, 4
DIL_GROUPS, DIL_HPG = 3, 4
DIL_PAIRS = ((128, 1), (512, 4), (2048, 16))
GRID_W, NA_KR, NA_KC = 64, 15, 31
T5_BUCKETS, T5_MAX_DIST = 32, 1024
LAM_INIT = 0.8 - 0.6 * math.exp(-0.3)
PEER_H, NKEYS, TOPK = 8, 128, 16
PEER_N = NKEYS * NKEYS
SLOTS = PEER_H * TOPK
ROWS = 8
GROUPS = SLOTS // ROWS
N_EXP, N_GRP, PER_GRP = 32, 4, 8
MOE_RING = 6
CAP = 64
FULL = CAP

C_ID, C_DIST, C_MASKT, C_NAM, C_BLK, C_IOTA = 0, 128, 512, 768, 832, 960
C_N = 1024
G_EVQ, G_EVK, G_ODQ, G_ODK, G_NAQ, G_NAK, G_DLQ, G_DLK, G_MMQ, G_MMK = range(10)
TW = 2 * S - 1
RW = 2 * GRID_W - 1
NDR = 7


def slope(h):
    return 2.0 ** (-8.0 * (h + 1) / 8)


def shape_constants():
    c = np.zeros((P, C_N), np.float32)
    p = np.arange(P)[:, None]
    c[:, C_ID:C_ID + P] = np.eye(P)
    dist = p + P - np.arange(3 * P)[None]
    c[:, C_DIST:C_DIST + 3 * P] = np.where(dist >= 0, dist, -NEG)
    c[:, C_MASKT:C_MASKT + S] = np.where(p <= np.arange(S)[None], 0, NEG)
    qc = p % GRID_W
    first = np.clip(qc - 8, 0, GRID_W - 16)
    kc = np.arange(GRID_W)[None]
    c[:, C_NAM:C_NAM + GRID_W] = np.where((kc >= first) & (kc < first + 16), 0, NEG)
    c[:, C_BLK:C_BLK + P] = (p // 64) == (np.arange(P)[None] // 64)
    c[:, C_IOTA:C_IOTA + CAP] = np.arange(CAP)[None]
    rel = np.arange(TW) - (S - 1)
    nb = T5_BUCKETS // 2
    exact = nb // 2
    n = np.abs(rel)
    nf = np.maximum(n, 1).astype(np.float32)
    large = exact + (np.log(nf / np.float32(exact)) / np.float32(math.log(T5_MAX_DIST / exact))
                     * np.float32(nb - exact)).astype(np.int32)
    bucket = (rel > 0) * nb + np.where(n < exact, n, np.minimum(large, nb - 1))
    onehot = np.zeros((T5_BUCKETS, TW), np.float32)
    onehot[bucket, np.arange(TW)] = 1
    dmask = np.zeros((DIL_HPG, DIL_GROUPS, TW), np.float32)
    for g, (win, dil) in enumerate(DIL_PAIRS):
        dmask[:, g] = np.where((rel % dil == 0) & (n <= win // 2), 0, NEG)
    return c, onehot, dmask


def weight_stream(a):
    def view(w, c0, n=CH):
        return w[:, c0:c0 + n].rearrange("(k p) n -> p k n", p=P)

    slots = []

    def ada(l):
        for n in range(12):
            slots.append((f"ada{l}", view(a["ada_w"][l], n * CH), [("bcast", n)]))

    def rows(name, w, c0, dst):
        slots.append((name, view(w, c0), [("rows", 0, dst), ("rows", 1, dst)]))

    def cols(name, w, c0, z0):
        slots.append((name, view(w, c0), [("cols", 0, z0), ("cols", 256, z0 + 2)]))

    ada(0)
    w = a["ev_w_in"][0]
    cols("in0", w, 0, 0)
    cols("in0", w, 512, 4)
    rows("in0", w, 1024, ("zn", 0))
    rows("in0", w, 1536, ("zn", 512))
    cols("in0", w, 2056, 8)
    cols("in0", w, 2568, 12)
    rows("in0", w, 3080, ("zn", 1024))
    for n in range(2):
        rows("out0", a["ev_w_out"][0], n * CH, ("y", n * CH))
    for n in range(4):
        cols("wq0", a["peer_wq"][0], n * CH, 4 * n)
    ada(1)
    for n in range(4):
        cols("in1", a["od_w_in"][0], n * CH, 4 * n)
    for n in range(2):
        rows("in1", a["od_w_in"][0], 2048 + n * CH, ("zn", n * CH))
    for n in range(2):
        rows("out1", a["od_w_out"][0], n * CH, ("y", n * CH))
    for n in range(4):
        cols("wq1", a["peer_wq"][1], n * CH, 4 * n)
    slots.append(("mem", view(a["w_mem_kv_2"][0], 0), [("cols", 0, 22), ("rows2", 256, ("zn", 1280))]))
    w = a["w_in_2"][0]
    cols("in2", w, 0, 0)
    cols("in2", w, 512, 4)
    rows("in2", w, 1024, ("zn", 0))
    cols("in2", w, 1536, 8)
    cols("in2", w, 2048, 12)
    cols("in2", w, 2560, 16)
    rows("in2", w, 3072, ("zn", 512))
    slots.append(("in2", view(w, 3584), [("rows2", 0, ("zn", 1024)), ("cols", 256, 20)]))
    for n in range(2):
        rows("out2", a["w_out_2"][0], n * CH, ("y", n * CH))
    return slots


def attention_segments(stage, v):
    zt, zn, dist, dil_bias, na_bias = v["zt"], v["zn"], v["dist"], v["dil_bias"], v["na_bias"]
    units, segs = [], []

    def head(tile, h):
        return zt(tile + h // 2), 64 * (h % 2)

    def unit(t, out, parts, tag=None):
        u = len(units)
        units.append(dict(t=t, out=out, first=len(segs), n=len(parts), tag=tag))
        for i, (qt, kt, base, bias, nk, val, dv) in enumerate(parts):
            segs.append(dict(u=u, q=qt[base:base + 64, t * P:(t + 1) * P], k=kt[base:base + 64, 0:nk],
                             bias=bias, nk=nk, v=val, dv=dv, first=i == 0, last=i == len(parts) - 1))

    if stage == "moba":
        for h in range(B_HEADS):
            for t in range(T):
                nk = (t + 1) * P
                qt, base = head(8, h)
                kt, _ = head(12, h)
                unit(t, 512 + 64 * h, [(qt, kt, base, ("alibi", dist[:, (1 - t) * P:(1 - t) * P + nk], -slope(h)), nk,
                                        1024 + 64 * h, 64)])
    if stage == "diff":
        for h in range(C_HEADS):
            for t in range(T):
                for c in range(2):
                    nk = (t + 1) * P
                    unit(t, P * h, [(zt(h), zt(8 + h), 64 * c,
                                     ("alibi", dist[:, (1 - t) * P:(1 - t) * P + nk], -slope(h)), nk, P * h, P)], c)
    if stage == "block2":
        for h in range(NA_HEADS):
            for t in range(T):
                qt, base = head(0, h)
                kt, _ = head(4, h)
                unit(t, 64 * h, [(qt, kt, base, ("add", na_bias[:, h, (2 - 2 * t) * GRID_W:(2 - 2 * t) * GRID_W + S]),
                                  S, 64 * h, 64)])
        for h in range(MEM_HEADS):
            for t in range(T):
                qt, base = head(20, h)
                kt, _ = head(22, h)
                unit(t, 768 + 64 * h, [(qt, kt, base, ("none",), S, 1280 + 64 * h, 64)])
        for h in range(DIL_HPG):
            for t in range(T):
                parts = []
                for g in range(DIL_GROUPS):
                    i = g * DIL_HPG + h
                    qt, base = head(8, i)
                    kt, _ = head(14, i)
                    parts.append((qt, kt, base, ("add", dil_bias[:, i, (1 - t) * P:(1 - t) * P + S]), S,
                                  512 + 64 * i, 64))
                unit(t, 512 + 64 * h, parts)
    return units, segs


def program(nc, a, out):
    ctx = ExitStack()
    with ctx:
        ctx.enter_context(nc.allow_non_contiguous_dma(reason="small parameter columns"))

        def sb(name, shape, dt=F32):
            return ctx.enter_context(nc.sbuf_tensor(name, shape, dt))

        def sem(name):
            return ctx.enter_context(nc.semaphore(name))

        x = sb("x", [P, T, D])
        h = sb("h", [P, T, D])
        y = sb("y", [P, T, D])
        hT = sb("hT", [P, KT, S])
        mod = sb("mod", [P, 5 * D])
        g2 = sb("g2", [P, 2, D])
        zbuf = sb("zbuf", [P, 8192])
        ring = sb("ring", [P, RING, KT * CH])
        tk = sb("tk", [P, 6144])
        work = sb("work", [P, 2048])
        gvec = sb("gvec", [P, D])
        cst = sb("cst", [P, C_N])
        ada_b = sb("ada_b", [12, CH])
        cact = sb("cact", [P, KT])
        gains = sb("gains", [P, 10])
        convw = sb("convw", [P, 8, 4])
        gate_w = sb("gate_w", [P, KT, 8])
        gate_b = sb("gate_b", [4, 2])
        idx = sb("idx", [P, T, SLOTS], U32)
        gate = sb("gate", [P, T, SLOTS])
        dots = sb("dots", [P, SLOTS])
        coef = sb("coef", [P, SLOTS])
        dots8 = sb("dots8", [P, ROWS])
        stage = sb("stage", [P, ROWS], U32)
        small = sb("small", [P, 64])
        nmax = sb("nmax", [P, 8])
        den = sb("den", [P, 8])
        eps = sb("eps", [P, 1])
        ones1 = sb("ones1", [P, 1])
        gw36 = sb("gw36", [P, KT, 36])
        lam_rows = sb("lam_rows", [P, 4, 64])
        onorm_t = sb("onorm", [P, P])
        onorm = onorm_t[:, :]

        ident = cst[:, C_ID:C_ID + P]
        dist = cst[:, C_DIST:C_DIST + 3 * P]
        maskT = cst[:, C_MASKT:C_MASKT + S]
        na_mask = cst[:, C_NAM:C_NAM + GRID_W]
        blk = cst[:, C_BLK:C_BLK + P]
        iota64 = cst[:, C_IOTA:C_IOTA + CAP]
        iota = cst[:, C_IOTA:C_IOTA + TOPK]
        na_bias = mod[:, 2048:5120].rearrange("p (h j) -> p h j", h=NA_HEADS)
        dil_bias = tk[:, 0:12 * 384].rearrange("p (i j) -> p i j", i=12)

        def zt(c):
            b, c = (zbuf, c) if c < 16 else (mod, c - 16)
            return b[:, c * S:(c + 1) * S]

        def zt2(c):
            b, c = (zbuf, c) if c < 16 else (mod, c - 16)
            return b[:, c * S:(c + 2) * S]

        zn = zbuf[:, 4096:4096 + T * 1536].rearrange("p (t n) -> p t n", t=T)
        rowbuf = zbuf[:, :].rearrange("p (r n) -> p r n", r=ROWS)

        gp = ctx.enter_context(nc.psum_tensor("gp", [P, 2, 512], F32))
        sp_ = ctx.enter_context(nc.psum_tensor("scores", [P, 2, 512], F32))
        tp = ctx.enter_context(nc.psum_tensor("turned", [P, 2, 512], F32))
        op = ctx.enter_context(nc.psum_tensor("summed", [P, 2, 512], F32))

        t5_rows = nc.dram_tensor("t5_rows", [12, TW], F32, kind="Internal").ap()
        t5_rep = nc.dram_tensor("t5_rep", [P, 12 * TW], F32, kind="Internal").ap()
        na_rows = nc.dram_tensor("na_rows", [NA_HEADS * NDR, RW], F32, kind="Internal").ap()
        na_rep = nc.dram_tensor("na_rep", [GRID_W, NA_HEADS * NDR * RW], F32, kind="Internal").ap()

        loaded = sem("loaded")
        c_ready = sem("c_ready")
        w_landed = [sem(f"w_landed{i}") for i in range(RING)]
        ada_b_in = sem("ada_b_in")
        gemm_done = sem("gemm_done")
        gemm_moved = sem("gemm_moved")
        gvec_in = sem("gvec_in")
        gvec_used = sem("gvec_used")
        sumsq = sem("sumsq")
        rootd = sem("rootd")
        h_ready = sem("h_ready")
        turn_done = sem("turn_done")
        turn_moved = sem("turn_moved")
        qk_sq = sem("qk_sq")
        qk_sum = sem("qk_sum")
        qk_root = sem("qk_root")
        qk_done = sem("qk_done")
        s_done = sem("s_done")
        s_read = sem("s_read")
        m_done = sem("m_done")
        e_done = sem("e_done")
        t_done = sem("t_done")
        t_moved = sem("t_moved")
        o_done = sem("o_done")
        o_read = sem("o_read")
        y_ready = sem("y_ready")
        x_ready = sem("x_ready")
        dve = sem("dve")
        act_own = sem("act_own")
        pool_own = sem("pool_own")
        conv_done = sem("conv_done")
        silu_done = sem("silu_done")
        gates_mm = sem("gates_mm")
        gates_f = sem("gates_f")
        gates_e = sem("gates_e")
        gates_l = sem("gates_l")
        gates_g = sem("gates_g")
        gates_t = sem("gates_t")
        gates_c = sem("gates_c")
        mm_s = sem("ml_scores")
        mm_b = sem("ml_bcast")
        mm_arg = sem("ml_arg")
        mm_exp = sem("ml_exp")
        mm_p = sem("ml_p")
        mm_o = sem("ml_o")
        mm_read = sem("ml_read")
        em_ready = sem("em_ready")
        sig_done = sem("sig_done")
        hn_sq = sem("hn_sq")
        hn_rt = sem("hn_rt")
        keys_in = sem("keys_in")
        keys_t = sem("keys_t")
        keys_m = sem("keys_m")
        sub_done = sem("sub_done")
        sub_moved = sem("sub_moved")
        sub_free = sem("sub_free")
        top_ready = sem("top_ready")
        gate_e = sem("gate_e")
        idx_ready = sem("idx_ready")
        row_in = [sem(f"row_in{k}") for k in range(ROWS)]
        row_free = sem("row_free")
        idx_staged = sem("idx_staged")
        udot = sem("udot")
        dots_all = sem("dots_all")
        gelu_done = sem("gelu_done")
        coef_ready = sem("coef_ready")
        diag_ready = sem("diag_ready")
        diag_free = sem("diag_free")
        vsum = sem("vsum")
        lam_s = sem("lam_s")
        lam_e = sem("lam_e")
        lam_in = sem("lam_in")
        hn_dots = sem("dots_kept")
        t5_in = sem("t5_in")
        t5_mm = sem("t5_mm")
        t5_sum = sem("t5_sum")
        t5_w = sem("t5_w")
        na_w = sem("na_w")
        bias_in = sem("bias_in")
        bias_ok = sem("bias_ok")
        mem_in = sem("mem_in")
        r_in = sem("r_in")
        r_mm = sem("r_mm")
        r_pre = sem("r_pre")
        r_exp = sem("r_exp")
        r_done = sem("r_done")
        e_in = [sem(f"e_in{i}") for i in range(MOE_RING)]
        e_up = sem("e_up")
        e_act = sem("e_act")
        e_sig = sem("e_sig")
        e_down = sem("e_down")
        e_acc = sem("e_acc")
        out_done = sem("out_done")
        f_in = [sem(f"f_in{i}") for i in range(MOE_RING)]
        rank_done = sem("rank_done")
        over_ready = sem("over_ready")
        over_sum = sem("over_sum")
        flag_ready = sem("flag_ready")
        sel_ready = sem("sel_ready")
        gath_done = sem("gath_done")
        selt_done = sem("selt_done")
        selt_moved = sem("selt_moved")
        xe_moved = sem("xe_moved")
        up_done = sem("up_done")
        up_silu = sem("up_silu")
        up_act = sem("up_act")
        down_done = sem("down_done")
        down_moved = sem("down_moved")
        scat_done = sem("scat_done")
        scat_read = sem("scat_read")

        slots = weight_stream(a)
        group_of, last_group, first_group, g_n = [], {}, {}, 0
        for name, _, groups in slots:
            group_of.append(g_n)
            first_group.setdefault(name, g_n)
            g_n += len(groups)
            last_group[name] = g_n
        phase_slots = {}
        for n, (name, _, _) in enumerate(slots):
            phase_slots.setdefault(name, []).append(n)

        NORMS = ["mix0", "ffn0", "mix1", "ffn1", "mem", "mix2", "ffn2"]
        NLOADS = 11
        views = dict(zt=zt, zn=zn, dist=dist, dil_bias=dil_bias, na_bias=na_bias)
        att = {s: attention_segments(s, views) for s in ("moba", "diff", "block2")}
        seg_base, unit_base, nsegs, nunits = {}, {}, 0, 0
        for s_name in ("moba", "diff", "block2"):
            seg_base[s_name], unit_base[s_name] = nsegs, nunits
            nsegs += len(att[s_name][1])
            nunits += len(att[s_name][0])
        LAG = 3
        SEGS = 6
        segbuf = work[:, 0:SEGS * S].rearrange("p (r n) -> p r n", r=SEGS)
        ptbuf = work[:, SEGS * S:2048].rearrange("p (r n) -> p r n", r=2)
        QK = {"moba": [(8, G_EVQ), (10, G_EVQ), (12, G_EVK), (14, G_EVK)],
              "diff": [(2 * i, G_ODQ if i < 4 else G_ODK) for i in range(8)],
              "block2": [(0, G_NAQ), (2, G_NAQ), (4, G_NAK), (6, G_NAK), (8, G_DLQ), (10, G_DLQ), (12, G_DLQ),
                         (14, G_DLK), (16, G_DLK), (18, G_DLK), (20, G_MMQ), (22, G_MMK)]}
        qk_base, n = {}, 0
        for s_name in ("moba", "diff", "block2"):
            qk_base[s_name] = n
            n += len(QK[s_name])

        sub = tk[:, 0:2048].rearrange("p (c n) -> p c n", c=2 * PEER_H)
        cand = tk[:, 2048:4096].rearrange("p (h n) -> p h n", h=PEER_H)
        hot = tk[:, 4096:6144].rearrange("p (c n) -> p c n", c=SLOTS)
        diag = work[:, 0:512].rearrange("p (r n) -> p r n", r=4)
        keys = work[:, 512:768].rearrange("p (c n) -> p c n", c=2)
        keysT = work[:, 768:1024].rearrange("p (c n) -> p c n", c=2)
        top = work[:, 1024:1280].rearrange("p (c n) -> p c n", c=2 * PEER_H)
        topi = work[:, 1280:1536].bitcast(U32).rearrange("p (c n) -> p c n", c=2 * PEER_H)
        topf = work[:, 1536:1792].rearrange("p (c n) -> p c n", c=2 * PEER_H)
        score = work[:, 1792:1920].rearrange("p (h n) -> p h n", h=PEER_H)
        pos = work[:, 1920:2048].bitcast(U32).rearrange("p (h n) -> p h n", h=PEER_H)

        ml_arg = tk[:, 0:2 * 384].rearrange("p (b n) -> p b n", b=2)
        ml_p = tk[:, 768:768 + 2 * 384].rearrange("p (b n) -> p b n", b=2)
        mo_sig = tk[:, 1536:2560].rearrange("p (t n) -> p t n", t=T)
        mnorm = tk[:, 2560:3072]
        ml_rows = tk[0:4, 3072:3072 + 9 * S].rearrange("p (r n) -> p r n", r=9)
        I_, F_, A_, E_, B_, G_, NM_, EM_, ONE_ = (ml_rows[:, i, :] for i in range(9))
        ml_cols = small[:, 0:16].rearrange("p (c t h) -> p c t h", c=2, t=T)
        t5_hot = tk[0:T5_BUCKETS, 0:TW]
        t5_mask = tk[0:DIL_HPG, 1024:1024 + 3 * TW]
        t5_out = tk[0:DIL_HPG, 2560:2560 + 3 * TW]
        t5_tab = work[0:T5_BUCKETS, 0:12]
        na_pad = tk[0:NA_HEADS * NDR, 4096:4096 + RW]

        moe_slot = [ring[:, i, :] for i in range(RING)] + [zbuf[:, 0:4096], tk[:, 0:4096]]
        aT = zbuf[:, 4096:5120].rearrange("p (c n) -> p c n", c=4)
        uT = zbuf[:, 5120:6144].rearrange("p (c n) -> p c n", c=4)
        w_gate = zbuf[:, 6144:6144 + T * N_EXP].rearrange("p (t n) -> p t n", t=T)
        route = zbuf[:, 6400:6400 + 256]
        route_u = zbuf[:, 6656:6672].bitcast(U32)
        rbias = zbuf[:, 6700:6736]
        picked = zbuf[:, 6800:6864].rearrange("p (t n) -> p t n", t=T)
        rank = zbuf[:, 6864:6928].rearrange("p (t n) -> p t n", t=T)
        w_over = zbuf[:, 6928:6992].rearrange("p (t n) -> p t n", t=T)
        below = zbuf[:, 6992:7056].rearrange("p (t n) -> p t n", t=T)
        over = zbuf[:, 7056:7058]
        flag = zbuf[:, 7058:7059].bitcast(U32)
        all_ones = gvec[:, 0:P]
        earlier = gvec[:, P:2 * P]
        xe = mod[:, 0:1024].rearrange("p (k n) -> p k n", k=KT)
        eout = mod[:, 1024:2048]
        selT = mod[:, 2048:2304].rearrange("p (t n) -> p t n", t=T)
        sel = mod[:, 2304:2560].rearrange("p (t n) -> p t n", t=T)
        selg = mod[:, 2560:2816].rearrange("p (t n) -> p t n", t=T)
        hid = mod[:, 2816:3328].rearrange("p (e f n) -> p e f n", e=2, f=4)
        hidu = mod[:, 3328:3840].rearrange("p (e n) -> p e n", e=2)
        w_e = [a["w1_2"][0], a["w3_2"][0], a["w2_2"][0]]

        block = ctx.enter_context(nc.Block())

        def moe_view(s, j):
            return moe_slot[s].rearrange("p (k c) -> p k c", k=KT if j < 2 else 4)

        def moe_src(j, e):
            w = w_e[j]
            v = w.rearrange("e (k p) n -> p e k n", p=P)
            if isinstance(e, int):
                return v[:, e, :, :]
            return v[:, bass.ds(e, 1), :, :].rearrange("p o k n -> p (o k) n")

        @block.sync
        def _(sync):
            sync.dma_start(x[:], a["x"][0].rearrange("(t p) n -> p t n", p=P)).then_inc(loaded, 16)
            sync.dma_start(cst[:], a["cst"]).then_inc(loaded, 16)
            sync.dma_start(cact[:], a["c"][0].rearrange("(k p) -> p k", p=P)).then_inc(loaded, 16)
            sync.dma_start(gains[:], a["gains"]).then_inc(loaded, 16)
            sync.dma_start(convw[:], a["conv_cols"]).then_inc(loaded, 16)
            sync.dma_start(gate_w[:], a["ev_w_in"][0][:, 2048:2056].rearrange("(k p) n -> p k n", p=P)).then_inc(loaded, 16)
            sync.dma_start(gate_b[:, 0:1], a["ev_igate_b"].rearrange("o h -> h o")).then_inc(loaded, 16)
            sync.dma_start(gate_b[:, 1:2], a["ev_fgate_b"].rearrange("o h -> h o")).then_inc(loaded, 16)
            sync.dma_start(ada_b[:], a["ada_b"][0].rearrange("(n c) -> n c", n=12)).then_inc(loaded, 16)
            sync.dma_start(gw36[:, :, 0:4], a["w_r1_2"][0].rearrange("(k p) n -> p k n", p=P)).then_inc(loaded, 16)
            sync.dma_start(gw36[:, :, 4:36], a["w_r2_2"][0].rearrange("(k p) n -> p k n", p=P)).then_inc(loaded, 16)
            for n, (name, w, _) in enumerate(slots):
                if n >= RING:
                    sync.wait_ge(gemm_done, group_of[n - RING] + len(slots[n - RING][2]))
                if n == phase_slots["ada1"][0]:
                    sync.dma_start(ada_b[:], a["ada_b"][1].rearrange("(n c) -> n c", n=12)).then_inc(ada_b_in, 16)
                dst = ring[:, n % RING, :].rearrange("p (k c) -> p k c", k=KT)
                sync.dma_start(dst, w).then_inc(w_landed[n % RING], 16)
            sync.wait_ge(gemm_done, g_n)
            sync.wait_ge(h_ready, 2 * len(NORMS))
            for s in range(MOE_RING):
                e, j = divmod(s, 3)
                sync.dma_start(moe_view(s, j), moe_src(j, e)).then_inc(e_in[s], 16)
            with sync.Fori(1, N_EXP // 2) as i:
                for s in range(MOE_RING):
                    e, j = divmod(s, 3)
                    sync.wait_ge(up_done if j < 2 else down_done, i * 2 + (e + 1 - 2))
                    sync.dma_start(moe_view(s, j), moe_src(j, i * 2 + e)).then_inc(e_in[s], 16)
            sync.wait_ge(flag_ready, 1)
            with sync.If(sync.value_load(flag[0:1, 0:1], min_val=0, max_val=2 * S) > 0):
                sync.wait_ge(up_done, N_EXP)
                sync.wait_ge(down_done, N_EXP)
                for s in range(MOE_RING):
                    e, j = divmod(s, 3)
                    sync.dma_start(moe_view(s, j), moe_src(j, e)).then_inc(f_in[s], 16)
                with sync.Fori(1, N_EXP // 2) as i:
                    for s in range(MOE_RING):
                        e, j = divmod(s, 3)
                        if j < 2:
                            sync.wait_ge(e_up, i * 8 + (4 * e + 2 * j + 2 - 8))
                        else:
                            sync.wait_ge(e_down, i * 8 + (4 * e + 4 - 8))
                        sync.dma_start(moe_view(s, j), moe_src(j, i * 2 + e)).then_inc(f_in[s], 16)
            sync.wait_ge(x_ready, 6 * T)
            sync.dma_start(out[0].rearrange("(t p) n -> p t n", p=P), x[:]).then_inc(out_done, 16)
            sync.wait_ge(out_done, 16)

        @block.gpsimd
        def _(pool):
            own = [0]

            def link(ins):
                own[0] += 1
                ins.then_inc(pool_own, 1)
                pool.wait_ge(pool_own, own[0])

            def load_gain(n, src):
                if n >= 1:
                    pool.wait_ge(gvec_used, T * n)
                row = bass.AP(tensor=src.tensor, offset=src.offset, ap=[[0, P], [1, D]])
                pool.dma_start(gvec[:], row).then_inc(gvec_in, 16)

            load_gain(0, a["norm_mix_g"][0])
            link(pool.memset(na_pad, 0.0))
            for hh in range(NA_HEADS):
                pool.dma_start(na_pad[hh * NDR:(hh + 1) * NDR, GRID_W - 16:GRID_W + 15],
                               a["na_rpb_2"][0, hh, 4:4 + NDR, :]).then_inc(t5_in, 16)
            pool.dma_start(t5_hot, a["t5_hot"]).then_inc(t5_in, 16)
            pool.dma_start(t5_mask.rearrange("p (g n) -> p g n", g=3), a["t5_mask"]).then_inc(t5_in, 16)
            pool.dma_start(t5_tab, a["t5_table_2"]).then_inc(t5_in, 16)
            pool.wait_ge(t5_in, 16 * (NA_HEADS + 3))
            pool.dma_start(na_rows, na_pad).then_inc(na_w, 16)
            pool.wait_ge(na_w, 16)
            W = NA_HEADS * NDR * RW
            pool.dma_start(na_rep, bass.AP(tensor=na_rows.tensor, offset=0, ap=[[0, GRID_W], [1, W]])).then_inc(na_w, 16)
            pool.wait_ge(t5_sum, 1)
            pool.dma_start(t5_rows.rearrange("(g h) n -> h g n", g=3), t5_out.rearrange("p (g n) -> p g n", g=3)).then_inc(t5_w, 16)
            pool.wait_ge(t5_w, 16)
            pool.dma_start(t5_rep, bass.AP(tensor=t5_rows.tensor, offset=0, ap=[[0, P], [1, 12 * TW]])).then_inc(t5_w, 16)
            pool.wait_ge(t5_w, 32)
            pool.wait_ge(na_w, 32)
            pool.dma_start(mnorm, bass.AP(tensor=a["ev_mnorm_g"].tensor, offset=0, ap=[[0, P], [1, 512]])).then_inc(mem_in, 16)

            pool.dma_start(lam_rows[:], bass.AP(tensor=a["od_lam"].tensor, offset=0, ap=[[0, P], [64, 4], [1, 64]])).then_inc(lam_in, 16)
            pool.dma_start(onorm, bass.AP(tensor=a["od_onorm_g"].tensor, offset=0, ap=[[0, P], [1, P]])).then_inc(lam_in, 16)
            load_gain(1, a["norm_ffn_g"][0])

            def peer(l):
                table = [a["peer_u"], a["peer_v"]]
                pool.wait_ge(gemm_moved, last_group[f"out{l}"])
                pool.wait_ge(y_ready, l + 1)
                pool.dma_start(keys, a["peer_keys"][l].rearrange("c n d -> n c d")).then_inc(keys_in, 16)

                def gather(phase, k, n, free=None):
                    t, which = divmod(phase % 4, 2)
                    if free is not None:
                        pool.wait_ge(*free)
                        pool.sem_inc(row_free, 1)
                    col = n - phase * SLOTS
                    src = idx[:, t, col:col + 1] if isinstance(col, int) else idx[:, t, bass.ds(col, 1)]
                    pool.tensor_copy(stage[:, k:k + 1], src).then_inc(idx_staged, 1)
                    pool.wait_ge(idx_staged, n + 1)
                    pool.sem_inc(row_free, 1)
                    pool.indirect_dma_start(rowbuf[:, k, :], None, table[which].rearrange("l n d -> (l n) d"),
                                            bass.IndirectOffsetOnAxis(ap=stage[:, k:k + 1], axis=0)).then_inc(row_in[k], 16)

                pool.wait_ge(sub_done, 8 * (l + 1))
                for phase in range(4 * l, 4 * l + 4):
                    t, which = divmod(phase % 4, 2)
                    mine, other = (udot, vsum) if which == 0 else (vsum, udot)
                    base = (2 * l + t) * SLOTS
                    if which == 0:
                        pool.wait_ge(idx_ready, 2 * l + t + 1)
                        other_base = base
                    else:
                        other_base = base + SLOTS
                    for k in range(ROWS):
                        free = None if phase == 4 * l else (other, other_base - ROWS + k + 1)
                        gather(phase, k, phase * SLOTS + k, free)
                    with pool.Fori(1, GROUPS) as i:
                        for k in range(ROWS):
                            n = i * ROWS + (phase * SLOTS + k)
                            pool.wait_ge(mine, i * ROWS + (base - ROWS + k + 1))
                            pool.sem_inc(row_free, 1)
                            pool.tensor_copy(stage[:, k:k + 1], idx[:, t, bass.ds(i * ROWS + k, 1)]).then_inc(idx_staged, 1)
                            pool.wait_ge(idx_staged, n + 1)
                            pool.sem_inc(row_free, 1)
                            pool.indirect_dma_start(rowbuf[:, k, :], None, table[which].rearrange("l n d -> (l n) d"),
                                                    bass.IndirectOffsetOnAxis(ap=stage[:, k:k + 1], axis=0)).then_inc(row_in[k], 16)

            peer(0)
            load_gain(2, a["norm_mix_g"][1])
            load_gain(3, a["norm_ffn_g"][1])
            peer(1)
            load_gain(4, a["g_mem_2"][0])
            pool.wait_ge(x_ready, 4 * T)
            pool.dma_start(y[:], a["mem_2"][0].rearrange("(t p) n -> p t n", p=P)).then_inc(mem_in, 16)
            pool.dma_start(dil_bias, bass.AP(tensor=t5_rep.tensor, offset=127,
                                             ap=[[12 * TW - 1, P], [TW, 12], [1, 384]])).then_inc(bias_in, 16)
            W = NA_HEADS * NDR * RW
            for hh in range(NA_HEADS):
                for r2 in range(2):
                    pool.dma_start(na_bias[r2 * GRID_W:(r2 + 1) * GRID_W, hh, :].rearrange("p (j n) -> p j n", j=6),
                                   bass.AP(tensor=na_rep.tensor,
                                           offset=hh * NDR * RW + (1 - r2) * RW + GRID_W - 1,
                                           ap=[[W - 1, GRID_W], [RW, 6], [1, GRID_W]])).then_inc(bias_in, 16)
            load_gain(5, a["g_mix_2"][0])
            load_gain(6, a["g_ffn_2"][0])
            pool.wait_ge(h_ready, 2 * len(NORMS))
            pool.dma_start(rbias[:, 0:4], bass.AP(tensor=a["b_r1_2"].tensor, offset=0, ap=[[0, P], [1, 4]])).then_inc(r_in, 16)
            pool.dma_start(rbias[:, 4:36], bass.AP(tensor=a["b_r2_2"].tensor, offset=0, ap=[[0, P], [1, 32]])).then_inc(r_in, 16)

        @block.tensor
        def _(pe):
            def project(name, lhs=None):
                for n in phase_slots[name]:
                    _, _, groups = slots[n]
                    w = ring[:, n % RING, :].rearrange("p (k c) -> p k c", k=KT)
                    pe.wait_ge(w_landed[n % RING], 16 * (n // RING + 1))
                    for i, grp in enumerate(groups):
                        g = group_of[n] + i
                        if g >= 2:
                            pe.wait_ge(gemm_moved, g - 1)
                        bank = gp[:, g % 2, :]
                        if grp[0] == "bcast":
                            for k in range(KT):
                                pe.matmul(bank, cact[:, k:k + 1].to_broadcast([P, P]), w[:, k, :], start=k == 0, stop=False)
                            mm = pe.matmul(bank, ident[0:12, grp[1]:grp[1] + 1].to_broadcast([12, P]), ada_b[:, :],
                                           start=False, stop=True)
                        elif grp[0] == "rows":
                            for k in range(KT):
                                mm = pe.matmul(bank, hT[:, k, grp[1] * P:(grp[1] + 1) * P], w[:, k, :],
                                               start=k == 0, stop=k == KT - 1)
                        elif grp[0] == "rows2":
                            for t in range(T):
                                for k in range(KT):
                                    mm = pe.matmul(bank[:, t * S:(t + 1) * S], hT[:, k, t * P:(t + 1) * P],
                                                   w[:, k, grp[1]:grp[1] + S], start=k == 0, stop=k == KT - 1)
                        else:
                            for c in range(2):
                                for k in range(KT):
                                    mm = pe.matmul(bank[:, c * S:(c + 1) * S], w[:, k, grp[1] + c * P:grp[1] + (c + 1) * P],
                                                   hT[:, k, :], start=k == 0, stop=k == KT - 1)
                        mm.then_inc(gemm_done, 1)

            turned = [0]

            def turn(src):
                for t in range(T):
                    for b in range(2):
                        n = turned[0]
                        if n >= 2:
                            pe.wait_ge(turn_moved, n - 1)
                        for c in range(4):
                            k = 4 * b + c
                            mm = pe.transpose(tp[:, n % 2, c * P:(c + 1) * P], src[:, t, k * P:(k + 1) * P], ident)
                        mm.then_inc(turn_done, 1)
                        turned[0] += 1

            def turn_h(n):
                pe.wait_ge(h_ready, T * (n + 1))
                turn(h if NORMS[n] != "mem" else y)

            def hT_ready():
                pe.wait_ge(turn_moved, turned[0])

            def head_sums(stage_name):
                for i in range(len(QK[stage_name])):
                    n = qk_base[stage_name] + i
                    pe.wait_ge(qk_sq, n + 1)
                    if i >= 2:
                        pe.wait_ge(qk_root, n - 1)
                    pe.matmul(tp[:, i % 2, :], blk, work[:, (i % 2) * 512:(i % 2) * 512 + 512],
                              start=True, stop=True).then_inc(qk_sum, 1)

            def attention(stage_name):
                units, segs = att[stage_name]
                b0 = seg_base[stage_name]
                u0 = unit_base[stage_name]
                for j in range(len(segs) + LAG + 1):
                    if j < len(segs):
                        sg = segs[j]
                        if j >= 2:
                            pe.wait_ge(s_read, b0 + j - 1)
                        pe.matmul(sp_[:, j % 2, 0:sg["nk"]], sg["q"], sg["k"], start=True, stop=True).then_inc(s_done, 1)
                    i = j - LAG
                    if 0 <= i < len(segs):
                        sg = segs[i]
                        pe.wait_ge(e_done, u0 + sg["u"] + 1)
                        if i >= 2:
                            pe.wait_ge(t_moved, b0 + i - 1)
                        for c in range(sg["nk"] // P):
                            mm = pe.transpose(tp[:, i % 2, c * P:(c + 1) * P], segbuf[:, i % SEGS, c * P:(c + 1) * P], ident)
                        mm.then_inc(t_done, 1)
                    i = j - LAG - 1
                    if 0 <= i < len(segs):
                        sg = segs[i]
                        pe.wait_ge(t_moved, b0 + i + 1)
                        if sg["first"] and sg["u"] >= 2:
                            pe.wait_ge(o_read, u0 + sg["u"] - 1)
                        nkt = sg["nk"] // P
                        for c in range(nkt):
                            mm = pe.matmul(op[:, sg["u"] % 2, 0:sg["dv"]], ptbuf[:, i % 2, c * P:(c + 1) * P],
                                           zn[:, c, sg["v"]:sg["v"] + sg["dv"]],
                                           start=sg["first"] and c == 0, stop=sg["last"] and c == nkt - 1)
                        mm.then_inc(o_done, 1)

            def mlstm():
                for part in range(2):
                    for k in range(KT):
                        mm = pe.matmul(sp_[0:4, part, 0:S], gate_w[:, k, 4 * part:4 * part + 4], hT[:, k, :],
                                       start=k == 0, stop=k == KT - 1)
                mm.then_inc(gates_mm, 1)
                pe.wait_ge(gates_g, 1)
                for c, row in enumerate((G_, EM_)):
                    for t in range(T):
                        mm = pe.transpose(tp[:, 0, 4 * (2 * c + t):4 * (2 * c + t) + 4], row[:, t * P:(t + 1) * P], ident[0:4, 0:4])
                mm.then_inc(gates_t, 1)
                pe.wait_ge(silu_done, 8)
                pe.wait_ge(gates_c, 1)
                for hh in range(M_HEADS):
                    if hh >= 2:
                        pe.wait_ge(mm_p, hh - 1)
                        pe.wait_ge(mm_arg, hh - 1)
                    q, k = zt(hh), zt(4 + hh)
                    pe.matmul(tp[:, hh % 2, 0:S], ident[0:4, hh:hh + 1].to_broadcast([4, P]), NM_,
                              start=True, stop=True).then_inc(mm_b, 1)
                    pe.matmul(sp_[:, hh % 2, 0:S], k[:, 0:P], q, start=True, stop=True)
                    pe.matmul(sp_[:, hh % 2, S:S + P], k[:, P:S], q[:, P:S], start=True, stop=True).then_inc(mm_s, 1)
                    pe.wait_ge(mm_p, hh + 1)
                    if hh >= 2:
                        pe.wait_ge(mm_read, hh - 1)
                    pt = ml_p[:, hh % 2, :]
                    o = op[:, hh % 2, :]
                    for rhs, c0, w in ((None, 0, P), (ones1, S, 1)):
                        for t in range(T):
                            for u in range(t + 1):
                                r = ones1[:, 0:1] if rhs is not None else zn[:, u, P * hh:P * (hh + 1)]
                                mm = pe.matmul(o[:, c0 + t * w:c0 + (t + 1) * w], pt[:, (t + u) * P:(t + u + 1) * P], r,
                                               start=u == 0, stop=u == t)
                    mm.then_inc(mm_o, 1)

            def peer(l):
                pe.wait_ge(keys_in, 16 * (l + 1))
                for c in range(2):
                    mm = pe.transpose(op[:, 0, c * P:(c + 1) * P], keys[:, c, :], ident)
                mm.then_inc(keys_t, 1)
                pe.wait_ge(keys_m, l + 1)
                pe.wait_ge(gemm_moved, last_group[f"wq{l}"])
                for t in range(T):
                    for b in range(4):
                        n = (2 * l + t) * 4 + b
                        if n >= 2:
                            pe.wait_ge(sub_moved, n - 1)
                        for c in range(4):
                            i = 4 * b + c
                            mm = pe.matmul(sp_[:, n % 2, c * P:(c + 1) * P], zt(i)[:, t * P:(t + 1) * P], keysT[:, i % 2, :],
                                           start=True, stop=True)
                        mm.then_inc(sub_done, 1)

            def peer_sum(l):
                for t in range(T):
                    phase = 4 * l + 2 * t + 1
                    base = (2 * l + t) * SLOTS
                    if l + t > 0:
                        pe.wait_ge(x_ready, T * (2 * l + 1) + t)

                    def add(i, k, first=False, last=False):
                        pe.wait_ge(row_in[k], i * 16 + 16 * (phase * GROUPS + 1))
                        pe.wait_ge(diag_ready, i * ROWS + (base + k + 1))
                        for n in range(2):
                            mm = pe.matmul(op[:, n, :], diag[:, k % 4, :], rowbuf[:, k, n * 512:(n + 1) * 512],
                                           start=first, stop=last, skip_group_check=True)
                        mm.then_inc(vsum, 1)

                    for k in range(ROWS):
                        add(0, k, first=k == 0)
                    with pe.Fori(1, GROUPS - 1) as i:
                        for k in range(ROWS):
                            add(i, k)
                    for k in range(ROWS):
                        add(GROUPS - 1, k, last=k == ROWS - 1)

            pe.wait_ge(loaded, 16 * NLOADS)
            pe.wait_ge(t5_in, 16 * (NA_HEADS + 3))
            for g in range(DIL_GROUPS):
                mm = pe.matmul((sp_ if g < 2 else op)[0:DIL_HPG, g % 2, 0:TW], t5_tab[:, g * DIL_HPG:(g + 1) * DIL_HPG], t5_hot,
                               start=True, stop=True)
            mm.then_inc(t5_mm, 1)
            pe.wait_ge(c_ready, 1)
            project("ada0")
            turn_h(0)
            hT_ready()
            pe.wait_ge(t5_sum, 1)
            project("in0")
            mlstm()
            head_sums("moba")
            pe.wait_ge(qk_done, len(QK["moba"]))
            attention("moba")
            pe.wait_ge(y_ready, 1)
            turn(y)
            hT_ready()
            project("out0")
            for l in range(2):
                turn_h(2 * l + 1)
                hT_ready()
                project(f"wq{l}")
                peer(l)
                if l == 0:
                    pe.wait_ge(ada_b_in, 16)
                    project("ada1")
                peer_sum(l)
                turn_h(2 * l + 2)
                hT_ready()
                if l == 0:
                    project("in1")
                    head_sums("diff")
                    pe.wait_ge(qk_done, qk_base["block2"])
                    attention("diff")
                    pe.wait_ge(y_ready, 2)
                    turn(y)
                    hT_ready()
                    project("out1")
            project("mem")
            turn_h(5)
            hT_ready()
            project("in2")
            head_sums("block2")
            pe.wait_ge(qk_done, qk_base["block2"] + len(QK["block2"]))
            attention("block2")
            pe.wait_ge(y_ready, 3)
            turn(y)
            hT_ready()
            project("out2")
            turn_h(6)
            hT_ready()
            for t in range(T):
                for k in range(KT):
                    mm = pe.matmul(op[:, t, 0:36], hT[:, k, t * P:(t + 1) * P], gw36[:, k, :], start=k == 0, stop=k == KT - 1)
            mm.then_inc(r_mm, 1)

            def expert(s0, i):
                e2 = s0 // 3
                for j in range(2):
                    pe.wait_ge(f_in[s0 + j], i * 16 + 16)
                    w = moe_slot[s0 + j].rearrange("p (k c) -> p k c", k=KT)
                    for b in range(2):
                        if not (isinstance(i, int) and e2 == 0):
                            pe.wait_ge(e_act, i * 4 + (2 * e2 + b - 1))
                        bank = (sp_ if j == 0 else gp)[:, b, :]
                        for c in range(2):
                            f = 2 * b + c
                            for k in range(KT):
                                mm = pe.matmul(bank[:, c * S:(c + 1) * S], w[:, k, f * P:(f + 1) * P], hT[:, k, :],
                                               start=k == 0, stop=k == KT - 1)
                        mm.then_inc(e_up, 1)
                pe.wait_ge(f_in[s0 + 2], i * 16 + 16)
                w = moe_slot[s0 + 2].rearrange("p (k c) -> p k c", k=4)
                pe.wait_ge(e_act, i * 4 + (2 * e2 + 2))
                for t in range(T):
                    for n in range(2):
                        if not (isinstance(i, int) and e2 == 0):
                            pe.wait_ge(e_acc, i * 8 + (4 * e2 + 2 * t + n - 3))
                        bank = (tp if t == 0 else op)[:, n, :]
                        for f in range(4):
                            mm = pe.matmul(bank, aT[:, f, t * P:(t + 1) * P], w[:, f, n * 512:(n + 1) * 512],
                                           start=f == 0, stop=f == 3)
                        mm.then_inc(e_down, 1)

            pe.wait_ge(r_done, 1)
            pe.matmul(tp[:, 0, 0:N_EXP], earlier, picked[:, 0, :], start=True, stop=True)
            pe.matmul(tp[:, 0, N_EXP:2 * N_EXP], all_ones, picked[:, 0, :], start=True, stop=False)
            pe.matmul(tp[:, 0, N_EXP:2 * N_EXP], earlier, picked[:, 1, :], start=False, stop=True).then_inc(rank_done, 1)
            pe.wait_ge(over_ready, 1)
            pe.matmul(tp[:, 1, 0:1], all_ones, over[:, 0:1], start=True, stop=True).then_inc(over_sum, 1)
            pe.wait_ge(flag_ready, 1)

            def gather_pair(p):
                pe.wait_ge(sel_ready, p + 1)
                if not isinstance(p, int):
                    pe.wait_ge(xe_moved, p)
                for k in range(KT):
                    for t in range(T):
                        mm = pe.matmul(op[:, k // 4, (k % 4) * P:(k % 4 + 1) * P], h[:, t, k * P:(k + 1) * P], sel[:, t, :],
                                       start=t == 0, stop=t == T - 1)
                mm.then_inc(gath_done, 1)

            def up(e2, p):
                for j in range(2):
                    pe.wait_ge(e_in[3 * e2 + j], p * 16 + 16)
                pe.wait_ge(xe_moved, p + 1)
                if not isinstance(p, int):
                    pe.wait_ge(up_act, p * 2 + (e2 - 1))
                for j in range(2):
                    w = moe_slot[3 * e2 + j].rearrange("p (k c) -> p k c", k=KT)
                    for f in range(4):
                        for k in range(KT):
                            mm = pe.matmul(gp[:, e2, (4 * j + f) * CAP:(4 * j + f + 1) * CAP], w[:, k, f * P:(f + 1) * P],
                                           xe[:, k, e2 * CAP:(e2 + 1) * CAP], start=k == 0, stop=k == KT - 1)
                mm.then_inc(up_done, 1)

            def scatter(p):
                pe.wait_ge(down_moved, p + 1)
                pe.wait_ge(selt_moved, p * 2 + 2)
                for n in range(4):
                    if n >= 2:
                        pe.wait_ge(scat_read, p * 4 + (n - 1))
                    pe.matmul(tp[:, n % 2, :], selT[:, n // 2, :], eout[:, (n % 2) * 512:(n % 2 + 1) * 512],
                              start=True, stop=True).then_inc(scat_done, 1)

            def turn_sel(p, before):
                pe.wait_ge(sel_ready, p + 1)
                for t in range(T):
                    if before:
                        pe.wait_ge(scat_read, p * 4 - (1 - t))
                    pe.transpose(tp[:, t, 0:P], selg[:, t, :], ident).then_inc(selt_done, 1)

            def down(p):
                if not isinstance(p, int):
                    pe.wait_ge(down_moved, p)
                for e2 in range(2):
                    pe.wait_ge(e_in[3 * e2 + 2], p * 16 + 16)
                    pe.wait_ge(up_act, p * 2 + (e2 + 1))
                    w = moe_slot[3 * e2 + 2].rearrange("p (k c) -> p k c", k=4)
                    for n in range(2):
                        for f in range(4):
                            mm = pe.matmul(sp_[e2 * CAP:(e2 + 1) * CAP, n, :], hid[:, e2, f, :], w[:, f, n * 512:(n + 1) * 512],
                                           start=f == 0, stop=f == 3)
                    mm.then_inc(down_done, 1)

            gather_pair(0)
            up(0, 0)
            turn_sel(0, False)
            up(1, 0)
            gather_pair1 = 1
            pe.wait_ge(sel_ready, 2)
            pe.wait_ge(xe_moved, 1)
            for k in range(KT):
                for t in range(T):
                    mm = pe.matmul(op[:, k // 4, (k % 4) * P:(k % 4 + 1) * P], h[:, t, k * P:(k + 1) * P], sel[:, t, :],
                                   start=t == 0, stop=t == T - 1)
            mm.then_inc(gath_done, 1)
            down(0)
            with pe.Fori(1, N_EXP // 2 - 1) as p:
                up(0, p)
                scatter(p - 1)
                turn_sel(p, True)
                up(1, p)
                gather_pair(p + 1)
                down(p)
            last = N_EXP // 2 - 1
            pe.wait_ge(up_act, 2 * last)
            up(0, last)
            scatter(last - 1)
            turn_sel(last, True)
            up(1, last)
            pe.wait_ge(down_moved, last)
            down(last)
            scatter(last)
            with pe.If(pe.value_load(flag[0:1, 0:1], min_val=0, max_val=2 * S) > 0):
                pe.wait_ge(scat_read, 2 * N_EXP)
                pe.wait_ge(down_moved, N_EXP // 2)
                expert(0, 0)
                expert(3, 0)
                with pe.Fori(1, N_EXP // 2) as i:
                    expert(0, i)
                    expert(3, i)

        @block.scalar
        def _(act):
            own = [0]

            def link(ins):
                own[0] += 1
                ins.then_inc(act_own, 1)
                act.wait_ge(act_own, own[0])

            def move(name):
                for n in phase_slots[name]:
                    for i, grp in enumerate(slots[n][2]):
                        g = group_of[n] + i
                        act.wait_ge(gemm_done, g + 1)
                        bank = gp[:, g % 2, :]
                        if grp[0] == "bcast":
                            m, half = divmod(grp[1], 2)
                            dst = mod[:, m * D + half * CH:m * D + (half + 1) * CH] if m < 5 else \
                                g2[:, int(name[-1]), half * CH:(half + 1) * CH]
                        elif grp[0] == "cols":
                            dst = zt2(grp[2])
                        else:
                            buf, c0 = grp[2]
                            buf = zn if buf == "zn" else y
                            if grp[0] == "rows":
                                dst = buf[:, grp[1], c0:c0 + CH]
                            else:
                                dst = buf[:, :, c0:c0 + S]
                                bank = bank.rearrange("p (t n) -> p t n", t=T)
                        act.activation(dst, bank, ACT.Copy).then_inc(gemm_moved, 1)

            turned = [0]

            def move_turned():
                for t in range(T):
                    for b in range(2):
                        n = turned[0]
                        act.wait_ge(turn_done, n + 1)
                        act.activation(hT[:, 4 * b:4 * b + 4, t * P:(t + 1) * P],
                                       tp[:, n % 2, :].rearrange("p (c n) -> p c n", c=4), ACT.Copy).then_inc(turn_moved, 1)
                        turned[0] += 1

            def norm(n):
                act.wait_ge(sumsq, n + 1)
                act.activation(small[:, 62:64], small[:, 60:62], ACT.Sqrt).then_inc(rootd, 1)

            def head_norms(stage_name):
                q = QK[stage_name]
                n0 = qk_base[stage_name]
                for i in range(len(q) + 1):
                    if i < len(q):
                        if i >= 2:
                            act.wait_ge(qk_done, n0 + i - 1)
                        act.activation(work[:, (i % 2) * 512:(i % 2) * 512 + 512], zt2(q[i][0]), ACT.Square).then_inc(qk_sq, 1)
                    if i >= 1:
                        m = i - 1
                        act.wait_ge(qk_sum, n0 + m + 1)
                        act.activation(work[:, (m % 2) * 512:(m % 2) * 512 + 512], tp[:, m % 2, :], ACT.Sqrt,
                                       scale=1.0 / 64, bias=eps[:, 0:1]).then_inc(qk_root, 1)

            def attention(stage_name):
                units, segs = att[stage_name]
                b0 = seg_base[stage_name]
                u0 = unit_base[stage_name]
                for j in range(len(segs) + LAG):
                    if j < len(segs) and segs[j]["last"]:
                        u = segs[j]["u"]
                        n = units[u]["n"]
                        act.wait_ge(m_done, u0 + u + 1)
                        r = (j - n + 1) % SEGS
                        w = (n - 1) * S + segs[j]["nk"]
                        lp = work[:, r * S:r * S + w]
                        act.activation(lp, lp, ACT.Exp, bias=nmax[:, u % 8:u % 8 + 1],
                                       accum_out=den[:, u % 8:u % 8 + 1]).then_inc(e_done, 1)
                    i = j - LAG
                    if 0 <= i < len(segs):
                        nk = segs[i]["nk"]
                        act.wait_ge(t_done, b0 + i + 1)
                        if i >= 2:
                            act.wait_ge(o_done, b0 + i - 1)
                        act.activation(ptbuf[:, i % 2, 0:nk], tp[:, i % 2, 0:nk], ACT.Copy).then_inc(t_moved, 1)

            def mlstm():
                for part, (dst, c) in enumerate(((I_, 0), (F_, 1))):
                    act.wait_ge(gates_mm, 1)
                    if part == 0:
                        act.wait_ge(mem_in, 16)
                    ins = act.activation(dst, sp_[0:4, part, 0:S], ACT.Identity, bias=gate_b[:, c:c + 1])
                ins.then_inc(gates_f, 1)
                act.wait_ge(gates_e, 1)
                link(act.activation(E_, A_, ACT.Exp, scale=-1.0))
                act.activation(E_, E_, ACT.Ln, bias=ones1[0:4, 0:1]).then_inc(gates_l, 1)
                act.wait_ge(gates_e, 2)
                act.activation(EM_, EM_, ACT.Exp, scale=-1.0).then_inc(em_ready, 1)
                act.wait_ge(gates_t, 1)
                act.activation(small[:, 0:16], tp[:, 0, 0:16], ACT.Copy).then_inc(gates_c, 1)
                for c in range(8):
                    act.wait_ge(conv_done, c + 1)
                    acc = work[:, (c % SEGS) * S:(c % SEGS + 1) * S]
                    act.activation(zt(c), acc, ACT.Silu).then_inc(silu_done, 1)
                act.wait_ge(gates_c, 1)
                for hh in range(M_HEADS):
                    act.wait_ge(mm_arg, hh + 1)
                    arg = ml_arg[:, hh % 2, :]
                    act.activation(arg[:, 0:S], arg[:, 0:S], ACT.Exp, bias=ml_cols[:, 0, 0, hh:hh + 1])
                    act.activation(arg[:, S:S + P], arg[:, S:S + P], ACT.Exp, bias=ml_cols[:, 0, 1, hh:hh + 1]).then_inc(mm_exp, 1)
                act.activation(mo_sig, zn[:, :, 512:1024], ACT.Sigmoid).then_inc(sig_done, 1)
                act.wait_ge(hn_sq, 1)
                act.activation(small[:, 32:40], small[:, 24:32], ACT.Sqrt).then_inc(hn_rt, 1)

            def peer(l):
                act.wait_ge(keys_t, l + 1)
                act.activation(keysT, op[:, 0, 0:S].rearrange("p (c n) -> p c n", c=2), ACT.Copy).then_inc(keys_m, 1)
                move_sub(l, 0)
                exp_scores(l, 0)
                move_sub(l, 1)

            def move_sub(l, t):
                for b in range(4):
                    n = (2 * l + t) * 4 + b
                    act.wait_ge(sub_done, n + 1)
                    if 2 * l + t > 0 and b == 0:
                        act.wait_ge(sub_free, 2 * l + t)
                    act.activation(sub[:, 4 * b:4 * b + 4, :], sp_[:, n % 2, :].rearrange("p (c n) -> p c n", c=4),
                                   ACT.Copy).then_inc(sub_moved, 1)

            def exp_scores(l, t):
                act.wait_ge(top_ready, 2 * l + t + 1)
                act.activation(gate[:, t, :], gate[:, t, :], ACT.Exp).then_inc(gate_e, 1)

            def peer_coef(l, t):
                n = 2 * l + t
                act.wait_ge(dots_all, n + 1)
                act.activation(coef[:, :], dots[:, :], ACT.Gelu).then_inc(gelu_done, 1)
                act.wait_ge(coef_ready, n + 1)
                base = n * SLOTS
                for k in range(ROWS):
                    if k >= 4:
                        act.wait_ge(vsum, base + k - 3)
                    elif n > 0:
                        act.wait_ge(vsum, base)
                    act.activation(diag[:, k % 4, :], ident, ACT.Copy, scale=coef[:, k:k + 1]).then_inc(diag_ready, 1)
                with act.Fori(1, GROUPS) as i:
                    for k in range(ROWS):
                        act.wait_ge(vsum, i * ROWS + (base + k - 3))
                        act.sem_inc(diag_free, 1)
                        act.activation(diag[:, k % 4, :], ident, ACT.Copy, scale=coef[:, bass.ds(i * ROWS + k, 1)]).then_inc(diag_ready, 1)

            act.wait_ge(loaded, 16 * NLOADS)
            act.activation(cact[:], cact[:], ACT.Silu).then_inc(c_ready, 1)
            move("ada0")
            norm(0)
            move_turned()
            move("in0")
            mlstm()
            head_norms("moba")
            attention("moba")
            move_turned()
            move("out0")
            for l in range(2):
                norm(2 * l + 1)
                move_turned()
                move(f"wq{l}")
                peer(l)
                if l == 0:
                    move("ada1")
                peer_coef(l, 0)
                exp_scores(l, 1)
                peer_coef(l, 1)
                norm(2 * l + 2)
                move_turned()
                if l == 0:
                    act.wait_ge(lam_s, 1)
                    act.activation(small[:, 42:44], small[:, 40:42], ACT.Exp).then_inc(lam_e, 1)
                    move("in1")
                    head_norms("diff")
                    attention("diff")
                    act.wait_ge(hn_sq, 2)
                    act.activation(small[:, 0:16], small[:, 0:16], ACT.Sqrt).then_inc(hn_rt, 1)
                    move_turned()
                    move("out1")
            move("mem")
            norm(5)
            move_turned()
            move("in2")
            head_norms("block2")
            attention("block2")
            move_turned()
            move("out2")
            norm(6)
            move_turned()
            act.wait_ge(r_pre, 1)
            act.activation(route[:, 128:136], route[:, 128:136], ACT.Exp).then_inc(r_exp, 1)
            act.wait_ge(r_pre, 2)
            act.activation(route[:, 136:138], route[:, 136:138], ACT.Exp).then_inc(r_exp, 1)

            def expert(e2, i):
                for b in range(2):
                    act.wait_ge(e_up, i * 8 + (4 * e2 + b + 1))
                    if not (isinstance(i, int) and e2 == 0):
                        act.wait_ge(e_act, i * 4 + (2 * e2 + b - 1))
                    act.activation(uT[:, 2 * b:2 * b + 2, :], sp_[:, b, :].rearrange("p (c n) -> p c n", c=2),
                                   ACT.Silu).then_inc(e_sig, 1)

            def move_pair(p):
                act.wait_ge(gath_done, p + 1)
                act.activation(xe, op[:, :, :].rearrange("p b (k n) -> p (b k) n", n=P), ACT.Copy).then_inc(xe_moved, 1)

            def silu(e2, p):
                act.wait_ge(up_done, p * 2 + (e2 + 1))
                act.activation(hidu[:, e2, :], gp[:, e2, 0:4 * CAP], ACT.Silu).then_inc(up_silu, 1)

            def move_sel(p):
                for t in range(T):
                    act.wait_ge(selt_done, p * 2 + (t + 1))
                    act.activation(selT[:, t, :], tp[:, t, 0:P], ACT.Copy).then_inc(selt_moved, 1)

            def move_down(p):
                act.wait_ge(down_done, p * 2 + 2)
                act.activation(eout, sp_[:, :, :].rearrange("p b n -> p (b n)"), ACT.Copy).then_inc(down_moved, 1)

            act.wait_ge(flag_ready, 1)
            move_pair(0)
            silu(0, 0)
            move_sel(0)
            silu(1, 0)
            move_pair(1)
            move_down(0)
            with act.Fori(1, N_EXP // 2 - 1) as p:
                silu(0, p)
                move_sel(p)
                silu(1, p)
                move_pair(p + 1)
                move_down(p)
            last = N_EXP // 2 - 1
            silu(0, last)
            move_sel(last)
            silu(1, last)
            move_down(last)
            with act.If(act.value_load(flag[0:1, 0:1], min_val=0, max_val=2 * S) > 0):
                expert(0, 0)
                expert(1, 0)
                with act.Fori(1, N_EXP // 2) as i:
                    expert(0, i)
                    expert(1, i)

        @block.vector
        def _(v):
            own = [0]

            def link(ins):
                own[0] += 1
                ins.then_inc(dve, 1)
                v.wait_ge(dve, own[0])

            def norm(n, src, sc=None, sh=None):
                dst = h if NORMS[n] != "mem" else y
                for t in range(T):
                    link(v.tensor_tensor_reduce(h[:, t, :], src[:, t, :], src[:, t, :], 1.0, 0.0, ALU.mult, ALU.add,
                                                small[:, 60 + t:61 + t]))
                v.tensor_scalar(small[:, 60:62], small[:, 60:62], 1.0 / D, EPS, ALU.mult, ALU.add).then_inc(sumsq, 1)
                v.wait_ge(rootd, n + 1)
                link(v.reciprocal(small[:, 58:60], small[:, 62:64]))
                v.wait_ge(gvec_in, 16 * (n + 1))
                for t in range(T):
                    ins = v.scalar_tensor_tensor(out=dst[:, t, :], in0=src[:, t, :], scalar=small[:, 58 + t:59 + t],
                                                 in1=gvec[:], op0=ALU.mult, op1=ALU.mult)
                    ins.then_inc(gvec_used, 1)
                    if sc is None:
                        v.wait_ge(gvec_used, T * n + t + 1)
                        v.sem_inc(h_ready, 1)
                        continue
                    v.wait_ge(gvec_used, T * n + t + 1)
                    link(v.scalar_tensor_tensor(out=h[:, t, :], in0=sc, scalar=1.0, in1=h[:, t, :], op0=ALU.add, op1=ALU.mult))
                    v.tensor_tensor(h[:, t, :], h[:, t, :], sh, ALU.add).then_inc(h_ready, 1)

            def modrow(i):
                return mod[:, i * D:(i + 1) * D]

            def head_norms(stage_name):
                q = QK[stage_name]
                n0 = qk_base[stage_name]
                for i, (c, g) in enumerate(q):
                    w = work[:, (i % 2) * 512:(i % 2) * 512 + 512]
                    v.wait_ge(qk_root, n0 + i + 1)
                    link(v.reciprocal(w, w))
                    v.scalar_tensor_tensor(out=zt2(c), in0=zt2(c), scalar=gains[:, g:g + 1], in1=w,
                                           op0=ALU.mult, op1=ALU.mult).then_inc(qk_done, 1)

            def attention(stage_name):
                units, segs = att[stage_name]
                b0 = seg_base[stage_name]
                u0 = unit_base[stage_name]
                for j in range(len(segs) + LAG + 2):
                    if j < len(segs):
                        sg = segs[j]
                        nk = sg["nk"]
                        dst = segbuf[:, j % SEGS, 0:nk]
                        sc = sp_[:, j % 2, 0:nk]
                        v.wait_ge(s_done, b0 + j + 1)
                        if j >= SEGS:
                            v.wait_ge(t_done, b0 + j - SEGS + 1)
                        if sg["bias"][0] == "alibi":
                            ins = v.scalar_tensor_tensor(out=dst, in0=sg["bias"][1], scalar=sg["bias"][2], in1=sc,
                                                         op0=ALU.mult, op1=ALU.add)
                        elif sg["bias"][0] == "add":
                            ins = v.tensor_tensor(dst, sg["bias"][1], sc, ALU.add)
                        else:
                            ins = v.tensor_copy(dst, sc)
                        ins.then_inc(s_read, 1)
                        if sg["last"]:
                            u = sg["u"]
                            n = units[u]["n"]
                            r = (j - n + 1) % SEGS
                            v.wait_ge(s_read, b0 + j + 1)
                            v.tensor_reduce(nmax[:, u % 8:u % 8 + 1], work[:, r * S:r * S + (n - 1) * S + nk], AX.X, ALU.max,
                                            negate=True).then_inc(m_done, 1)
                    i = j - LAG - 2
                    if i >= 0 and segs[i]["last"]:
                        u = segs[i]["u"]
                        un = units[u]
                        dv = segs[i]["dv"]
                        o = op[:, u % 2, 0:dv]
                        dst = y[:, un["t"], un["out"]:un["out"] + dv]
                        d = den[:, u % 8:u % 8 + 1]
                        link(v.reciprocal(small[:, 48:49], d))
                        v.wait_ge(o_done, b0 + i + 1)
                        if un["tag"] == 1:
                            link(v.tensor_tensor(small[:, 49:50], small[:, 48:49], small[:, 44:45], ALU.mult))
                            v.scalar_tensor_tensor(out=dst, in0=o, scalar=small[:, 49:50], in1=dst, op0=ALU.mult,
                                                   op1=ALU.add).then_inc(o_read, 1)
                        else:
                            v.tensor_scalar(dst, o, small[:, 48:49], None, ALU.mult).then_inc(o_read, 1)
                        v.wait_ge(o_read, u0 + u + 1)

            def mlstm():
                v.wait_ge(mem_in, 16)
                link(v.memset(ONE_, 1.0))
                v.wait_ge(gates_f, 1)
                v.scalar_tensor_tensor(out=A_, in0=F_, scalar=-1.0, in1=F_, op0=ALU.mult, op1=ALU.max).then_inc(gates_e, 1)
                v.wait_ge(gates_l, 1)
                link(v.scalar_tensor_tensor(out=A_, in0=F_, scalar=0.0, in1=E_, op0=ALU.min, op1=ALU.subtract))
                link(v.tensor_tensor_scan(B_, ONE_, A_, 0.0, ALU.mult, ALU.add))
                link(v.tensor_tensor(G_, I_, B_, ALU.subtract))
                link(v.tensor_tensor_scan(NM_, ONE_, G_, 0.0, ALU.mult, ALU.max))
                v.tensor_tensor(EM_, B_, NM_, ALU.add).then_inc(gates_e, 1)
                link(v.tensor_scalar(NM_, NM_, -1.0, None, ALU.mult))
                v.wait_ge(em_ready, 1)
                v.sem_inc(gates_g, 1)
                for c in range(8):
                    acc = work[:, (c % SEGS) * S:(c % SEGS + 1) * S]
                    if c >= SEGS:
                        v.wait_ge(silu_done, c - SEGS + 1)
                    link(v.tensor_scalar(acc, zt(c), convw[:, c, 3:4], None, ALU.mult))
                    for tap in (2, 1, 0):
                        s = 3 - tap
                        ins = v.scalar_tensor_tensor(out=acc[:, s:S], in0=zt(c)[:, 0:S - s], scalar=convw[:, c, tap:tap + 1],
                                                     in1=acc[:, s:S], op0=ALU.mult, op1=ALU.add)
                        if tap:
                            link(ins)
                    ins.then_inc(conv_done, 1)
                v.wait_ge(gates_c, 1)
                for hh in range(M_HEADS):
                    arg = ml_arg[:, hh % 2, :]
                    pt = ml_p[:, hh % 2, :]
                    v.wait_ge(mm_b, hh + 1)
                    v.tensor_tensor(arg[:, 0:S], maskT, tp[:, hh % 2, 0:S], ALU.add)
                    v.tensor_tensor(arg[:, S:S + P], maskT[:, 0:P], tp[:, hh % 2, P:S], ALU.add).then_inc(mm_arg, 1)
                    v.wait_ge(mm_exp, hh + 1)
                    v.wait_ge(mm_s, hh + 1)
                    if hh >= 2:
                        v.wait_ge(mm_o, hh - 1)
                    v.scalar_tensor_tensor(out=pt, in0=sp_[:, hh % 2, 0:384], scalar=M_DH ** -0.5, in1=arg,
                                           op0=ALU.mult, op1=ALU.mult).then_inc(mm_p, 1)
                    v.wait_ge(mm_o, hh + 1)
                    o = op[:, hh % 2, :]
                    d = small[:, 50:52]
                    link(v.tensor_scalar(small[:, 52:54], o[:, S:S + 2], -1.0, None, ALU.mult))
                    link(v.tensor_tensor(d, small[:, 52:54], o[:, S:S + 2], ALU.max))
                    link(v.tensor_tensor(d, d, ml_cols[:, 1, :, hh], ALU.max))
                    link(v.reciprocal(d, d))
                    for t in range(T):
                        ins = v.tensor_scalar(y[:, t, P * hh:P * (hh + 1)], o[:, t * P:(t + 1) * P], d[:, t:t + 1], None, ALU.mult)
                        link(ins)
                    v.sem_inc(mm_read, 1)
                yh = y[:, :, 0:512].rearrange("p t (h n) -> p t h n", h=M_HEADS)
                sq = h[:, :, 0:512].rearrange("p t (h n) -> p t h n", h=M_HEADS)
                rms_heads(yh, sq, 24, 32, M_HEADS, M_DH, 1)
                r = small[:, 32:40].rearrange("p (t h) -> p t h", t=T)
                v.wait_ge(sig_done, 1)
                for t in range(T):
                    link(v.tensor_tensor(yh[:, t], yh[:, t], r[:, t, :].unsqueeze(2).to_broadcast([P, M_HEADS, M_DH]), ALU.mult))
                    link(v.tensor_tensor(y[:, t, 0:512], y[:, t, 0:512], mnorm, ALU.mult))
                    link(v.tensor_tensor(y[:, t, 0:512], y[:, t, 0:512], mo_sig[:, t, :], ALU.mult))

            def rms_heads(yh, sq, c0, c1, nh, dh, n):
                for t in range(T):
                    link(v.tensor_tensor(sq[:, t], yh[:, t], yh[:, t], ALU.mult))
                    link(v.tensor_reduce(small[:, c0 + t * nh:c0 + (t + 1) * nh], sq[:, t], AX.X, ALU.add))
                v.tensor_scalar(small[:, c0:c0 + T * nh], small[:, c0:c0 + T * nh], 1.0 / dh, EPS, ALU.mult, ALU.add).then_inc(hn_sq, 1)
                v.wait_ge(hn_rt, n)
                link(v.reciprocal(small[:, c1:c1 + T * nh], small[:, c1:c1 + T * nh]))

            def residual(g, name, n):
                v.wait_ge(gemm_moved, last_group[name])
                for t in range(T):
                    if g is None:
                        v.tensor_tensor(x[:, t, :], x[:, t, :], y[:, t, :], ALU.add).then_inc(x_ready, 1)
                        continue
                    link(v.tensor_tensor(y[:, t, :], y[:, t, :], g, ALU.mult))
                    v.tensor_tensor(x[:, t, :], x[:, t, :], y[:, t, :], ALU.add).then_inc(x_ready, 1)
                v.wait_ge(x_ready, n)

            def topk(l, t):
                v.wait_ge(sub_moved, 4 * (2 * l + t + 1))
                for c in range(2 * PEER_H):
                    s = sub[:, c, :]
                    link(v.max(top[:, c, 0:8], s))
                    link(v.max_index(topi[:, c, 0:8], top[:, c, 0:8], s))
                    link(v.match_replace(s, top[:, c, 0:8], s, -3e38))
                    link(v.max(top[:, c, 8:16], s))
                    link(v.max_index(topi[:, c, 8:16], top[:, c, 8:16], s))
                v.sem_inc(sub_free, 1)
                link(v.tensor_copy(topf, topi))
                for hh in range(PEER_H):
                    link(v.tensor_tensor(cand[:, hh, :].rearrange("p (i j) -> p i j", i=TOPK),
                                         top[:, 2 * hh, :].unsqueeze(2).to_broadcast([P, TOPK, TOPK]),
                                         top[:, 2 * hh + 1, :].unsqueeze(1).to_broadcast([P, TOPK, TOPK]), ALU.add))
                    s = cand[:, hh, :]
                    link(v.max(score[:, hh, 0:8], s))
                    link(v.max_index(pos[:, hh, 0:8], score[:, hh, 0:8], s))
                    link(v.match_replace(s, score[:, hh, 0:8], s, -3e38))
                    link(v.max(score[:, hh, 8:16], s))
                    link(v.max_index(pos[:, hh, 8:16], score[:, hh, 8:16], s))
                gt = gate[:, t, :].rearrange("p (h k) -> p h k", h=PEER_H)
                v.tensor_tensor(gt, score, score[:, :, 0:1].to_broadcast([P, PEER_H, TOPK]), ALU.subtract).then_inc(top_ready, 1)
                posf = pos.rearrange("p h k -> p (h k)")
                hi = cand[:, 0, 0:SLOTS].bitcast(U32)
                lo = cand[:, 1, 0:SLOTS].bitcast(U32)
                link(v.tensor_scalar(hi, posf, 4, None, ALU.logical_shift_right))
                link(v.tensor_scalar(lo, posf, 15, None, ALU.bitwise_and))
                num = []
                for c, part in enumerate((hi, lo)):
                    pf = cand[:, 2 + c, 0:SLOTS]
                    link(v.tensor_copy(pf, part))
                    link(v.tensor_tensor(hot, pf.unsqueeze(2).to_broadcast([P, SLOTS, TOPK]),
                                         iota.unsqueeze(1).to_broadcast([P, SLOTS, TOPK]), ALU.is_equal))
                    for hh in range(PEER_H):
                        link(v.tensor_tensor(hot[:, TOPK * hh:TOPK * (hh + 1), :], hot[:, TOPK * hh:TOPK * (hh + 1), :],
                                             topf[:, 2 * hh + c, :].unsqueeze(1).to_broadcast([P, TOPK, TOPK]), ALU.mult))
                    nf = cand[:, 4 + c, 0:SLOTS]
                    link(v.tensor_reduce(nf, hot, AX.X, ALU.add))
                    num.append(nf)
                link(v.tensor_scalar(num[0], num[0], float(NKEYS), float(l * PEER_N), ALU.mult, ALU.add))
                link(v.tensor_tensor(num[0], num[0], num[1], ALU.add))
                v.tensor_copy(idx[:, t, :], num[0]).then_inc(idx_ready, 1)
                v.wait_ge(idx_ready, 2 * l + t + 1)

            def gates_norm(l, t):
                gt = gate[:, t, :].rearrange("p (h k) -> p h k", h=PEER_H)
                v.wait_ge(gate_e, 2 * l + t + 1)
                link(v.tensor_reduce(small[:, 0:8], gt, AX.X, ALU.add))
                link(v.reciprocal(small[:, 8:16], small[:, 0:8]))
                link(v.tensor_tensor(gt, gt, small[:, 8:16].unsqueeze(2).to_broadcast([P, PEER_H, TOPK]), ALU.mult))

            def peer_dots(l, t):
                n = 2 * l + t
                phase = 4 * l + 2 * t
                base = n * SLOTS
                with v.Fori(0, GROUPS) as i:
                    for k in range(ROWS):
                        v.wait_ge(row_in[k], i * 16 + 16 * (phase * GROUPS + 1))
                        v.tensor_tensor_reduce(y[:, 0, :], rowbuf[:, k, :], h[:, t, :], 1.0, 0.0, ALU.mult, ALU.add,
                                               dots8[:, k:k + 1]).then_inc(udot, 1)
                        v.wait_ge(udot, i * ROWS + (base + k + 1))
                    v.tensor_copy(dots[:, bass.ds(i * ROWS, ROWS)], dots8[:]).then_inc(hn_dots, 1)
                    v.wait_ge(hn_dots, i + (n * GROUPS + 1))
                v.sem_inc(dots_all, 1)
                v.wait_ge(gelu_done, n + 1)
                v.tensor_tensor(coef[:], coef[:], gate[:, t, :], ALU.mult).then_inc(coef_ready, 1)

            def peer_residual(l, t):
                v.wait_ge(vsum, (2 * l + t + 1) * SLOTS)
                for n in range(2):
                    link(v.tensor_tensor(y[:, 1, n * 512:(n + 1) * 512], g2[:, l, n * 512:(n + 1) * 512], op[:, n, :], ALU.mult))
                v.tensor_tensor(x[:, t, :], x[:, t, :], y[:, 1, :], ALU.add).then_inc(x_ready, 1)
                v.wait_ge(x_ready, T * (2 * l + 1) + t + 1)

            v.memset(eps[:], EPS)
            v.wait_ge(loaded, 16 * NLOADS)
            link(v.memset(ones1[:], 1.0))
            for g in (G_EVQ, G_ODQ, G_NAQ, G_DLQ, G_MMQ):
                link(v.tensor_scalar(gains[:, g:g + 1], gains[:, g:g + 1], 0.125, None, ALU.mult))
            v.wait_ge(t5_in, 16 * (NA_HEADS + 3))
            v.wait_ge(t5_mm, 1)
            for g in range(DIL_GROUPS):
                ins = v.tensor_tensor(t5_out[:, g * TW:(g + 1) * TW], t5_mask[:, g * TW:(g + 1) * TW],
                                      (sp_ if g < 2 else op)[0:DIL_HPG, g % 2, 0:TW], ALU.add)
                link(ins)
            v.sem_inc(t5_sum, 1)

            v.wait_ge(gemm_moved, last_group["ada0"])
            norm(0, x, modrow(1), modrow(0))
            v.wait_ge(gemm_moved, last_group["in0"])
            mlstm()
            head_norms("moba")
            attention("moba")
            v.sem_inc(y_ready, 1)
            residual(modrow(2), "out0", T)
            for l in range(2):
                norm(2 * l + 1, x, modrow(4), modrow(3))
                v.wait_ge(keys_m, l + 1)
                topk(l, 0)
                gates_norm(l, 0)
                peer_dots(l, 0)
                topk(l, 1)
                gates_norm(l, 1)
                peer_residual(l, 0)
                peer_dots(l, 1)
                peer_residual(l, 1)
                if l == 0:
                    v.wait_ge(gemm_moved, last_group["ada1"])
                    norm(2, x, modrow(1), modrow(0))
                    v.wait_ge(lam_in, 32)
                    for c in range(2):
                        link(v.tensor_tensor_reduce(y[:, 0, 0:64], lam_rows[:, 2 * c, :], lam_rows[:, 2 * c + 1, :], 1.0, 0.0,
                                                    ALU.mult, ALU.add, small[:, 40 + c:41 + c]))
                    v.sem_inc(lam_s, 1)
                    v.wait_ge(lam_e, 1)
                    link(v.tensor_tensor(small[:, 44:45], small[:, 43:44], small[:, 42:43], ALU.subtract))
                    link(v.tensor_scalar(small[:, 44:45], small[:, 44:45], -LAM_INIT, None, ALU.add))
                    v.wait_ge(gemm_moved, last_group["in1"])
                    head_norms("diff")
                    attention("diff")
                    yh = y[:, :, :].rearrange("p t (h n) -> p t h n", h=C_HEADS)
                    sq = h[:, :, :].rearrange("p t (h n) -> p t h n", h=C_HEADS)
                    rms_heads(yh, sq, 0, 0, C_HEADS, P, 2)
                    r = small[:, 0:16].rearrange("p (t h) -> p t h", t=T)
                    for t in range(T):
                        link(v.tensor_tensor(yh[:, t], yh[:, t], r[:, t, :].unsqueeze(2).to_broadcast([P, C_HEADS, P]), ALU.mult))
                        link(v.tensor_tensor(yh[:, t], yh[:, t], onorm.unsqueeze(1).to_broadcast([P, C_HEADS, P]), ALU.mult))
                        link(v.tensor_scalar(y[:, t, :], y[:, t, :], 1.0 - LAM_INIT, None, ALU.mult))
                    v.sem_inc(y_ready, 1)
                    residual(modrow(2), "out1", T * 3)
            v.wait_ge(mem_in, 32)
            norm(4, y)
            norm(5, x)
            v.wait_ge(bias_in, 16 * 17)
            for hh in range(NA_HEADS):
                nb = na_bias[:, hh, :].rearrange("p (j n) -> p j n", j=6)
                ins = v.tensor_tensor(nb, nb, na_mask.unsqueeze(1).to_broadcast([P, 6, GRID_W]), ALU.add)
            link(ins)
            v.wait_ge(gemm_moved, last_group["in2"])
            head_norms("block2")
            attention("block2")
            v.sem_inc(y_ready, 1)
            residual(None, "out2", T * 5)
            norm(6, x)

            v.wait_ge(r_mm, 1)
            v.wait_ge(r_in, 32)
            gl8 = route[:, 0:16].rearrange("p (t n) -> p t n", t=T)
            fine = route[:, 16:80].rearrange("p (t n) -> p t n", t=T)
            gm = route[:, 80:96].rearrange("p (t n) -> p t n", t=T)
            fsel = route[:, 96:112].rearrange("p (t n) -> p t n", t=T)
            fm = route[:, 112:128].rearrange("p (t n) -> p t n", t=T)
            ge = route[:, 128:136].rearrange("p (t n) -> p t n", t=T)
            p1 = route[:, 136:138]
            gsum = route[:, 138:140]
            oh = route[:, 140:148].rearrange("p (t n) -> p t n", t=T)
            fi = route[:, 148:152].rearrange("p (t n) -> p t n", t=T)
            tmp = route[:, 152:216].rearrange("p (t g n) -> p t g n", t=T, g=N_GRP)
            w8 = route[:, 216:232].rearrange("p (t n) -> p t n", t=T)
            gg = route[:, 232:236].rearrange("p (t n) -> p t n", t=T)
            gi = route[:, 236:238]
            link(v.memset(route[:, 0:16], NEG))
            for t in range(T):
                link(v.tensor_tensor(gl8[:, t, 0:4], rbias[:, 0:4], op[:, t, 0:4], ALU.add))
                link(v.tensor_tensor(fine[:, t, :], rbias[:, 4:36], op[:, t, 4:36], ALU.add))
                link(v.max(gm[:, t, :], gl8[:, t, :]))
                link(v.max_index(route_u[:, 0:8], gm[:, t, :], gl8[:, t, :]))
                link(v.tensor_copy(gi[:, t:t + 1], route_u[:, 0:1]))
                link(v.tensor_scalar(ge[:, t, :], gl8[:, t, 0:4], gm[:, t, 0:1], None, ALU.subtract))
                link(v.tensor_scalar(oh[:, t, :], iota[:, 0:4], gi[:, t:t + 1], None, ALU.is_equal))
                link(v.tensor_tensor(tmp[:, t], fine[:, t, :].rearrange("p (g n) -> p g n", g=N_GRP),
                                     oh[:, t, :].unsqueeze(2).to_broadcast([P, N_GRP, PER_GRP]), ALU.mult))
                link(v.tensor_reduce(fsel[:, t, :], tmp[:, t].rearrange("p g n -> p n g"), AX.X, ALU.add))
                link(v.max(fm[:, t, :], fsel[:, t, :]))
                link(v.max_index(route_u[:, 8:16], fm[:, t, :], fsel[:, t, :]))
                link(v.tensor_copy(fi[:, t, :], route_u[:, 8:10]))
                link(v.tensor_tensor(p1[:, t:t + 1], fm[:, t, 1:2], fm[:, t, 0:1], ALU.subtract))
            v.sem_inc(r_pre, 2)
            v.wait_ge(r_exp, 2)
            link(v.tensor_reduce(gsum, ge, AX.X, ALU.add))
            for t in range(T):
                link(v.tensor_scalar(gg[:, t, 0:1], p1[:, t:t + 1], 1.0, gsum[:, t:t + 1], ALU.add, ALU.mult))
                link(v.reciprocal(gg[:, t, 0:1], gg[:, t, 0:1]))
                link(v.tensor_tensor(gg[:, t, 1:2], gg[:, t, 0:1], p1[:, t:t + 1], ALU.mult))
                link(v.tensor_scalar(w8[:, t, :], iota[:, 0:8], fi[:, t, 0:1], gg[:, t, 0:1], ALU.is_equal, ALU.mult))
                link(v.tensor_scalar(fm[:, t, :], iota[:, 0:8], fi[:, t, 1:2], gg[:, t, 1:2], ALU.is_equal, ALU.mult))
                link(v.tensor_tensor(w8[:, t, :], w8[:, t, :], fm[:, t, :], ALU.add))
                link(v.tensor_scalar(fsel[:, t, :], iota[:, 0:8], fi[:, t, 0:1], None, ALU.is_equal))
                link(v.tensor_scalar(fm[:, t, :], iota[:, 0:8], fi[:, t, 1:2], None, ALU.is_equal))
                link(v.tensor_tensor(fm[:, t, :], fsel[:, t, :], fm[:, t, :], ALU.add))
                link(v.tensor_tensor(picked[:, t, :].rearrange("p (g n) -> p g n", g=N_GRP),
                                     oh[:, t, :].unsqueeze(2).to_broadcast([P, N_GRP, PER_GRP]),
                                     fm[:, t, :].unsqueeze(1).to_broadcast([P, N_GRP, PER_GRP]), ALU.mult))
                link(v.tensor_tensor(w_gate[:, t, :].rearrange("p (g n) -> p g n", g=N_GRP),
                                     oh[:, t, :].unsqueeze(2).to_broadcast([P, N_GRP, PER_GRP]),
                                     w8[:, t, :].unsqueeze(1).to_broadcast([P, N_GRP, PER_GRP]), ALU.mult))
            link(v.memset(gvec[:, 0:2 * P], 1.0))
            link(v.memset(earlier[:, 0:1], 0.0))
            link(v.tensor_scalar(earlier[:, 1:P], maskT[:, 0:P - 1], 0.0, None, ALU.is_equal))
            v.sem_inc(r_done, 1)
            v.wait_ge(rank_done, 1)
            flat = [q.rearrange("p t n -> p (t n)") for q in (rank, below, picked, w_gate, w_over)]
            link(v.tensor_copy(flat[0], tp[:, 0, 0:2 * N_EXP]))
            link(v.tensor_scalar(flat[1], flat[0], float(FULL), None, ALU.is_lt))
            link(v.tensor_tensor(flat[4], flat[3], flat[1], ALU.mult))
            link(v.tensor_tensor(route[:, 0:64], flat[2], flat[1], ALU.mult))
            link(v.tensor_tensor(route[:, 64:128], flat[2], route[:, 0:64], ALU.subtract))
            v.tensor_reduce(over[:, 0:1], route[:, 64:128], AX.X, ALU.add).then_inc(over_ready, 1)
            v.wait_ge(over_sum, 1)
            link(v.tensor_copy(flag, tp[:, 1, 0:1]))
            link(v.tensor_tensor(route[:, 128:192], flat[3], flat[4], ALU.subtract))
            link(v.tensor_copy(flat[3], flat[4]))
            link(v.tensor_copy(flat[4], route[:, 128:192]))
            link(v.tensor_copy(flat[2], route[:, 0:64]))
            v.sem_inc(flag_ready, 1)

            def select(p):
                for e2 in range(2):
                    for t in range(T):
                        def at(q):
                            return q[:, t, p * 2 + e2:p * 2 + e2 + 1] if isinstance(p, int) else q[:, t, bass.ds(p * 2 + e2, 1)]
                        c = slice(e2 * CAP, (e2 + 1) * CAP)
                        v.tensor_scalar(sel[:, t, c], iota64, at(rank), at(picked), ALU.is_equal, ALU.mult)
                        ins = v.tensor_scalar(selg[:, t, c], iota64, at(rank), at(w_gate), ALU.is_equal, ALU.mult)
                ins.then_inc(sel_ready, 1)

            def take_up(e2, p):
                v.wait_ge(up_silu, p * 2 + (e2 + 1))
                v.tensor_tensor(hid[:, e2].rearrange("p f n -> p (f n)"), hidu[:, e2, :], gp[:, e2, 4 * CAP:8 * CAP],
                                ALU.mult).then_inc(up_act, 1)

            def add_pair(p):
                for n in range(4):
                    v.wait_ge(scat_done, p * 4 + (n + 1))
                    acc = x[:, n // 2, (n % 2) * 512:(n % 2 + 1) * 512]
                    v.tensor_tensor(acc, acc, tp[:, n % 2, :], ALU.add).then_inc(scat_read, 1)

            def next_select(p):
                v.wait_ge(gath_done, p)
                v.wait_ge(selt_done, p * 2)
                select(p)

            select(0)
            take_up(0, 0)
            next_select(1)
            take_up(1, 0)
            with v.Fori(1, N_EXP // 2 - 1) as p:
                take_up(0, p)
                add_pair(p - 1)
                next_select(p + 1)
                take_up(1, p)
            last = N_EXP // 2 - 1
            take_up(0, last)
            add_pair(last - 1)
            take_up(1, last)
            add_pair(last)

            def expert(e2, i):
                for b in range(2):
                    v.wait_ge(e_sig, i * 4 + (2 * e2 + b + 1))
                    v.wait_ge(e_up, i * 8 + (4 * e2 + 2 + b + 1))
                    if not (isinstance(i, int) and e2 == 0) and b == 0:
                        v.wait_ge(e_down, i * 8 + 4 * e2)
                    v.tensor_tensor(aT[:, 2 * b:2 * b + 2, :], uT[:, 2 * b:2 * b + 2, :],
                                    gp[:, b, :].rearrange("p (c n) -> p c n", c=2), ALU.mult).then_inc(e_act, 1)
                for t in range(T):
                    if isinstance(i, int):
                        col = w_over[:, t, e2:e2 + 1]
                    else:
                        col = w_over[:, t, bass.ds(i * 2 + e2, 1)]
                    for n in range(2):
                        v.wait_ge(e_down, i * 8 + (4 * e2 + 2 * t + n + 1))
                        bank = (tp if t == 0 else op)[:, n, :]
                        acc = x[:, t, n * 512:(n + 1) * 512]
                        v.scalar_tensor_tensor(out=acc, in0=bank, scalar=col, in1=acc, op0=ALU.mult, op1=ALU.add).then_inc(e_acc, 1)

            v.wait_ge(scat_read, 2 * N_EXP)
            with v.If(v.value_load(flag[0:1, 0:1], min_val=0, max_val=2 * S) > 0):
                expert(0, 0)
                v.wait_ge(e_acc, 4)
                expert(1, 0)
                with v.Fori(1, N_EXP // 2) as i:
                    v.wait_ge(e_acc, i * 8)
                    expert(0, i)
                    v.wait_ge(e_acc, i * 8 + 4)
                    expert(1, i)
                v.wait_ge(e_acc, 4 * N_EXP)
            v.sem_inc(x_ready, T)


_INS = ["x", "c", "ada_w", "ada_b", "norm_mix_g", "norm_ffn_g", "ev_w_in", "ev_igate_b", "ev_fgate_b", "ev_mnorm_g",
        "ev_w_out", "od_w_in", "od_lam", "od_onorm_g", "od_w_out", "peer_wq", "peer_keys", "peer_u", "peer_v", "mem_2",
        "g_mix_2", "w_in_2", "na_rpb_2", "t5_table_2", "g_mem_2", "w_mem_kv_2", "w_out_2", "g_ffn_2", "w_r1_2", "b_r1_2",
        "w_r2_2", "b_r2_2", "w1_2", "w3_2", "w2_2"]


def kernel(**inputs):
    import numpy as _np
    import concourse.bacc as _bacc
    from concourse import mybir as _mybir
    from concourse.bass_utils import run_bass_kernel_spmd as _run

    nc = _bacc.Bacc("TRN2", target_bir_lowering=False, num_devices=1)
    arrays, args = {}, {}

    def give(name, a):
        a = _np.ascontiguousarray(a)
        arrays[f"in_{name}_dram"] = a
        args[name] = nc.dram_tensor(f"in_{name}_dram", a.shape, _mybir.dt.from_np(a.dtype), kind="ExternalInput").ap()

    for name in _INS:
        give(name, inputs[name])
    cst, hot, dmask = shape_constants()
    give("cst", cst)
    give("t5_hot", hot)
    give("t5_mask", dmask)
    qk = _np.asarray(inputs["qk_gain_2"])[0].reshape(6, 64)
    cols = [_np.asarray(inputs[k])[0] for k in ("ev_qn_g", "ev_kn_g", "od_qn_g", "od_kn_g")] + list(qk)
    col = _np.stack(cols, axis=1)
    give("gains", _np.concatenate([col, col], axis=0))
    give("conv_cols", _np.asarray(inputs["ev_conv_w"])[0].reshape(4, 8, 128).transpose(2, 1, 0))
    out = nc.dram_tensor("out_0_dram", (1, S, D), _mybir.dt.float32, kind="ExternalOutput").ap()
    program(nc, args, out)
    r = _run(nc, [arrays], core_ids=[0])
    return r.results[0]["out_0_dram"]
```

```python
import math
from contextlib import ExitStack

import numpy as np

import concourse.bass as bass
from concourse import mybir

F32 = mybir.dt.float32
U32 = mybir.dt.uint32
ALU = mybir.AluOpType
ACT = mybir.ActivationFunctionType
AX = mybir.AxisListType

P = 128
D = 1024
S = 256
T = S // P
KT = D // P
EPS = 1e-6
NEG = -1e30
RING = 4
CH = 512

M_HEADS, M_DH = 4, 128
B_HEADS, C_HEADS, NA_HEADS, MEM_HEADS = 8, 8, 8, 4
DIL_GROUPS, DIL_HPG = 3, 4
DIL_PAIRS = ((128, 1), (512, 4), (2048, 16))
GRID_W, NA_KR, NA_KC = 64, 15, 31
T5_BUCKETS, T5_MAX_DIST = 32, 1024
LAM_INIT = 0.8 - 0.6 * math.exp(-0.3)
PEER_H, NKEYS, TOPK = 8, 128, 16
PEER_N = NKEYS * NKEYS
SLOTS = PEER_H * TOPK
ROWS = 8
GROUPS = SLOTS // ROWS
SHARED = (GROUPS // 3, 1)
PE_ROWS, DVE_ROWS = (0, 1, 2, 4, 5, 6), (3, 7)
N_EXP, N_GRP, PER_GRP = 32, 4, 8
MOE_RING = 6
CAP = 64
FULL = CAP

C_ID, C_DIST, C_MASKT, C_NAM, C_BLK, C_IOTA = 0, 128, 512, 768, 832, 960
C_N = 1024
G_EVQ, G_EVK, G_ODQ, G_ODK, G_NAQ, G_NAK, G_DLQ, G_DLK, G_MMQ, G_MMK = range(10)
TW = 2 * S - 1
RW = 2 * GRID_W - 1
NDR = 7


def pe_rows_before(n):
    return sum(ROWS * SHARED[m % 2] + len(PE_ROWS) * (GROUPS - SHARED[m % 2]) for m in range(n))


def dve_rows_before(n):
    return sum(len(DVE_ROWS) * (GROUPS - SHARED[m % 2]) for m in range(n))


def slope(h):
    return 2.0 ** (-8.0 * (h + 1) / 8)


def shape_constants():
    c = np.zeros((P, C_N), np.float32)
    p = np.arange(P)[:, None]
    c[:, C_ID:C_ID + P] = np.eye(P)
    dist = p + P - np.arange(3 * P)[None]
    c[:, C_DIST:C_DIST + 3 * P] = np.where(dist >= 0, dist, -NEG)
    c[:, C_MASKT:C_MASKT + S] = np.where(p <= np.arange(S)[None], 0, NEG)
    qc = p % GRID_W
    first = np.clip(qc - 8, 0, GRID_W - 16)
    kc = np.arange(GRID_W)[None]
    c[:, C_NAM:C_NAM + GRID_W] = np.where((kc >= first) & (kc < first + 16), 0, NEG)
    c[:, C_BLK:C_BLK + P] = (p // 64) == (np.arange(P)[None] // 64)
    c[:, C_IOTA:C_IOTA + CAP] = np.arange(CAP)[None]
    rel = np.arange(TW) - (S - 1)
    nb = T5_BUCKETS // 2
    exact = nb // 2
    n = np.abs(rel)
    nf = np.maximum(n, 1).astype(np.float32)
    large = exact + (np.log(nf / np.float32(exact)) / np.float32(math.log(T5_MAX_DIST / exact))
                     * np.float32(nb - exact)).astype(np.int32)
    bucket = (rel > 0) * nb + np.where(n < exact, n, np.minimum(large, nb - 1))
    onehot = np.zeros((T5_BUCKETS, TW), np.float32)
    onehot[bucket, np.arange(TW)] = 1
    dmask = np.zeros((DIL_HPG, DIL_GROUPS, TW), np.float32)
    for g, (win, dil) in enumerate(DIL_PAIRS):
        dmask[:, g] = np.where((rel % dil == 0) & (n <= win // 2), 0, NEG)
    return c, onehot, dmask


def weight_stream(a):
    def view(w, c0, n=CH):
        return w[:, c0:c0 + n].rearrange("(k p) n -> p k n", p=P)

    slots = []

    def ada(l):
        for n in range(12):
            slots.append((f"ada{l}", view(a["ada_w"][l], n * CH), [("bcast", n)]))

    def rows(name, w, c0, dst):
        slots.append((name, view(w, c0), [("rows", 0, dst), ("rows", 1, dst)]))

    def cols(name, w, c0, z0):
        slots.append((name, view(w, c0), [("cols", 0, z0), ("cols", 256, z0 + 2)]))

    ada(0)
    w = a["ev_w_in"][0]
    cols("in0", w, 0, 0)
    cols("in0", w, 512, 4)
    rows("in0", w, 1024, ("zn", 0))
    rows("in0", w, 1536, ("zn", 512))
    cols("in0", w, 2056, 8)
    cols("in0", w, 2568, 12)
    rows("in0", w, 3080, ("zn", 1024))
    for n in range(2):
        rows("out0", a["ev_w_out"][0], n * CH, ("y", n * CH))
    for n in range(4):
        cols("wq0", a["peer_wq"][0], n * CH, 4 * n)
    ada(1)
    for n in range(4):
        cols("in1", a["od_w_in"][0], n * CH, 4 * n)
    for n in range(2):
        rows("in1", a["od_w_in"][0], 2048 + n * CH, ("zn", n * CH))
    for n in range(2):
        rows("out1", a["od_w_out"][0], n * CH, ("y", n * CH))
    for n in range(4):
        cols("wq1", a["peer_wq"][1], n * CH, 4 * n)
    slots.append(("mem", view(a["w_mem_kv_2"][0], 0), [("cols", 0, 22), ("rows2", 256, ("zn", 1280))]))
    w = a["w_in_2"][0]
    cols("in2", w, 0, 0)
    cols("in2", w, 512, 4)
    rows("in2", w, 1024, ("zn", 0))
    cols("in2", w, 1536, 8)
    cols("in2", w, 2048, 12)
    cols("in2", w, 2560, 16)
    rows("in2", w, 3072, ("zn", 512))
    slots.append(("in2", view(w, 3584), [("rows2", 0, ("zn", 1024)), ("cols", 256, 20)]))
    for n in range(2):
        rows("out2", a["w_out_2"][0], n * CH, ("y", n * CH))
    return slots


def attention_segments(stage, v):
    zt, zn, dist, dil_bias, na_bias = v["zt"], v["zn"], v["dist"], v["dil_bias"], v["na_bias"]
    units, segs = [], []

    def head(tile, h):
        return zt(tile + h // 2), 64 * (h % 2)

    def unit(t, out, parts, tag=None):
        u = len(units)
        units.append(dict(t=t, out=out, first=len(segs), n=len(parts), tag=tag))
        for i, (qt, kt, base, bias, nk, val, dv) in enumerate(parts):
            segs.append(dict(u=u, q=qt[base:base + 64, t * P:(t + 1) * P], k=kt[base:base + 64, 0:nk],
                             bias=bias, nk=nk, v=val, dv=dv, first=i == 0, last=i == len(parts) - 1))

    if stage == "moba":
        for h in range(B_HEADS):
            for t in range(T):
                nk = (t + 1) * P
                qt, base = head(8, h)
                kt, _ = head(12, h)
                unit(t, 512 + 64 * h, [(qt, kt, base, ("alibi", dist[:, (1 - t) * P:(1 - t) * P + nk], -slope(h)), nk,
                                        1024 + 64 * h, 64)])
    if stage == "diff":
        for h in range(C_HEADS):
            for t in range(T):
                for c in range(2):
                    nk = (t + 1) * P
                    unit(t, P * h, [(zt(h), zt(8 + h), 64 * c,
                                     ("alibi", dist[:, (1 - t) * P:(1 - t) * P + nk], -slope(h)), nk, P * h, P)], c)
    if stage == "block2":
        for h in range(NA_HEADS):
            for t in range(T):
                qt, base = head(0, h)
                kt, _ = head(4, h)
                unit(t, 64 * h, [(qt, kt, base, ("add", na_bias[:, h, (2 - 2 * t) * GRID_W:(2 - 2 * t) * GRID_W + S]),
                                  S, 64 * h, 64)])
        for h in range(MEM_HEADS):
            for t in range(T):
                qt, base = head(20, h)
                kt, _ = head(22, h)
                unit(t, 768 + 64 * h, [(qt, kt, base, ("none",), S, 1280 + 64 * h, 64)])
        for h in range(DIL_HPG):
            for t in range(T):
                parts = []
                for g in range(DIL_GROUPS):
                    i = g * DIL_HPG + h
                    qt, base = head(8, i)
                    kt, _ = head(14, i)
                    parts.append((qt, kt, base, ("add", dil_bias[:, i, (1 - t) * P:(1 - t) * P + S]), S,
                                  512 + 64 * i, 64))
                unit(t, 512 + 64 * h, parts)
    return units, segs


def program(nc, a, out):
    ctx = ExitStack()
    with ctx:
        ctx.enter_context(nc.allow_non_contiguous_dma(reason="small parameter columns"))

        def sb(name, shape, dt=F32):
            return ctx.enter_context(nc.sbuf_tensor(name, shape, dt))

        def sem(name):
            return ctx.enter_context(nc.semaphore(name))

        x = sb("x", [P, T, D])
        h = sb("h", [P, T, D])
        y = sb("y", [P, T, D])
        hT = sb("hT", [P, KT, S])
        mod = sb("mod", [P, 5 * D])
        g2 = sb("g2", [P, 2, D])
        zbuf = sb("zbuf", [P, 8192])
        ring = sb("ring", [P, RING, KT * CH])
        tk = sb("tk", [P, 6144])
        work = sb("work", [P, 2048])
        gvec = sb("gvec", [P, D])
        cst = sb("cst", [P, C_N])
        ada_b = sb("ada_b", [12, CH])
        cact = sb("cact", [P, KT])
        gains = sb("gains", [P, 10])
        convw = sb("convw", [P, 8, 4])
        gate_w = sb("gate_w", [P, KT, 8])
        gate_b = sb("gate_b", [4, 2])
        idx = sb("idx", [P, T, SLOTS], U32)
        gate = sb("gate", [P, T, SLOTS])
        dots = sb("dots", [P, SLOTS])
        coef = sb("coef", [P, SLOTS])
        dots8 = sb("dots8", [P, ROWS])
        stage = sb("stage", [P, ROWS], U32)
        small = sb("small", [P, 64])
        nmax = sb("nmax", [P, 8])
        den = sb("den", [P, 8])
        eps = sb("eps", [P, 1])
        ones1 = sb("ones1", [P, 1])
        gw36 = sb("gw36", [P, KT, 36])
        lam_rows = sb("lam_rows", [P, 4, 64])
        onorm_t = sb("onorm", [P, P])
        onorm = onorm_t[:, :]

        ident = cst[:, C_ID:C_ID + P]
        dist = cst[:, C_DIST:C_DIST + 3 * P]
        maskT = cst[:, C_MASKT:C_MASKT + S]
        na_mask = cst[:, C_NAM:C_NAM + GRID_W]
        blk = cst[:, C_BLK:C_BLK + P]
        iota64 = cst[:, C_IOTA:C_IOTA + CAP]
        iota = cst[:, C_IOTA:C_IOTA + TOPK]
        na_bias = mod[:, 2048:5120].rearrange("p (h j) -> p h j", h=NA_HEADS)
        dil_bias = tk[:, 0:12 * 384].rearrange("p (i j) -> p i j", i=12)

        def zt(c):
            b, c = (zbuf, c) if c < 16 else (mod, c - 16)
            return b[:, c * S:(c + 1) * S]

        def zt2(c):
            b, c = (zbuf, c) if c < 16 else (mod, c - 16)
            return b[:, c * S:(c + 2) * S]

        zn = zbuf[:, 4096:4096 + T * 1536].rearrange("p (t n) -> p t n", t=T)
        rowbuf = zbuf[:, :].rearrange("p (r n) -> p r n", r=ROWS)

        gp = ctx.enter_context(nc.psum_tensor("gp", [P, 2, 512], F32))
        sp_ = ctx.enter_context(nc.psum_tensor("scores", [P, 2, 512], F32))
        tp = ctx.enter_context(nc.psum_tensor("turned", [P, 2, 512], F32))
        op = ctx.enter_context(nc.psum_tensor("summed", [P, 2, 512], F32))

        t5_rows = nc.dram_tensor("t5_rows", [12, TW], F32, kind="Internal").ap()
        t5_rep = nc.dram_tensor("t5_rep", [P, 12 * TW], F32, kind="Internal").ap()
        na_rows = nc.dram_tensor("na_rows", [NA_HEADS * NDR, RW], F32, kind="Internal").ap()
        na_rep = nc.dram_tensor("na_rep", [GRID_W, NA_HEADS * NDR * RW], F32, kind="Internal").ap()

        loaded = sem("loaded")
        c_ready = sem("c_ready")
        w_landed = [sem(f"w_landed{i}") for i in range(RING)]
        ada_b_in = sem("ada_b_in")
        gemm_done = sem("gemm_done")
        gemm_moved = sem("gemm_moved")
        gvec_in = sem("gvec_in")
        gvec_used = sem("gvec_used")
        sumsq = sem("sumsq")
        rootd = sem("rootd")
        h_ready = sem("h_ready")
        turn_done = sem("turn_done")
        turn_moved = sem("turn_moved")
        qk_sq = sem("qk_sq")
        qk_sum = sem("qk_sum")
        qk_root = sem("qk_root")
        qk_inv = sem("qk_inv")
        qk_spread = sem("qk_spread")
        qk_done = sem("qk_done")
        s_done = sem("s_done")
        s_read = sem("s_read")
        m_done = sem("m_done")
        e_done = sem("e_done")
        t_done = sem("t_done")
        t_moved = sem("t_moved")
        o_done = sem("o_done")
        o_read = sem("o_read")
        y_ready = sem("y_ready")
        x_ready = sem("x_ready")
        dve = sem("dve")
        act_own = sem("act_own")
        pool_own = sem("pool_own")
        conv_done = sem("conv_done")
        silu_done = sem("silu_done")
        gates_mm = sem("gates_mm")
        gates_f = sem("gates_f")
        gates_e = sem("gates_e")
        gates_l = sem("gates_l")
        gates_g = sem("gates_g")
        gates_t = sem("gates_t")
        gates_c = sem("gates_c")
        mm_s = sem("ml_scores")
        mm_b = sem("ml_bcast")
        mm_arg = sem("ml_arg")
        mm_exp = sem("ml_exp")
        mm_p = sem("ml_p")
        mm_o = sem("ml_o")
        mm_read = sem("ml_read")
        em_ready = sem("em_ready")
        sig_done = sem("sig_done")
        hn_sq = sem("hn_sq")
        hn_rt = sem("hn_rt")
        keys_in = sem("keys_in")
        keys_t = sem("keys_t")
        keys_m = sem("keys_m")
        sub_done = sem("sub_done")
        sub_moved = sem("sub_moved")
        sub_free = sem("sub_free")
        top_ready = sem("top_ready")
        gate_e = sem("gate_e")
        idx_ready = sem("idx_ready")
        row_in = [sem(f"row_in{k}") for k in range(ROWS)]
        row_free = sem("row_free")
        idx_staged = sem("idx_staged")
        udot = sem("udot")
        dots_all = sem("dots_all")
        gelu_done = sem("gelu_done")
        coef_ready = sem("coef_ready")
        diag_ready = sem("diag_ready")
        diag_free = sem("diag_free")
        vsum = sem("vsum")
        vshare = sem("vshare")
        lam_s = sem("lam_s")
        lam_e = sem("lam_e")
        lam_in = sem("lam_in")
        hn_dots = sem("dots_kept")
        t5_in = sem("t5_in")
        t5_mm = sem("t5_mm")
        t5_sum = sem("t5_sum")
        t5_w = sem("t5_w")
        na_w = sem("na_w")
        bias_in = sem("bias_in")
        bias_ok = sem("bias_ok")
        mem_in = sem("mem_in")
        r_in = sem("r_in")
        r_mm = sem("r_mm")
        r_pre = sem("r_pre")
        r_exp = sem("r_exp")
        r_done = sem("r_done")
        e_in = [sem(f"e_in{i}") for i in range(MOE_RING)]
        e_up = sem("e_up")
        e_act = sem("e_act")
        e_sig = sem("e_sig")
        e_down = sem("e_down")
        e_acc = sem("e_acc")
        out_done = sem("out_done")
        f_in = [sem(f"f_in{i}") for i in range(MOE_RING)]
        rank_done = sem("rank_done")
        over_ready = sem("over_ready")
        over_sum = sem("over_sum")
        flag_ready = sem("flag_ready")
        sel_ready = sem("sel_ready")
        gath_done = sem("gath_done")
        selt_done = sem("selt_done")
        selt_moved = sem("selt_moved")
        xe_moved = sem("xe_moved")
        up_done = sem("up_done")
        up_silu = sem("up_silu")
        up_act = sem("up_act")
        hid_turned = sem("hid_turned")
        hid_moved = sem("hid_moved")
        down_done = sem("down_done")
        down_moved = sem("down_moved")
        scat_done = sem("scat_done")
        scat_read = sem("scat_read")

        slots = weight_stream(a)
        group_of, last_group, first_group, g_n = [], {}, {}, 0
        for name, _, groups in slots:
            group_of.append(g_n)
            first_group.setdefault(name, g_n)
            g_n += len(groups)
            last_group[name] = g_n
        phase_slots = {}
        for n, (name, _, _) in enumerate(slots):
            phase_slots.setdefault(name, []).append(n)

        NORMS = ["mix0", "ffn0", "mix1", "ffn1", "mem", "mix2", "ffn2"]
        NLOADS = 11
        ADA_EARLY, ADA_LATE = slice(0, 6), slice(6, None)
        views = dict(zt=zt, zn=zn, dist=dist, dil_bias=dil_bias, na_bias=na_bias)
        att = {s: attention_segments(s, views) for s in ("moba", "diff", "block2")}
        seg_base, unit_base, nsegs, nunits = {}, {}, 0, 0
        for s_name in ("moba", "diff", "block2"):
            seg_base[s_name], unit_base[s_name] = nsegs, nunits
            nsegs += len(att[s_name][1])
            nunits += len(att[s_name][0])
        LAG = 3
        SEGS = 6
        segbuf = work[:, 0:SEGS * S].rearrange("p (r n) -> p r n", r=SEGS)
        ptbuf = work[:, SEGS * S:2048].rearrange("p (r n) -> p r n", r=2)
        QK = {"moba": [(8, G_EVQ), (10, G_EVQ), (12, G_EVK), (14, G_EVK)],
              "diff": [(2 * i, G_ODQ if i < 4 else G_ODK) for i in range(8)],
              "block2": [(0, G_NAQ), (2, G_NAQ), (4, G_NAK), (6, G_NAK), (8, G_DLQ), (10, G_DLQ), (12, G_DLQ),
                         (14, G_DLK), (16, G_DLK), (18, G_DLK), (20, G_MMQ), (22, G_MMK)]}
        def norm_bank(b):
            return (sp_[:, 0, :], sp_[:, 1, :], op[:, 0, :])[b]

        def norm_scale(b):
            return (work[:, 1024:1536], work[:, 1536:2048], work[:, 0:512])[b]

        qk_base, qk_bank, n = {}, {}, 0
        for s_name in ("moba", "diff", "block2"):
            qk_base[s_name] = n
            qk_bank[s_name] = n // 4
            n += len(QK[s_name])

        sub = tk[:, 0:2048].rearrange("p (c n) -> p c n", c=2 * PEER_H)
        cand = tk[:, 2048:4096].rearrange("p (h n) -> p h n", h=PEER_H)
        hot = tk[:, 4096:6144].rearrange("p (c n) -> p c n", c=SLOTS)
        diag = work[:, 0:512].rearrange("p (r n) -> p r n", r=4)
        keys = work[:, 512:768].rearrange("p (c n) -> p c n", c=2)
        keysT = work[:, 768:1024].rearrange("p (c n) -> p c n", c=2)
        top = work[:, 1024:1280].rearrange("p (c n) -> p c n", c=2 * PEER_H)
        topi = work[:, 1280:1536].bitcast(U32).rearrange("p (c n) -> p c n", c=2 * PEER_H)
        topf = work[:, 1536:1792].rearrange("p (c n) -> p c n", c=2 * PEER_H)
        score = work[:, 1792:1920].rearrange("p (h n) -> p h n", h=PEER_H)
        pos = work[:, 1920:2048].bitcast(U32).rearrange("p (h n) -> p h n", h=PEER_H)

        ml_arg = tk[:, 0:2 * 384].rearrange("p (b n) -> p b n", b=2)
        ml_p = tk[:, 768:768 + 2 * 384].rearrange("p (b n) -> p b n", b=2)
        mo_sig = tk[:, 1536:2560].rearrange("p (t n) -> p t n", t=T)
        mnorm = tk[:, 2560:3072]
        ml_rows = tk[0:4, 3072:3072 + 9 * S].rearrange("p (r n) -> p r n", r=9)
        I_, F_, A_, E_, B_, G_, NM_, EM_, ONE_ = (ml_rows[:, i, :] for i in range(9))
        ml_cols = small[:, 0:16].rearrange("p (c t h) -> p c t h", c=2, t=T)
        t5_hot = tk[0:T5_BUCKETS, 0:TW]
        t5_mask = tk[0:DIL_HPG, 1024:1024 + 3 * TW]
        t5_out = tk[0:DIL_HPG, 2560:2560 + 3 * TW]
        t5_tab = work[0:T5_BUCKETS, 0:12]
        na_pad = tk[0:NA_HEADS * NDR, 4096:4096 + RW]

        moe_slot = [ring[:, i, :] for i in range(RING)] + [zbuf[:, 0:4096], tk[:, 0:4096]]
        aT = zbuf[:, 4096:5120].rearrange("p (c n) -> p c n", c=4)
        uT = zbuf[:, 5120:6144].rearrange("p (c n) -> p c n", c=4)
        w_gate = zbuf[:, 6144:6144 + T * N_EXP].rearrange("p (t n) -> p t n", t=T)
        route = zbuf[:, 6400:6400 + 256]
        route_u = zbuf[:, 6656:6672].bitcast(U32)
        rbias = zbuf[:, 6700:6736]
        picked = zbuf[:, 6800:6864].rearrange("p (t n) -> p t n", t=T)
        rank = zbuf[:, 6864:6928].rearrange("p (t n) -> p t n", t=T)
        w_over = zbuf[:, 6928:6992].rearrange("p (t n) -> p t n", t=T)
        below = zbuf[:, 6992:7056].rearrange("p (t n) -> p t n", t=T)
        over = zbuf[:, 7056:7058]
        flag = zbuf[:, 7058:7059].bitcast(U32)
        all_ones = gvec[:, 0:P]
        earlier = gvec[:, P:2 * P]
        xe = mod[:, 0:1024].rearrange("p (k n) -> p k n", k=KT)
        eout = mod[:, 1024:2048]
        selT = mod[:, 2048:2304].rearrange("p (t n) -> p t n", t=T)
        sel = mod[:, 2304:2560].rearrange("p (t n) -> p t n", t=T)
        selg = mod[:, 2560:2816].rearrange("p (t n) -> p t n", t=T)
        hid = mod[:, 2816:3328].rearrange("p (f n) -> p f n", f=4)
        hid_rows = mod[:, 3328:3840]
        w_e = [a["w1_2"][0], a["w3_2"][0], a["w2_2"][0]]

        block = ctx.enter_context(nc.Block())

        def moe_view(s, j):
            return moe_slot[s].rearrange("p (k c) -> p k c", k=KT if j < 2 else 4)

        def moe_src(j, e):
            w = w_e[j]
            v = w.rearrange("e (k p) n -> p e k n", p=P)
            if isinstance(e, int):
                return v[:, e, :, :]
            return v[:, bass.ds(e, 1), :, :].rearrange("p o k n -> p (o k) n")

        @block.sync
        def _(sync):
            sync.dma_start(x[:], a["x"][0].rearrange("(t p) n -> p t n", p=P)).then_inc(loaded, 16)
            sync.dma_start(cst[:], a["cst"]).then_inc(loaded, 16)
            sync.dma_start(cact[:], a["c"][0].rearrange("(k p) -> p k", p=P)).then_inc(loaded, 16)
            sync.dma_start(gains[:], a["gains"]).then_inc(loaded, 16)
            sync.dma_start(convw[:], a["conv_cols"]).then_inc(loaded, 16)
            sync.dma_start(gate_w[:], a["ev_w_in"][0][:, 2048:2056].rearrange("(k p) n -> p k n", p=P)).then_inc(loaded, 16)
            sync.dma_start(gate_b[:, 0:1], a["ev_igate_b"].rearrange("o h -> h o")).then_inc(loaded, 16)
            sync.dma_start(gate_b[:, 1:2], a["ev_fgate_b"].rearrange("o h -> h o")).then_inc(loaded, 16)
            sync.dma_start(ada_b[:], a["ada_b"][0].rearrange("(n c) -> n c", n=12)).then_inc(loaded, 16)
            sync.dma_start(gw36[:, :, 0:4], a["w_r1_2"][0].rearrange("(k p) n -> p k n", p=P)).then_inc(loaded, 16)
            sync.dma_start(gw36[:, :, 4:36], a["w_r2_2"][0].rearrange("(k p) n -> p k n", p=P)).then_inc(loaded, 16)
            for n, (name, w, _) in enumerate(slots):
                if n >= RING:
                    sync.wait_ge(gemm_done, group_of[n - RING] + len(slots[n - RING][2]))
                if n == phase_slots["ada1"][0]:
                    sync.dma_start(ada_b[:], a["ada_b"][1].rearrange("(n c) -> n c", n=12)).then_inc(ada_b_in, 16)
                dst = ring[:, n % RING, :].rearrange("p (k c) -> p k c", k=KT)
                sync.dma_start(dst, w).then_inc(w_landed[n % RING], 16)
            sync.wait_ge(gemm_done, g_n)
            sync.wait_ge(h_ready, 2 * len(NORMS))
            sync.wait_ge(r_in, 32)
            for s in (0, 3, 1, 4, 2, 5):
                e, j = divmod(s, 3)
                sync.dma_start(moe_view(s, j), moe_src(j, e)).then_inc(e_in[s], 16)
            with sync.Fori(1, N_EXP // 2) as i:
                for s in (0, 3, 1, 4, 2, 5):
                    e, j = divmod(s, 3)
                    if j < 2:
                        sync.wait_ge(up_done, i * 2 + (j + 1 - 2))
                    else:
                        sync.wait_ge(down_done, i)
                    sync.dma_start(moe_view(s, j), moe_src(j, i * 2 + e)).then_inc(e_in[s], 16)
            sync.wait_ge(flag_ready, 1)
            with sync.If(sync.value_load(flag[0:1, 0:1], min_val=0, max_val=2 * S) > 0):
                sync.wait_ge(up_done, N_EXP)
                sync.wait_ge(down_done, N_EXP // 2)
                for s in range(MOE_RING):
                    e, j = divmod(s, 3)
                    sync.dma_start(moe_view(s, j), moe_src(j, e)).then_inc(f_in[s], 16)
                with sync.Fori(1, N_EXP // 2) as i:
                    for s in range(MOE_RING):
                        e, j = divmod(s, 3)
                        if j < 2:
                            sync.wait_ge(e_up, i * 8 + (4 * e + 2 * j + 2 - 8))
                        else:
                            sync.wait_ge(e_down, i * 8 + (4 * e + 4 - 8))
                        sync.dma_start(moe_view(s, j), moe_src(j, i * 2 + e)).then_inc(f_in[s], 16)
            sync.wait_ge(x_ready, 6 * T)
            sync.dma_start(out[0].rearrange("(t p) n -> p t n", p=P), x[:]).then_inc(out_done, 16)
            sync.wait_ge(out_done, 16)

        @block.gpsimd
        def _(pool):
            own = [0]

            def link(ins):
                own[0] += 1
                ins.then_inc(pool_own, 1)
                pool.wait_ge(pool_own, own[0])

            def load_gain(n, src):
                if n >= 1:
                    pool.wait_ge(gvec_used, T * n)
                row = bass.AP(tensor=src.tensor, offset=src.offset, ap=[[0, P], [1, D]])
                pool.dma_start(gvec[:], row).then_inc(gvec_in, 16)

            load_gain(0, a["norm_mix_g"][0])
            link(pool.memset(na_pad, 0.0))
            for hh in range(NA_HEADS):
                pool.dma_start(na_pad[hh * NDR:(hh + 1) * NDR, GRID_W - 16:GRID_W + 15],
                               a["na_rpb_2"][0, hh, 4:4 + NDR, :]).then_inc(t5_in, 16)
            pool.dma_start(t5_hot, a["t5_hot"]).then_inc(t5_in, 16)
            pool.dma_start(t5_mask.rearrange("p (g n) -> p g n", g=3), a["t5_mask"]).then_inc(t5_in, 16)
            pool.dma_start(t5_tab, a["t5_table_2"]).then_inc(t5_in, 16)
            pool.wait_ge(t5_in, 16 * (NA_HEADS + 3))
            pool.dma_start(na_rows, na_pad).then_inc(na_w, 16)
            pool.wait_ge(na_w, 16)
            W = NA_HEADS * NDR * RW
            pool.dma_start(na_rep, bass.AP(tensor=na_rows.tensor, offset=0, ap=[[0, GRID_W], [1, W]])).then_inc(na_w, 16)
            pool.wait_ge(t5_sum, 1)
            pool.dma_start(t5_rows.rearrange("(g h) n -> h g n", g=3), t5_out.rearrange("p (g n) -> p g n", g=3)).then_inc(t5_w, 16)
            pool.wait_ge(t5_w, 16)
            pool.dma_start(t5_rep, bass.AP(tensor=t5_rows.tensor, offset=0, ap=[[0, P], [1, 12 * TW]])).then_inc(t5_w, 16)
            pool.wait_ge(t5_w, 32)
            pool.wait_ge(na_w, 32)
            pool.dma_start(mnorm, bass.AP(tensor=a["ev_mnorm_g"].tensor, offset=0, ap=[[0, P], [1, 512]])).then_inc(mem_in, 16)

            pool.dma_start(lam_rows[:], bass.AP(tensor=a["od_lam"].tensor, offset=0, ap=[[0, P], [64, 4], [1, 64]])).then_inc(lam_in, 16)
            pool.dma_start(onorm, bass.AP(tensor=a["od_onorm_g"].tensor, offset=0, ap=[[0, P], [1, P]])).then_inc(lam_in, 16)
            load_gain(1, a["norm_ffn_g"][0])

            def peer(l):
                table = [a["peer_u"], a["peer_v"]]
                pool.wait_ge(gemm_moved, last_group[f"out{l}"])
                pool.wait_ge(y_ready, l + 1)
                pool.dma_start(keys, a["peer_keys"][l].rearrange("c n d -> n c d")).then_inc(keys_in, 16)

                def row_used(phase, i, k, shared=False):
                    n = phase // 2
                    if phase % 2 == 0:
                        return udot, i * ROWS + (n * SLOTS + k + 1)
                    if not shared:
                        return vsum, i * ROWS + (pe_rows_before(n) + k + 1)
                    f = SHARED[n % 2]
                    if k in PE_ROWS:
                        w = len(PE_ROWS)
                        return vsum, i * w + (pe_rows_before(n) + (ROWS - w) * f + PE_ROWS.index(k) + 1)
                    w = len(DVE_ROWS)
                    return vshare, i * w + (dve_rows_before(n) - w * f + DVE_ROWS.index(k) + 1)

                def gather(phase, i, k, used=None):
                    t, which = divmod(phase % 4, 2)
                    if used is not None:
                        pool.wait_ge(*used)
                        pool.sem_inc(row_free, 1)
                    c = i * ROWS + k
                    src = idx[:, t, c:c + 1] if isinstance(c, int) else idx[:, t, bass.ds(c, 1)]
                    pool.tensor_copy(stage[:, k:k + 1], src).then_inc(idx_staged, 1)
                    pool.wait_ge(idx_staged, i * ROWS + (phase * SLOTS + k + 1))
                    pool.sem_inc(row_free, 1)
                    pool.indirect_dma_start(rowbuf[:, k, :], None, table[which].rearrange("l n d -> (l n) d"),
                                            bass.IndirectOffsetOnAxis(ap=stage[:, k:k + 1], axis=0)).then_inc(row_in[k], 16)

                pool.wait_ge(sub_done, 8 * (l + 1))
                for phase in range(4 * l, 4 * l + 4):
                    t, which = divmod(phase % 4, 2)
                    if which == 0:
                        pool.wait_ge(idx_ready, 2 * l + t + 1)
                    for k in range(ROWS):
                        gather(phase, 0, k, None if phase == 4 * l else row_used(phase - 1, GROUPS - 1, k, True))
                    whole = GROUPS if which == 0 else SHARED[t] + 1
                    with pool.Fori(1, whole) as i:
                        for k in range(ROWS):
                            gather(phase, i, k, row_used(phase, i - 1, k))
                    if which == 1:
                        with pool.Fori(whole, GROUPS) as i:
                            for k in range(ROWS):
                                gather(phase, i, k, row_used(phase, i - 1, k, True))

            peer(0)
            load_gain(2, a["norm_mix_g"][1])
            load_gain(3, a["norm_ffn_g"][1])
            peer(1)
            load_gain(4, a["g_mem_2"][0])
            pool.wait_ge(x_ready, 4 * T)
            pool.dma_start(y[:], a["mem_2"][0].rearrange("(t p) n -> p t n", p=P)).then_inc(mem_in, 16)
            pool.dma_start(dil_bias, bass.AP(tensor=t5_rep.tensor, offset=127,
                                             ap=[[12 * TW - 1, P], [TW, 12], [1, 384]])).then_inc(bias_in, 16)
            W = NA_HEADS * NDR * RW
            for hh in range(NA_HEADS):
                for r2 in range(2):
                    pool.dma_start(na_bias[r2 * GRID_W:(r2 + 1) * GRID_W, hh, :].rearrange("p (j n) -> p j n", j=6),
                                   bass.AP(tensor=na_rep.tensor,
                                           offset=hh * NDR * RW + (1 - r2) * RW + GRID_W - 1,
                                           ap=[[W - 1, GRID_W], [RW, 6], [1, GRID_W]])).then_inc(bias_in, 16)
            load_gain(5, a["g_mix_2"][0])
            load_gain(6, a["g_ffn_2"][0])
            pool.wait_ge(h_ready, 2 * len(NORMS))
            pool.dma_start(rbias[:, 0:4], bass.AP(tensor=a["b_r1_2"].tensor, offset=0, ap=[[0, P], [1, 4]])).then_inc(r_in, 16)
            pool.dma_start(rbias[:, 4:36], bass.AP(tensor=a["b_r2_2"].tensor, offset=0, ap=[[0, P], [1, 32]])).then_inc(r_in, 16)

        @block.tensor
        def _(pe):
            def project(name, part=slice(None)):
                for n in phase_slots[name][part]:
                    _, _, groups = slots[n]
                    w = ring[:, n % RING, :].rearrange("p (k c) -> p k c", k=KT)
                    pe.wait_ge(w_landed[n % RING], 16 * (n // RING + 1))
                    for i, grp in enumerate(groups):
                        g = group_of[n] + i
                        if g >= 2:
                            pe.wait_ge(gemm_moved, g - 1)
                        bank = gp[:, g % 2, :]
                        if grp[0] == "bcast":
                            for k in range(KT):
                                pe.matmul(bank, cact[:, k:k + 1].to_broadcast([P, P]), w[:, k, :], start=k == 0, stop=False)
                            mm = pe.matmul(bank, ident[0:12, grp[1]:grp[1] + 1].to_broadcast([12, P]), ada_b[:, :],
                                           start=False, stop=True)
                        elif grp[0] == "rows":
                            for k in range(KT):
                                mm = pe.matmul(bank, hT[:, k, grp[1] * P:(grp[1] + 1) * P], w[:, k, :],
                                               start=k == 0, stop=k == KT - 1)
                        elif grp[0] == "rows2":
                            for t in range(T):
                                for k in range(KT):
                                    mm = pe.matmul(bank[:, t * S:(t + 1) * S], hT[:, k, t * P:(t + 1) * P],
                                                   w[:, k, grp[1]:grp[1] + S], start=k == 0, stop=k == KT - 1)
                        else:
                            for c in range(2):
                                for k in range(KT):
                                    mm = pe.matmul(bank[:, c * S:(c + 1) * S], w[:, k, grp[1] + c * P:grp[1] + (c + 1) * P],
                                                   hT[:, k, :], start=k == 0, stop=k == KT - 1)
                        mm.then_inc(gemm_done, 1)

            def keep_clock(name, n):
                pe.wait_ge(gemm_moved, last_group[name])
                for _ in range(n):
                    pe.matmul(gp[:, 0, :], ident, cst[:, 0:512], start=True, stop=True)

            turned = [0]

            def turn(src):
                for t in range(T):
                    for b in range(2):
                        n = turned[0]
                        if n >= 2:
                            pe.wait_ge(turn_moved, n - 1)
                        for c in range(4):
                            k = 4 * b + c
                            mm = pe.transpose(tp[:, n % 2, c * P:(c + 1) * P], src[:, t, k * P:(k + 1) * P], ident)
                        mm.then_inc(turn_done, 1)
                        turned[0] += 1

            def turn_h(n):
                pe.wait_ge(h_ready, T * (n + 1))
                turn(h if NORMS[n] != "mem" else y)

            def hT_ready():
                pe.wait_ge(turn_moved, turned[0])

            def head_sums(stage_name):
                n0 = qk_base[stage_name]
                pairs = len(QK[stage_name])
                for i in range(pairs):
                    b, j = divmod(i, 4)
                    pe.wait_ge(qk_sq, n0 + i + 1)
                    pe.matmul(norm_bank(b)[32 * j:32 * (j + 1), :], blk[:, 48:80], work[:, (i % 2) * 512:(i % 2) * 512 + 512],
                              start=True, stop=True).then_inc(qk_sum, 1)
                keep_clock({"moba": "in0", "diff": "in1", "block2": "in2"}[stage_name], 3)
                for i in range(pairs):
                    b, j = divmod(i, 4)
                    if j == 0:
                        pe.wait_ge(qk_inv, qk_bank[stage_name] + b + 1)
                    if i >= 2:
                        pe.wait_ge(qk_done, n0 + i - 1)
                    for half in range(2):
                        r = 32 * j + 16 * half
                        mm = pe.matmul(tp[64 * half:64 * (half + 1), i % 2, :], ident[:, r:r + 1].to_broadcast([P, 64]),
                                       norm_scale(b), start=True, stop=True)
                    mm.then_inc(qk_spread, 1)

            def attention(stage_name):
                units, segs = att[stage_name]
                b0 = seg_base[stage_name]
                u0 = unit_base[stage_name]
                for j in range(len(segs) + LAG + 1):
                    if j < len(segs):
                        sg = segs[j]
                        if j >= 2:
                            pe.wait_ge(s_read, b0 + j - 1)
                        pe.matmul(sp_[:, j % 2, 0:sg["nk"]], sg["q"], sg["k"], start=True, stop=True).then_inc(s_done, 1)
                    i = j - LAG
                    if 0 <= i < len(segs):
                        sg = segs[i]
                        pe.wait_ge(e_done, u0 + sg["u"] + 1)
                        if i >= 2:
                            pe.wait_ge(t_moved, b0 + i - 1)
                        for c in range(sg["nk"] // P):
                            mm = pe.transpose(tp[:, i % 2, c * P:(c + 1) * P], segbuf[:, i % SEGS, c * P:(c + 1) * P], ident)
                        mm.then_inc(t_done, 1)
                    i = j - LAG - 1
                    if 0 <= i < len(segs):
                        sg = segs[i]
                        pe.wait_ge(t_moved, b0 + i + 1)
                        if sg["first"] and sg["u"] >= 2:
                            pe.wait_ge(o_read, u0 + sg["u"] - 1)
                        nkt = sg["nk"] // P
                        for c in range(nkt):
                            mm = pe.matmul(op[:, sg["u"] % 2, 0:sg["dv"]], ptbuf[:, i % 2, c * P:(c + 1) * P],
                                           zn[:, c, sg["v"]:sg["v"] + sg["dv"]],
                                           start=sg["first"] and c == 0, stop=sg["last"] and c == nkt - 1)
                        mm.then_inc(o_done, 1)

            def mlstm():
                for part in range(2):
                    for k in range(KT):
                        mm = pe.matmul(sp_[0:4, part, 0:S], gate_w[:, k, 4 * part:4 * part + 4], hT[:, k, :],
                                       start=k == 0, stop=k == KT - 1)
                mm.then_inc(gates_mm, 1)
                pe.wait_ge(gates_g, 1)
                for c, row in enumerate((G_, EM_)):
                    for t in range(T):
                        mm = pe.transpose(tp[:, 0, 4 * (2 * c + t):4 * (2 * c + t) + 4], row[:, t * P:(t + 1) * P], ident[0:4, 0:4])
                mm.then_inc(gates_t, 1)
                keep_clock("in0", 4)
                pe.wait_ge(silu_done, 8)
                pe.wait_ge(gates_c, 1)

                def scores(hh):
                    if hh >= 2:
                        pe.wait_ge(mm_p, hh - 1)
                        pe.wait_ge(mm_arg, hh - 1)
                    q, k = zt(hh), zt(4 + hh)
                    pe.matmul(tp[:, hh % 2, 0:S], ident[0:4, hh:hh + 1].to_broadcast([4, P]), NM_,
                              start=True, stop=True).then_inc(mm_b, 1)
                    pe.matmul(sp_[:, hh % 2, 0:S], k[:, 0:P], q, start=True, stop=True)
                    pe.matmul(sp_[:, hh % 2, S:S + P], k[:, P:S], q[:, P:S], start=True, stop=True).then_inc(mm_s, 1)

                scores(0)
                for hh in range(M_HEADS):
                    if hh + 1 < M_HEADS:
                        scores(hh + 1)
                    pe.wait_ge(mm_p, hh + 1)
                    if hh >= 2:
                        pe.wait_ge(mm_read, hh - 1)
                    pt = ml_p[:, hh % 2, :]
                    o = op[:, hh % 2, :]
                    for rhs, c0, w in ((None, 0, P), (ones1, S, 1)):
                        for t in range(T):
                            for u in range(t + 1):
                                r = ones1[:, 0:1] if rhs is not None else zn[:, u, P * hh:P * (hh + 1)]
                                mm = pe.matmul(o[:, c0 + t * w:c0 + (t + 1) * w], pt[:, (t + u) * P:(t + u + 1) * P], r,
                                               start=u == 0, stop=u == t)
                    mm.then_inc(mm_o, 1)

            def peer(l):
                pe.wait_ge(keys_in, 16 * (l + 1))
                for c in range(2):
                    mm = pe.transpose(op[:, 0, c * P:(c + 1) * P], keys[:, c, :], ident)
                mm.then_inc(keys_t, 1)
                pe.wait_ge(keys_m, l + 1)
                pe.wait_ge(gemm_moved, last_group[f"wq{l}"])
                for t in range(T):
                    for b in range(4):
                        n = (2 * l + t) * 4 + b
                        if n >= 2:
                            pe.wait_ge(sub_moved, n - 1)
                        for c in range(4):
                            i = 4 * b + c
                            mm = pe.matmul(sp_[:, n % 2, c * P:(c + 1) * P], zt(i)[:, t * P:(t + 1) * P], keysT[:, i % 2, :],
                                           start=True, stop=True)
                        mm.then_inc(sub_done, 1)
                    if l == 0 and t == 0:
                        pe.wait_ge(ada_b_in, 16)
                        project("ada1", ADA_EARLY)

            def peer_sum(l):
                for t in range(T):
                    phase = 4 * l + 2 * t + 1
                    base = pe_rows_before(2 * l + t)
                    f = SHARED[t]
                    w = len(PE_ROWS)
                    if l + t > 0:
                        pe.wait_ge(x_ready, T * (2 * l + 1) + t)

                    def add(i, k, shared, last=False):
                        pe.wait_ge(row_in[k], i * 16 + 16 * (phase * GROUPS + 1))
                        if shared:
                            m = PE_ROWS.index(k)
                            pe.wait_ge(diag_ready, i * w + (base + (ROWS - w) * f + m + 1))
                            d = diag[:, m % 3, :]
                        else:
                            pe.wait_ge(diag_ready, i * ROWS + (base + k + 1))
                            d = diag[:, k % 4, :]
                        for n in range(2):
                            mm = pe.matmul(op[:, n, :], d, rowbuf[:, k, n * 512:(n + 1) * 512],
                                           start=isinstance(i, int) and i + k == 0, stop=last, skip_group_check=True)
                        mm.then_inc(vsum, 1)

                    for k in range(ROWS):
                        add(0, k, False)
                    if f > 1:
                        with pe.Fori(1, f) as i:
                            for k in range(ROWS):
                                add(i, k, False)
                    with pe.Fori(f, GROUPS - 1) as i:
                        for k in PE_ROWS:
                            add(i, k, True)
                    for k in PE_ROWS:
                        add(GROUPS - 1, k, True, last=k == PE_ROWS[-1])

            pe.wait_ge(loaded, 16 * NLOADS)
            pe.wait_ge(c_ready, 1)
            project("ada0")
            pe.wait_ge(t5_in, 16 * (NA_HEADS + 3))
            for g in range(DIL_GROUPS):
                mm = pe.matmul((sp_ if g < 2 else op)[0:DIL_HPG, g % 2, 0:TW], t5_tab[:, g * DIL_HPG:(g + 1) * DIL_HPG], t5_hot,
                               start=True, stop=True)
            mm.then_inc(t5_mm, 1)
            keep_clock("ada0", 6)
            turn_h(0)
            hT_ready()
            pe.wait_ge(t5_sum, 1)
            project("in0")
            mlstm()
            head_sums("moba")
            pe.wait_ge(qk_done, len(QK["moba"]))
            attention("moba")
            pe.wait_ge(y_ready, 1)
            turn(y)
            hT_ready()
            project("out0")
            for l in range(2):
                keep_clock(f"out{l}", 15)
                turn_h(2 * l + 1)
                hT_ready()
                project(f"wq{l}")
                peer(l)
                if l == 0:
                    project("ada1", ADA_LATE)
                peer_sum(l)
                keep_clock(f"wq{l}" if l else "ada1", 13)
                turn_h(2 * l + 2)
                hT_ready()
                if l == 0:
                    project("in1")
                    head_sums("diff")
                    pe.wait_ge(qk_done, qk_base["block2"])
                    attention("diff")
                    keep_clock("in1", 12)
                    pe.wait_ge(y_ready, 2)
                    turn(y)
                    hT_ready()
                    project("out1")
            project("mem")
            turn_h(5)
            hT_ready()
            project("in2")
            head_sums("block2")
            pe.wait_ge(qk_done, qk_base["block2"] + len(QK["block2"]))
            attention("block2")
            pe.wait_ge(y_ready, 3)
            turn(y)
            hT_ready()
            project("out2")
            keep_clock("out2", 8)
            turn_h(6)
            hT_ready()
            for t in range(T):
                for k in range(KT):
                    mm = pe.matmul(op[:, t, 0:36], hT[:, k, t * P:(t + 1) * P], gw36[:, k, :], start=k == 0, stop=k == KT - 1)
            mm.then_inc(r_mm, 1)

            def expert(s0, i):
                e2 = s0 // 3
                for j in range(2):
                    pe.wait_ge(f_in[s0 + j], i * 16 + 16)
                    w = moe_slot[s0 + j].rearrange("p (k c) -> p k c", k=KT)
                    for b in range(2):
                        if not (isinstance(i, int) and e2 == 0):
                            pe.wait_ge(e_act, i * 4 + (2 * e2 + b - 1))
                        bank = (sp_ if j == 0 else gp)[:, b, :]
                        for c in range(2):
                            f = 2 * b + c
                            for k in range(KT):
                                mm = pe.matmul(bank[:, c * S:(c + 1) * S], w[:, k, f * P:(f + 1) * P], hT[:, k, :],
                                               start=k == 0, stop=k == KT - 1)
                        mm.then_inc(e_up, 1)
                pe.wait_ge(f_in[s0 + 2], i * 16 + 16)
                w = moe_slot[s0 + 2].rearrange("p (k c) -> p k c", k=4)
                pe.wait_ge(e_act, i * 4 + (2 * e2 + 2))
                for t in range(T):
                    for n in range(2):
                        if not (isinstance(i, int) and e2 == 0):
                            pe.wait_ge(e_acc, i * 8 + (4 * e2 + 2 * t + n - 3))
                        bank = (tp if t == 0 else op)[:, n, :]
                        for f in range(4):
                            mm = pe.matmul(bank, aT[:, f, t * P:(t + 1) * P], w[:, f, n * 512:(n + 1) * 512],
                                           start=f == 0, stop=f == 3)
                        mm.then_inc(e_down, 1)

            pe.wait_ge(r_done, 1)
            pe.matmul(tp[:, 0, 0:N_EXP], earlier, picked[:, 0, :], start=True, stop=True)
            pe.matmul(tp[:, 0, N_EXP:2 * N_EXP], all_ones, picked[:, 0, :], start=True, stop=False)
            pe.matmul(tp[:, 0, N_EXP:2 * N_EXP], earlier, picked[:, 1, :], start=False, stop=True).then_inc(rank_done, 1)
            pe.wait_ge(over_ready, 1)
            pe.matmul(tp[:, 1, 0:1], all_ones, over[:, 0:1], start=True, stop=True).then_inc(over_sum, 1)
            pe.wait_ge(flag_ready, 1)

            def first(p):
                return isinstance(p, int) and p == 0

            def gather_pair(p):
                pe.wait_ge(sel_ready, p + 1)
                if not first(p):
                    pe.wait_ge(xe_moved, p)
                for k in range(KT):
                    for t in range(T):
                        mm = pe.matmul(op[:, k // 4, (k % 4) * P:(k % 4 + 1) * P], h[:, t, k * P:(k + 1) * P], sel[:, t, :],
                                       start=t == 0, stop=t == T - 1)
                mm.then_inc(gath_done, 1)

            def up(p):
                pe.wait_ge(xe_moved, p + 1)
                if not first(p):
                    pe.wait_ge(hid_moved, p)
                for j in range(2):
                    for e2 in range(2):
                        pe.wait_ge(e_in[3 * e2 + j], p * 16 + 16)
                    for k in range(KT):
                        for e2 in range(2):
                            w = moe_slot[3 * e2 + j].rearrange("p (k c) -> p k c", k=KT)
                            mm = pe.matmul(gp[e2 * CAP:(e2 + 1) * CAP, j, :], xe[:, k, e2 * CAP:(e2 + 1) * CAP], w[:, k, :],
                                           start=k == 0, stop=k == KT - 1, skip_group_check=True)
                    mm.then_inc(up_done, 1)

            def turn_hidden(p):
                pe.wait_ge(up_act, p + 1)
                for f in range(4):
                    mm = pe.transpose(gp[:, 0, f * P:(f + 1) * P], hid_rows[:, f * P:(f + 1) * P], ident)
                mm.then_inc(hid_turned, 1)

            def scatter(p):
                pe.wait_ge(down_moved, p + 1)
                pe.wait_ge(selt_moved, p * 2 + 2)
                for n in range(4):
                    if n >= 2:
                        pe.wait_ge(scat_read, p * 4 + (n - 1))
                    pe.matmul(tp[:, n % 2, :], selT[:, n // 2, :], eout[:, (n % 2) * 512:(n % 2 + 1) * 512],
                              start=True, stop=True).then_inc(scat_done, 1)

            def turn_sel(p, before):
                pe.wait_ge(sel_ready, p + 1)
                for t in range(T):
                    if before:
                        pe.wait_ge(scat_read, p * 4 - (1 - t))
                    pe.transpose(tp[:, t, 0:P], selg[:, t, :], ident).then_inc(selt_done, 1)

            def down(p):
                pe.wait_ge(hid_moved, p + 1)
                if not first(p):
                    pe.wait_ge(down_moved, p)
                for e2 in range(2):
                    pe.wait_ge(e_in[3 * e2 + 2], p * 16 + 16)
                for n in range(2):
                    for f in range(4):
                        for e2 in range(2):
                            w = moe_slot[3 * e2 + 2].rearrange("p (k c) -> p k c", k=4)
                            mm = pe.matmul(sp_[e2 * CAP:(e2 + 1) * CAP, n, :], hid[:, f, e2 * CAP:(e2 + 1) * CAP],
                                           w[:, f, n * 512:(n + 1) * 512], start=f == 0, stop=f == 3, skip_group_check=True)
                mm.then_inc(down_done, 1)

            gather_pair(0)
            up(0)
            turn_sel(0, False)
            turn_hidden(0)
            gather_pair(1)
            down(0)
            with pe.Fori(1, N_EXP // 2 - 1) as p:
                up(p)
                scatter(p - 1)
                turn_sel(p, True)
                turn_hidden(p)
                gather_pair(p + 1)
                down(p)
            last = N_EXP // 2 - 1
            up(last)
            scatter(last - 1)
            turn_sel(last, True)
            turn_hidden(last)
            down(last)
            scatter(last)
            with pe.If(pe.value_load(flag[0:1, 0:1], min_val=0, max_val=2 * S) > 0):
                pe.wait_ge(scat_read, 2 * N_EXP)
                pe.wait_ge(down_moved, N_EXP // 2)
                expert(0, 0)
                expert(3, 0)
                with pe.Fori(1, N_EXP // 2) as i:
                    expert(0, i)
                    expert(3, i)

        @block.scalar
        def _(act):
            own = [0]

            def link(ins):
                own[0] += 1
                ins.then_inc(act_own, 1)
                act.wait_ge(act_own, own[0])

            def move(name, part=slice(None)):
                for n in phase_slots[name][part]:
                    for i, grp in enumerate(slots[n][2]):
                        g = group_of[n] + i
                        act.wait_ge(gemm_done, g + 1)
                        bank = gp[:, g % 2, :]
                        if grp[0] == "bcast":
                            m, half = divmod(grp[1], 2)
                            dst = mod[:, m * D + half * CH:m * D + (half + 1) * CH] if m < 5 else \
                                g2[:, int(name[-1]), half * CH:(half + 1) * CH]
                        elif grp[0] == "cols":
                            dst = zt2(grp[2])
                        else:
                            buf, c0 = grp[2]
                            buf = zn if buf == "zn" else y
                            if grp[0] == "rows":
                                dst = buf[:, grp[1], c0:c0 + CH]
                            else:
                                dst = buf[:, :, c0:c0 + S]
                                bank = bank.rearrange("p (t n) -> p t n", t=T)
                        act.activation(dst, bank, ACT.Copy).then_inc(gemm_moved, 1)

            turned = [0]

            def move_turned():
                for t in range(T):
                    for b in range(2):
                        n = turned[0]
                        act.wait_ge(turn_done, n + 1)
                        act.activation(hT[:, 4 * b:4 * b + 4, t * P:(t + 1) * P],
                                       tp[:, n % 2, :].rearrange("p (c n) -> p c n", c=4), ACT.Copy).then_inc(turn_moved, 1)
                        turned[0] += 1

            def norm(n):
                act.wait_ge(sumsq, n + 1)
                act.activation(small[:, 62:64], small[:, 60:62], ACT.Sqrt).then_inc(rootd, 1)

            def head_norms(stage_name):
                q = QK[stage_name]
                n0 = qk_base[stage_name]
                for i in range(len(q) + 1):
                    if i < len(q):
                        if i >= 2:
                            act.wait_ge(qk_sum, n0 + i - 1)
                        act.activation(work[:, (i % 2) * 512:(i % 2) * 512 + 512], zt2(q[i][0]), ACT.Square).then_inc(qk_sq, 1)
                    if i >= 1 and i % 4 == 0:
                        act.wait_ge(qk_sum, n0 + i)
                        b = i // 4 - 1
                        act.activation(norm_scale(b), norm_bank(b), ACT.Sqrt, scale=1.0 / 64,
                                       bias=eps[:, 0:1]).then_inc(qk_root, 1)

            def attention(stage_name):
                units, segs = att[stage_name]
                b0 = seg_base[stage_name]
                u0 = unit_base[stage_name]
                for j in range(len(segs) + LAG):
                    i = j - LAG
                    if 0 <= i < len(segs):
                        nk = segs[i]["nk"]
                        act.wait_ge(t_done, b0 + i + 1)
                        if i >= 2:
                            act.wait_ge(o_done, b0 + i - 1)
                        act.activation(ptbuf[:, i % 2, 0:nk], tp[:, i % 2, 0:nk], ACT.Copy).then_inc(t_moved, 1)
                    if j < len(segs) and segs[j]["last"]:
                        u = segs[j]["u"]
                        n = units[u]["n"]
                        act.wait_ge(m_done, u0 + u + 1)
                        r = (j - n + 1) % SEGS
                        w = (n - 1) * S + segs[j]["nk"]
                        lp = work[:, r * S:r * S + w]
                        act.activation(lp, lp, ACT.Exp, bias=nmax[:, u % 8:u % 8 + 1],
                                       accum_out=den[:, u % 8:u % 8 + 1]).then_inc(e_done, 1)

            def mlstm():
                for part, (dst, c) in enumerate(((I_, 0), (F_, 1))):
                    act.wait_ge(gates_mm, 1)
                    if part == 0:
                        act.wait_ge(mem_in, 16)
                    ins = act.activation(dst, sp_[0:4, part, 0:S], ACT.Identity, bias=gate_b[:, c:c + 1])
                ins.then_inc(gates_f, 1)
                act.wait_ge(gates_e, 1)
                link(act.activation(E_, A_, ACT.Exp, scale=-1.0))
                act.activation(E_, E_, ACT.Ln, bias=ones1[0:4, 0:1]).then_inc(gates_l, 1)
                act.wait_ge(gates_e, 2)
                act.activation(EM_, EM_, ACT.Exp, scale=-1.0).then_inc(em_ready, 1)
                act.wait_ge(gates_t, 1)
                act.activation(small[:, 0:16], tp[:, 0, 0:16], ACT.Copy).then_inc(gates_c, 1)
                for c in range(8):
                    act.wait_ge(conv_done, c + 1)
                    acc = work[:, (c % SEGS) * S:(c % SEGS + 1) * S]
                    act.activation(zt(c), acc, ACT.Silu).then_inc(silu_done, 1)
                act.wait_ge(gates_c, 1)
                for hh in range(M_HEADS):
                    act.wait_ge(mm_arg, hh + 1)
                    arg = ml_arg[:, hh % 2, :]
                    act.activation(arg[:, 0:S], arg[:, 0:S], ACT.Exp, bias=ml_cols[:, 0, 0, hh:hh + 1])
                    act.activation(arg[:, S:S + P], arg[:, S:S + P], ACT.Exp, bias=ml_cols[:, 0, 1, hh:hh + 1]).then_inc(mm_exp, 1)
                act.activation(mo_sig, zn[:, :, 512:1024], ACT.Sigmoid).then_inc(sig_done, 1)
                act.wait_ge(hn_sq, 1)
                act.activation(small[:, 32:40], small[:, 24:32], ACT.Sqrt).then_inc(hn_rt, 1)

            def peer(l):
                act.wait_ge(keys_t, l + 1)
                act.activation(keysT, op[:, 0, 0:S].rearrange("p (c n) -> p c n", c=2), ACT.Copy).then_inc(keys_m, 1)
                move_sub(l, 0)
                if l == 0:
                    move("ada1", ADA_EARLY)
                exp_scores(l, 0)
                move_sub(l, 1)

            def move_sub(l, t):
                for b in range(4):
                    n = (2 * l + t) * 4 + b
                    act.wait_ge(sub_done, n + 1)
                    if 2 * l + t > 0 and b == 0:
                        act.wait_ge(sub_free, 2 * l + t)
                    act.activation(sub[:, 4 * b:4 * b + 4, :], sp_[:, n % 2, :].rearrange("p (c n) -> p c n", c=4),
                                   ACT.Copy).then_inc(sub_moved, 1)

            def exp_scores(l, t):
                act.wait_ge(top_ready, 2 * l + t + 1)
                act.activation(gate[:, t, :], gate[:, t, :], ACT.Exp).then_inc(gate_e, 1)

            def peer_coef(l, t):
                n = 2 * l + t
                act.wait_ge(dots_all, n + 1)
                act.activation(coef[:, :], dots[:, :], ACT.Gelu).then_inc(gelu_done, 1)
                act.wait_ge(coef_ready, n + 1)
                base = pe_rows_before(n)
                f = SHARED[t]
                w = len(PE_ROWS)
                for k in range(ROWS):
                    if k >= 4:
                        act.wait_ge(vsum, base + k - 3)
                    elif n > 0:
                        act.wait_ge(vsum, base)
                    act.activation(diag[:, k % 4, :], ident, ACT.Copy, scale=coef[:, k:k + 1]).then_inc(diag_ready, 1)
                if f > 1:
                    with act.Fori(1, f) as i:
                        for k in range(ROWS):
                            act.wait_ge(vsum, i * ROWS + (base + k - 3))
                            act.sem_inc(diag_free, 1)
                            act.activation(diag[:, k % 4, :], ident, ACT.Copy, scale=coef[:, bass.ds(i * ROWS + k, 1)]).then_inc(diag_ready, 1)
                if t == 0:
                    exp_scores(l, 1)
                with act.Fori(f, GROUPS) as i:
                    for m, k in enumerate(PE_ROWS):
                        act.wait_ge(vsum, i * w + (base + (ROWS - w) * f + m - 2))
                        act.sem_inc(diag_free, 1)
                        act.activation(diag[:, m % 3, :], ident, ACT.Copy, scale=coef[:, bass.ds(i * ROWS + k, 1)]).then_inc(diag_ready, 1)

            act.wait_ge(loaded, 16 * NLOADS)
            act.activation(cact[:], cact[:], ACT.Silu).then_inc(c_ready, 1)
            move("ada0")
            norm(0)
            move_turned()
            move("in0")
            mlstm()
            head_norms("moba")
            attention("moba")
            move_turned()
            move("out0")
            for l in range(2):
                norm(2 * l + 1)
                move_turned()
                move(f"wq{l}")
                peer(l)
                if l == 0:
                    move("ada1", ADA_LATE)
                peer_coef(l, 0)
                peer_coef(l, 1)
                norm(2 * l + 2)
                move_turned()
                if l == 0:
                    act.wait_ge(lam_s, 1)
                    act.activation(small[:, 42:44], small[:, 40:42], ACT.Exp).then_inc(lam_e, 1)
                    move("in1")
                    head_norms("diff")
                    attention("diff")
                    act.wait_ge(hn_sq, 2)
                    act.activation(small[:, 0:16], small[:, 0:16], ACT.Sqrt).then_inc(hn_rt, 1)
                    move_turned()
                    move("out1")
            move("mem")
            norm(5)
            move_turned()
            move("in2")
            head_norms("block2")
            attention("block2")
            move_turned()
            move("out2")
            norm(6)
            move_turned()
            act.wait_ge(r_pre, 1)
            act.activation(route[:, 128:136], route[:, 128:136], ACT.Exp).then_inc(r_exp, 1)
            act.wait_ge(r_pre, 2)
            act.activation(route[:, 136:138], route[:, 136:138], ACT.Exp).then_inc(r_exp, 1)

            def expert(e2, i):
                for b in range(2):
                    act.wait_ge(e_up, i * 8 + (4 * e2 + b + 1))
                    if not (isinstance(i, int) and e2 == 0):
                        act.wait_ge(e_act, i * 4 + (2 * e2 + b - 1))
                    act.activation(uT[:, 2 * b:2 * b + 2, :], sp_[:, b, :].rearrange("p (c n) -> p c n", c=2),
                                   ACT.Silu).then_inc(e_sig, 1)

            def move_pair(p):
                act.wait_ge(gath_done, p + 1)
                act.activation(xe, op[:, :, :].rearrange("p b (k n) -> p (b k) n", n=P), ACT.Copy).then_inc(xe_moved, 1)

            def silu(p):
                act.wait_ge(up_done, p * 2 + 2)
                act.activation(hid_rows, gp[:, 0, :], ACT.Silu).then_inc(up_silu, 1)

            def move_hidden(p):
                act.wait_ge(hid_turned, p + 1)
                act.activation(hid, gp[:, 0, :].rearrange("p (f n) -> p f n", f=4), ACT.Copy).then_inc(hid_moved, 1)

            def move_sel(p):
                for t in range(T):
                    act.wait_ge(selt_done, p * 2 + (t + 1))
                    act.activation(selT[:, t, :], tp[:, t, 0:P], ACT.Copy).then_inc(selt_moved, 1)

            def move_down(p):
                act.wait_ge(down_done, p + 1)
                act.activation(eout, sp_[:, :, :].rearrange("p b n -> p (b n)"), ACT.Copy).then_inc(down_moved, 1)

            act.wait_ge(flag_ready, 1)
            move_pair(0)
            silu(0)
            move_sel(0)
            move_hidden(0)
            move_pair(1)
            move_down(0)
            with act.Fori(1, N_EXP // 2 - 1) as p:
                silu(p)
                move_sel(p)
                move_hidden(p)
                move_pair(p + 1)
                move_down(p)
            last = N_EXP // 2 - 1
            silu(last)
            move_sel(last)
            move_hidden(last)
            move_down(last)
            with act.If(act.value_load(flag[0:1, 0:1], min_val=0, max_val=2 * S) > 0):
                expert(0, 0)
                expert(1, 0)
                with act.Fori(1, N_EXP // 2) as i:
                    expert(0, i)
                    expert(1, i)

        @block.vector
        def _(v):
            own = [0]

            def link(ins):
                own[0] += 1
                ins.then_inc(dve, 1)
                v.wait_ge(dve, own[0])

            def norm(n, src, sc=None, sh=None):
                dst = h if NORMS[n] != "mem" else y
                for t in range(T):
                    link(v.tensor_tensor_reduce(h[:, t, :], src[:, t, :], src[:, t, :], 1.0, 0.0, ALU.mult, ALU.add,
                                                small[:, 60 + t:61 + t]))
                v.tensor_scalar(small[:, 60:62], small[:, 60:62], 1.0 / D, EPS, ALU.mult, ALU.add).then_inc(sumsq, 1)
                v.wait_ge(rootd, n + 1)
                link(v.reciprocal(small[:, 58:60], small[:, 62:64]))
                v.wait_ge(gvec_in, 16 * (n + 1))
                for t in range(T):
                    ins = v.scalar_tensor_tensor(out=dst[:, t, :], in0=src[:, t, :], scalar=small[:, 58 + t:59 + t],
                                                 in1=gvec[:], op0=ALU.mult, op1=ALU.mult)
                    ins.then_inc(gvec_used, 1)
                    if sc is None:
                        v.wait_ge(gvec_used, T * n + t + 1)
                        v.sem_inc(h_ready, 1)
                        continue
                    v.wait_ge(gvec_used, T * n + t + 1)
                    link(v.scalar_tensor_tensor(out=h[:, t, :], in0=sc, scalar=1.0, in1=h[:, t, :], op0=ALU.add, op1=ALU.mult))
                    v.tensor_tensor(h[:, t, :], h[:, t, :], sh, ALU.add).then_inc(h_ready, 1)

            def modrow(i):
                return mod[:, i * D:(i + 1) * D]

            def head_norms(stage_name):
                q = QK[stage_name]
                n0 = qk_base[stage_name]
                b0 = qk_bank[stage_name]
                for b in range(len(q) // 4):
                    v.wait_ge(qk_root, b0 + b + 1)
                    v.reciprocal(norm_scale(b), norm_scale(b)).then_inc(qk_inv, 1)
                for i, (c, g) in enumerate(q):
                    v.wait_ge(qk_spread, n0 + i + 1)
                    v.scalar_tensor_tensor(out=zt2(c), in0=zt2(c), scalar=gains[:, g:g + 1], in1=tp[:, i % 2, :],
                                           op0=ALU.mult, op1=ALU.mult).then_inc(qk_done, 1)

            def attention(stage_name):
                units, segs = att[stage_name]
                b0 = seg_base[stage_name]
                u0 = unit_base[stage_name]
                for j in range(len(segs) + LAG + 2):
                    if j < len(segs):
                        sg = segs[j]
                        nk = sg["nk"]
                        dst = segbuf[:, j % SEGS, 0:nk]
                        sc = sp_[:, j % 2, 0:nk]
                        v.wait_ge(s_done, b0 + j + 1)
                        if j >= SEGS:
                            v.wait_ge(t_done, b0 + j - SEGS + 1)
                        if sg["bias"][0] == "alibi":
                            ins = v.scalar_tensor_tensor(out=dst, in0=sg["bias"][1], scalar=sg["bias"][2], in1=sc,
                                                         op0=ALU.mult, op1=ALU.add)
                        elif sg["bias"][0] == "add":
                            ins = v.tensor_tensor(dst, sg["bias"][1], sc, ALU.add)
                        else:
                            ins = v.tensor_copy(dst, sc)
                        ins.then_inc(s_read, 1)
                        if sg["last"]:
                            u = sg["u"]
                            n = units[u]["n"]
                            r = (j - n + 1) % SEGS
                            v.wait_ge(s_read, b0 + j + 1)
                            v.tensor_reduce(nmax[:, u % 8:u % 8 + 1], work[:, r * S:r * S + (n - 1) * S + nk], AX.X, ALU.max,
                                            negate=True).then_inc(m_done, 1)
                    i = j - LAG - 2
                    if i >= 0 and segs[i]["last"]:
                        u = segs[i]["u"]
                        un = units[u]
                        dv = segs[i]["dv"]
                        o = op[:, u % 2, 0:dv]
                        dst = y[:, un["t"], un["out"]:un["out"] + dv]
                        d = den[:, u % 8:u % 8 + 1]
                        link(v.reciprocal(d, d))
                        v.wait_ge(o_done, b0 + i + 1)
                        if un["tag"] == 1:
                            link(v.tensor_tensor(d, d, small[:, 44:45], ALU.mult))
                            v.wait_ge(o_read, u0 + u)
                            v.scalar_tensor_tensor(out=dst, in0=o, scalar=d, in1=dst, op0=ALU.mult,
                                                   op1=ALU.add).then_inc(o_read, 1)
                        else:
                            v.tensor_scalar(dst, o, d, None, ALU.mult).then_inc(o_read, 1)
                v.wait_ge(o_read, u0 + len(units))

            def mlstm():
                v.wait_ge(mem_in, 16)
                link(v.memset(ONE_, 1.0))

                def convolve(c):
                    acc = work[:, (c % SEGS) * S:(c % SEGS + 1) * S]
                    if c >= SEGS:
                        v.wait_ge(silu_done, c - SEGS + 1)
                    link(v.tensor_scalar(acc, zt(c), convw[:, c, 3:4], None, ALU.mult))
                    for tap in (2, 1, 0):
                        s = 3 - tap
                        ins = v.scalar_tensor_tensor(out=acc[:, s:S], in0=zt(c)[:, 0:S - s], scalar=convw[:, c, tap:tap + 1],
                                                     in1=acc[:, s:S], op0=ALU.mult, op1=ALU.add)
                        if tap:
                            link(ins)
                    ins.then_inc(conv_done, 1)

                for c in range(3):
                    convolve(c)
                v.wait_ge(gates_f, 1)
                v.scalar_tensor_tensor(out=A_, in0=F_, scalar=-1.0, in1=F_, op0=ALU.mult, op1=ALU.max).then_inc(gates_e, 1)
                v.wait_ge(gates_l, 1)
                link(v.scalar_tensor_tensor(out=A_, in0=F_, scalar=0.0, in1=E_, op0=ALU.min, op1=ALU.subtract))
                link(v.tensor_tensor_scan(B_, ONE_, A_, 0.0, ALU.mult, ALU.add))
                link(v.tensor_tensor(G_, I_, B_, ALU.subtract))
                link(v.tensor_tensor_scan(NM_, ONE_, G_, 0.0, ALU.mult, ALU.max))
                v.tensor_tensor(EM_, B_, NM_, ALU.add).then_inc(gates_e, 1)
                link(v.tensor_scalar(NM_, NM_, -1.0, None, ALU.mult))
                v.wait_ge(em_ready, 1)
                v.sem_inc(gates_g, 1)
                for c in range(3, 8):
                    convolve(c)
                v.wait_ge(gates_c, 1)

                def log_weights(hh):
                    arg = ml_arg[:, hh % 2, :]
                    v.wait_ge(mm_b, hh + 1)
                    v.tensor_tensor(arg[:, 0:S], maskT, tp[:, hh % 2, 0:S], ALU.add)
                    v.tensor_tensor(arg[:, S:S + P], maskT[:, 0:P], tp[:, hh % 2, P:S], ALU.add).then_inc(mm_arg, 1)

                log_weights(0)
                for hh in range(M_HEADS):
                    arg = ml_arg[:, hh % 2, :]
                    pt = ml_p[:, hh % 2, :]
                    if hh + 1 < M_HEADS:
                        log_weights(hh + 1)
                    v.wait_ge(mm_exp, hh + 1)
                    v.wait_ge(mm_s, hh + 1)
                    if hh >= 2:
                        v.wait_ge(mm_o, hh - 1)
                    v.scalar_tensor_tensor(out=pt, in0=sp_[:, hh % 2, 0:384], scalar=M_DH ** -0.5, in1=arg,
                                           op0=ALU.mult, op1=ALU.mult).then_inc(mm_p, 1)
                    v.wait_ge(mm_o, hh + 1)
                    o = op[:, hh % 2, :]
                    d = small[:, 50:52]
                    link(v.tensor_scalar(small[:, 52:54], o[:, S:S + 2], -1.0, None, ALU.mult))
                    link(v.tensor_tensor(d, small[:, 52:54], o[:, S:S + 2], ALU.max))
                    link(v.tensor_tensor(d, d, ml_cols[:, 1, :, hh], ALU.max))
                    link(v.reciprocal(d, d))
                    for t in range(T):
                        ins = v.tensor_scalar(y[:, t, P * hh:P * (hh + 1)], o[:, t * P:(t + 1) * P], d[:, t:t + 1], None, ALU.mult)
                        link(ins)
                    v.sem_inc(mm_read, 1)
                yh = y[:, :, 0:512].rearrange("p t (h n) -> p t h n", h=M_HEADS)
                sq = h[:, :, 0:512].rearrange("p t (h n) -> p t h n", h=M_HEADS)
                rms_heads(yh, sq, 24, 32, M_HEADS, M_DH, 1)
                r = small[:, 32:40].rearrange("p (t h) -> p t h", t=T)
                v.wait_ge(sig_done, 1)
                for t in range(T):
                    link(v.tensor_tensor(yh[:, t], yh[:, t], r[:, t, :].unsqueeze(2).to_broadcast([P, M_HEADS, M_DH]), ALU.mult))
                    link(v.tensor_tensor(y[:, t, 0:512], y[:, t, 0:512], mnorm, ALU.mult))
                    link(v.tensor_tensor(y[:, t, 0:512], y[:, t, 0:512], mo_sig[:, t, :], ALU.mult))

            def rms_heads(yh, sq, c0, c1, nh, dh, n):
                for t in range(T):
                    link(v.tensor_tensor(sq[:, t], yh[:, t], yh[:, t], ALU.mult))
                    link(v.tensor_reduce(small[:, c0 + t * nh:c0 + (t + 1) * nh], sq[:, t], AX.X, ALU.add))
                v.tensor_scalar(small[:, c0:c0 + T * nh], small[:, c0:c0 + T * nh], 1.0 / dh, EPS, ALU.mult, ALU.add).then_inc(hn_sq, 1)
                v.wait_ge(hn_rt, n)
                link(v.reciprocal(small[:, c1:c1 + T * nh], small[:, c1:c1 + T * nh]))

            def residual(g, name, n):
                v.wait_ge(gemm_moved, last_group[name])
                for t in range(T):
                    if g is None:
                        v.tensor_tensor(x[:, t, :], x[:, t, :], y[:, t, :], ALU.add).then_inc(x_ready, 1)
                        continue
                    link(v.tensor_tensor(y[:, t, :], y[:, t, :], g, ALU.mult))
                    v.tensor_tensor(x[:, t, :], x[:, t, :], y[:, t, :], ALU.add).then_inc(x_ready, 1)
                v.wait_ge(x_ready, n)

            def best_two_rounds(rows, best, where):
                for r in range(2):
                    part = slice(8 * r, 8 * r + 8)
                    for s, b in zip(rows, best):
                        ins = v.max(b[:, part], s)
                    link(ins)
                    for s, b, w in zip(rows, best, where):
                        ins = v.max_index(w[:, part], b[:, part], s)
                    link(ins)
                    if r == 0:
                        for s, b in zip(rows, best):
                            ins = v.match_replace(s, b[:, part], s, -3e38)
                        link(ins)

            def topk(l, t):
                v.wait_ge(sub_moved, 4 * (2 * l + t + 1))
                cols = range(2 * PEER_H)
                best_two_rounds([sub[:, c, :] for c in cols], [top[:, c, :] for c in cols], [topi[:, c, :] for c in cols])
                v.sem_inc(sub_free, 1)
                heads = range(PEER_H)
                v.tensor_copy(topf, topi)
                for hh in heads:
                    ins = v.tensor_tensor(cand[:, hh, :].rearrange("p (i j) -> p i j", i=TOPK),
                                          top[:, 2 * hh, :].unsqueeze(2).to_broadcast([P, TOPK, TOPK]),
                                          top[:, 2 * hh + 1, :].unsqueeze(1).to_broadcast([P, TOPK, TOPK]), ALU.add)
                link(ins)
                best_two_rounds([cand[:, hh, :] for hh in heads], [score[:, hh, :] for hh in heads], [pos[:, hh, :] for hh in heads])
                gt = gate[:, t, :].rearrange("p (h k) -> p h k", h=PEER_H)
                v.tensor_tensor(gt, score, score[:, :, 0:1].to_broadcast([P, PEER_H, TOPK]), ALU.subtract).then_inc(top_ready, 1)
                posf = pos.rearrange("p h k -> p (h k)")
                hi = cand[:, 0, 0:SLOTS].bitcast(U32)
                lo = cand[:, 1, 0:SLOTS].bitcast(U32)
                v.tensor_scalar(hi, posf, 4, None, ALU.logical_shift_right)
                link(v.tensor_scalar(lo, posf, 15, None, ALU.bitwise_and))
                num = []
                for c, part in enumerate((hi, lo)):
                    pf = cand[:, 2 + c, 0:SLOTS]
                    link(v.tensor_copy(pf, part))
                    link(v.tensor_tensor(hot, pf.unsqueeze(2).to_broadcast([P, SLOTS, TOPK]),
                                         iota.unsqueeze(1).to_broadcast([P, SLOTS, TOPK]), ALU.is_equal))
                    for hh in range(PEER_H):
                        ins = v.tensor_tensor(hot[:, TOPK * hh:TOPK * (hh + 1), :], hot[:, TOPK * hh:TOPK * (hh + 1), :],
                                              topf[:, 2 * hh + c, :].unsqueeze(1).to_broadcast([P, TOPK, TOPK]), ALU.mult)
                    link(ins)
                    nf = cand[:, 4 + c, 0:SLOTS]
                    link(v.tensor_reduce(nf, hot, AX.X, ALU.add))
                    num.append(nf)
                link(v.tensor_scalar(num[0], num[0], float(NKEYS), float(l * PEER_N), ALU.mult, ALU.add))
                link(v.tensor_tensor(num[0], num[0], num[1], ALU.add))
                v.tensor_copy(idx[:, t, :], num[0]).then_inc(idx_ready, 1)
                v.wait_ge(idx_ready, 2 * l + t + 1)

            def gates_norm(l, t):
                gt = gate[:, t, :].rearrange("p (h k) -> p h k", h=PEER_H)
                v.wait_ge(gate_e, 2 * l + t + 1)
                link(v.tensor_reduce(small[:, 0:8], gt, AX.X, ALU.add))
                link(v.reciprocal(small[:, 8:16], small[:, 0:8]))
                link(v.tensor_tensor(gt, gt, small[:, 8:16].unsqueeze(2).to_broadcast([P, PEER_H, TOPK]), ALU.mult))

            def peer_dots(l, t):
                n = 2 * l + t
                phase = 4 * l + 2 * t
                base = n * SLOTS
                with v.Fori(0, GROUPS) as i:
                    for k in range(ROWS):
                        v.wait_ge(row_in[k], i * 16 + 16 * (phase * GROUPS + 1))
                        v.tensor_tensor_reduce(y[:, 0, :], rowbuf[:, k, :], h[:, t, :], 1.0, 0.0, ALU.mult, ALU.add,
                                               dots8[:, k:k + 1]).then_inc(udot, 1)
                        v.wait_ge(udot, i * ROWS + (base + k + 1))
                    v.tensor_copy(dots[:, bass.ds(i * ROWS, ROWS)], dots8[:]).then_inc(hn_dots, 1)
                    v.wait_ge(hn_dots, i + (n * GROUPS + 1))
                v.sem_inc(dots_all, 1)
                v.wait_ge(gelu_done, n + 1)
                v.tensor_tensor(coef[:], coef[:], gate[:, t, :], ALU.mult).then_inc(coef_ready, 1)

            def peer_share(l, t):
                n = 2 * l + t
                phase = 4 * l + 2 * t + 1
                f = SHARED[t]
                w = len(DVE_ROWS)
                base = dve_rows_before(n)
                v.wait_ge(coef_ready, n + 1)

                def add(i, k, col):
                    m = DVE_ROWS.index(k)
                    v.wait_ge(row_in[k], i * 16 + 16 * (phase * GROUPS + 1))
                    if isinstance(i, int) and m == 0:
                        v.tensor_scalar(y[:, 0, :], rowbuf[:, k, :], col, None, ALU.mult).then_inc(vshare, 1)
                        return
                    v.wait_ge(vshare, i * w + (base - w * f + m))
                    v.scalar_tensor_tensor(out=y[:, 0, :], in0=rowbuf[:, k, :], scalar=col, in1=y[:, 0, :],
                                           op0=ALU.mult, op1=ALU.add).then_inc(vshare, 1)

                for k in DVE_ROWS:
                    add(f, k, coef[:, f * ROWS + k:f * ROWS + k + 1])
                with v.Fori(f + 1, GROUPS) as i:
                    for k in DVE_ROWS:
                        add(i, k, coef[:, bass.ds(i * ROWS + k, 1)])
                v.wait_ge(vshare, dve_rows_before(n + 1))

            def peer_residual(l, t):
                v.wait_ge(vsum, pe_rows_before(2 * l + t + 1))
                for n in range(2):
                    ins = v.tensor_tensor(y[:, 0, n * 512:(n + 1) * 512], y[:, 0, n * 512:(n + 1) * 512], op[:, n, :], ALU.add)
                link(ins)
                link(v.tensor_tensor(y[:, 0, :], g2[:, l, :], y[:, 0, :], ALU.mult))
                v.tensor_tensor(x[:, t, :], x[:, t, :], y[:, 0, :], ALU.add).then_inc(x_ready, 1)
                v.wait_ge(x_ready, T * (2 * l + 1) + t + 1)

            v.memset(eps[:], EPS)
            v.wait_ge(loaded, 16 * NLOADS)
            link(v.memset(ones1[:], 1.0))
            for g in (G_EVQ, G_ODQ, G_NAQ, G_DLQ, G_MMQ):
                link(v.tensor_scalar(gains[:, g:g + 1], gains[:, g:g + 1], 0.125, None, ALU.mult))
            v.wait_ge(t5_in, 16 * (NA_HEADS + 3))
            v.wait_ge(t5_mm, 1)
            for g in range(DIL_GROUPS):
                ins = v.tensor_tensor(t5_out[:, g * TW:(g + 1) * TW], t5_mask[:, g * TW:(g + 1) * TW],
                                      (sp_ if g < 2 else op)[0:DIL_HPG, g % 2, 0:TW], ALU.add)
                link(ins)
            v.sem_inc(t5_sum, 1)

            v.wait_ge(gemm_moved, last_group["ada0"])
            norm(0, x, modrow(1), modrow(0))
            v.wait_ge(gemm_moved, last_group["in0"])
            mlstm()
            head_norms("moba")
            attention("moba")
            v.sem_inc(y_ready, 1)
            residual(modrow(2), "out0", T)
            for l in range(2):
                norm(2 * l + 1, x, modrow(4), modrow(3))
                v.wait_ge(keys_m, l + 1)
                topk(l, 0)
                gates_norm(l, 0)
                peer_dots(l, 0)
                topk(l, 1)
                gates_norm(l, 1)
                peer_share(l, 0)
                peer_residual(l, 0)
                peer_dots(l, 1)
                peer_share(l, 1)
                peer_residual(l, 1)
                if l == 0:
                    v.wait_ge(gemm_moved, last_group["ada1"])
                    norm(2, x, modrow(1), modrow(0))
                    v.wait_ge(lam_in, 32)
                    for c in range(2):
                        link(v.tensor_tensor_reduce(y[:, 0, 0:64], lam_rows[:, 2 * c, :], lam_rows[:, 2 * c + 1, :], 1.0, 0.0,
                                                    ALU.mult, ALU.add, small[:, 40 + c:41 + c]))
                    v.sem_inc(lam_s, 1)
                    v.wait_ge(lam_e, 1)
                    link(v.tensor_tensor(small[:, 44:45], small[:, 43:44], small[:, 42:43], ALU.subtract))
                    link(v.tensor_scalar(small[:, 44:45], small[:, 44:45], -LAM_INIT, None, ALU.add))
                    v.wait_ge(gemm_moved, last_group["in1"])
                    head_norms("diff")
                    attention("diff")
                    yh = y[:, :, :].rearrange("p t (h n) -> p t h n", h=C_HEADS)
                    sq = h[:, :, :].rearrange("p t (h n) -> p t h n", h=C_HEADS)
                    rms_heads(yh, sq, 0, 0, C_HEADS, P, 2)
                    r = small[:, 0:16].rearrange("p (t h) -> p t h", t=T)
                    for t in range(T):
                        link(v.tensor_tensor(yh[:, t], yh[:, t], r[:, t, :].unsqueeze(2).to_broadcast([P, C_HEADS, P]), ALU.mult))
                        link(v.tensor_tensor(yh[:, t], yh[:, t], onorm.unsqueeze(1).to_broadcast([P, C_HEADS, P]), ALU.mult))
                        link(v.tensor_scalar(y[:, t, :], y[:, t, :], 1.0 - LAM_INIT, None, ALU.mult))
                    v.sem_inc(y_ready, 1)
                    residual(modrow(2), "out1", T * 3)
            v.wait_ge(mem_in, 32)
            norm(4, y)
            norm(5, x)
            v.wait_ge(bias_in, 16 * 17)
            for hh in range(NA_HEADS):
                nb = na_bias[:, hh, :].rearrange("p (j n) -> p j n", j=6)
                ins = v.tensor_tensor(nb, nb, na_mask.unsqueeze(1).to_broadcast([P, 6, GRID_W]), ALU.add)
            link(ins)
            v.wait_ge(gemm_moved, last_group["in2"])
            head_norms("block2")
            attention("block2")
            v.sem_inc(y_ready, 1)
            residual(None, "out2", T * 5)
            norm(6, x)

            link(v.memset(gvec[:, 0:2 * P], 1.0))
            link(v.memset(earlier[:, 0:1], 0.0))
            link(v.tensor_scalar(earlier[:, 1:P], maskT[:, 0:P - 1], 0.0, None, ALU.is_equal))
            v.wait_ge(r_mm, 1)
            v.wait_ge(r_in, 32)
            gl8 = route[:, 0:16].rearrange("p (t n) -> p t n", t=T)
            fine = route[:, 16:80].rearrange("p (t n) -> p t n", t=T)
            gm = route[:, 80:96].rearrange("p (t n) -> p t n", t=T)
            fsel = route[:, 96:112].rearrange("p (t n) -> p t n", t=T)
            fm = route[:, 112:128].rearrange("p (t n) -> p t n", t=T)
            ge = route[:, 128:136].rearrange("p (t n) -> p t n", t=T)
            p1 = route[:, 136:138]
            gsum = route[:, 138:140]
            oh = route[:, 140:148].rearrange("p (t n) -> p t n", t=T)
            fi = route[:, 148:152].rearrange("p (t n) -> p t n", t=T)
            tmp = route[:, 152:216].rearrange("p (t g n) -> p t g n", t=T, g=N_GRP)
            w8 = route[:, 216:232].rearrange("p (t n) -> p t n", t=T)
            gg = route[:, 232:236].rearrange("p (t n) -> p t n", t=T)
            gi = route[:, 236:238]
            link(v.memset(route[:, 0:16], NEG))
            for t in range(T):
                link(v.tensor_tensor(gl8[:, t, 0:4], rbias[:, 0:4], op[:, t, 0:4], ALU.add))
                link(v.tensor_tensor(fine[:, t, :], rbias[:, 4:36], op[:, t, 4:36], ALU.add))
                link(v.max(gm[:, t, :], gl8[:, t, :]))
                link(v.max_index(route_u[:, 0:8], gm[:, t, :], gl8[:, t, :]))
                link(v.tensor_copy(gi[:, t:t + 1], route_u[:, 0:1]))
                link(v.tensor_scalar(ge[:, t, :], gl8[:, t, 0:4], gm[:, t, 0:1], None, ALU.subtract))
                link(v.tensor_scalar(oh[:, t, :], iota[:, 0:4], gi[:, t:t + 1], None, ALU.is_equal))
                link(v.tensor_tensor(tmp[:, t], fine[:, t, :].rearrange("p (g n) -> p g n", g=N_GRP),
                                     oh[:, t, :].unsqueeze(2).to_broadcast([P, N_GRP, PER_GRP]), ALU.mult))
                link(v.tensor_reduce(fsel[:, t, :], tmp[:, t].rearrange("p g n -> p n g"), AX.X, ALU.add))
                link(v.max(fm[:, t, :], fsel[:, t, :]))
                link(v.max_index(route_u[:, 8:16], fm[:, t, :], fsel[:, t, :]))
                link(v.tensor_copy(fi[:, t, :], route_u[:, 8:10]))
                link(v.tensor_tensor(p1[:, t:t + 1], fm[:, t, 1:2], fm[:, t, 0:1], ALU.subtract))
            v.sem_inc(r_pre, 2)
            v.wait_ge(r_exp, 2)
            link(v.tensor_reduce(gsum, ge, AX.X, ALU.add))
            for t in range(T):
                link(v.tensor_scalar(gg[:, t, 0:1], p1[:, t:t + 1], 1.0, gsum[:, t:t + 1], ALU.add, ALU.mult))
                link(v.reciprocal(gg[:, t, 0:1], gg[:, t, 0:1]))
                link(v.tensor_tensor(gg[:, t, 1:2], gg[:, t, 0:1], p1[:, t:t + 1], ALU.mult))
                link(v.tensor_scalar(w8[:, t, :], iota[:, 0:8], fi[:, t, 0:1], gg[:, t, 0:1], ALU.is_equal, ALU.mult))
                link(v.tensor_scalar(fm[:, t, :], iota[:, 0:8], fi[:, t, 1:2], gg[:, t, 1:2], ALU.is_equal, ALU.mult))
                link(v.tensor_tensor(w8[:, t, :], w8[:, t, :], fm[:, t, :], ALU.add))
                link(v.tensor_scalar(fsel[:, t, :], iota[:, 0:8], fi[:, t, 0:1], None, ALU.is_equal))
                link(v.tensor_scalar(fm[:, t, :], iota[:, 0:8], fi[:, t, 1:2], None, ALU.is_equal))
                link(v.tensor_tensor(fm[:, t, :], fsel[:, t, :], fm[:, t, :], ALU.add))
                link(v.tensor_tensor(picked[:, t, :].rearrange("p (g n) -> p g n", g=N_GRP),
                                     oh[:, t, :].unsqueeze(2).to_broadcast([P, N_GRP, PER_GRP]),
                                     fm[:, t, :].unsqueeze(1).to_broadcast([P, N_GRP, PER_GRP]), ALU.mult))
                link(v.tensor_tensor(w_gate[:, t, :].rearrange("p (g n) -> p g n", g=N_GRP),
                                     oh[:, t, :].unsqueeze(2).to_broadcast([P, N_GRP, PER_GRP]),
                                     w8[:, t, :].unsqueeze(1).to_broadcast([P, N_GRP, PER_GRP]), ALU.mult))
            v.sem_inc(r_done, 1)
            v.wait_ge(rank_done, 1)
            flat = [q.rearrange("p t n -> p (t n)") for q in (rank, below, picked, w_gate, w_over)]
            link(v.tensor_copy(flat[0], tp[:, 0, 0:2 * N_EXP]))
            link(v.tensor_scalar(flat[1], flat[0], float(FULL), None, ALU.is_lt))
            link(v.tensor_tensor(flat[4], flat[3], flat[1], ALU.mult))
            link(v.tensor_tensor(route[:, 0:64], flat[2], flat[1], ALU.mult))
            link(v.tensor_tensor(route[:, 64:128], flat[2], route[:, 0:64], ALU.subtract))
            v.tensor_reduce(over[:, 0:1], route[:, 64:128], AX.X, ALU.add).then_inc(over_ready, 1)
            v.wait_ge(over_sum, 1)
            link(v.tensor_copy(flag, tp[:, 1, 0:1]))
            link(v.tensor_tensor(route[:, 128:192], flat[3], flat[4], ALU.subtract))
            link(v.tensor_copy(flat[3], flat[4]))
            link(v.tensor_copy(flat[4], route[:, 128:192]))
            link(v.tensor_copy(flat[2], route[:, 0:64]))
            v.sem_inc(flag_ready, 1)

            def select(p):
                for e2 in range(2):
                    for t in range(T):
                        def at(q):
                            return q[:, t, p * 2 + e2:p * 2 + e2 + 1] if isinstance(p, int) else q[:, t, bass.ds(p * 2 + e2, 1)]
                        c = slice(e2 * CAP, (e2 + 1) * CAP)
                        v.tensor_scalar(sel[:, t, c], iota64, at(rank), at(picked), ALU.is_equal, ALU.mult)
                        ins = v.tensor_scalar(selg[:, t, c], iota64, at(rank), at(w_gate), ALU.is_equal, ALU.mult)
                ins.then_inc(sel_ready, 1)

            def take_up(p):
                v.wait_ge(up_silu, p + 1)
                v.tensor_tensor(hid_rows, hid_rows, gp[:, 1, :], ALU.mult).then_inc(up_act, 1)

            def add_pair(p):
                for n in range(4):
                    v.wait_ge(scat_done, p * 4 + (n + 1))
                    acc = x[:, n // 2, (n % 2) * 512:(n % 2 + 1) * 512]
                    v.tensor_tensor(acc, acc, tp[:, n % 2, :], ALU.add).then_inc(scat_read, 1)

            def next_select(p):
                v.wait_ge(gath_done, p)
                v.wait_ge(selt_done, p * 2)
                select(p)

            select(0)
            take_up(0)
            next_select(1)
            with v.Fori(1, N_EXP // 2 - 1) as p:
                take_up(p)
                add_pair(p - 1)
                next_select(p + 1)
            last = N_EXP // 2 - 1
            take_up(last)
            add_pair(last - 1)
            add_pair(last)

            def expert(e2, i):
                for b in range(2):
                    v.wait_ge(e_sig, i * 4 + (2 * e2 + b + 1))
                    v.wait_ge(e_up, i * 8 + (4 * e2 + 2 + b + 1))
                    if not (isinstance(i, int) and e2 == 0) and b == 0:
                        v.wait_ge(e_down, i * 8 + 4 * e2)
                    v.tensor_tensor(aT[:, 2 * b:2 * b + 2, :], uT[:, 2 * b:2 * b + 2, :],
                                    gp[:, b, :].rearrange("p (c n) -> p c n", c=2), ALU.mult).then_inc(e_act, 1)
                for t in range(T):
                    if isinstance(i, int):
                        col = w_over[:, t, e2:e2 + 1]
                    else:
                        col = w_over[:, t, bass.ds(i * 2 + e2, 1)]
                    for n in range(2):
                        v.wait_ge(e_down, i * 8 + (4 * e2 + 2 * t + n + 1))
                        bank = (tp if t == 0 else op)[:, n, :]
                        acc = x[:, t, n * 512:(n + 1) * 512]
                        v.scalar_tensor_tensor(out=acc, in0=bank, scalar=col, in1=acc, op0=ALU.mult, op1=ALU.add).then_inc(e_acc, 1)

            v.wait_ge(scat_read, 2 * N_EXP)
            with v.If(v.value_load(flag[0:1, 0:1], min_val=0, max_val=2 * S) > 0):
                expert(0, 0)
                v.wait_ge(e_acc, 4)
                expert(1, 0)
                with v.Fori(1, N_EXP // 2) as i:
                    v.wait_ge(e_acc, i * 8)
                    expert(0, i)
                    v.wait_ge(e_acc, i * 8 + 4)
                    expert(1, i)
                v.wait_ge(e_acc, 4 * N_EXP)
            v.sem_inc(x_ready, T)


_INS = ["x", "c", "ada_w", "ada_b", "norm_mix_g", "norm_ffn_g", "ev_w_in", "ev_igate_b", "ev_fgate_b", "ev_mnorm_g",
        "ev_w_out", "od_w_in", "od_lam", "od_onorm_g", "od_w_out", "peer_wq", "peer_keys", "peer_u", "peer_v", "mem_2",
        "g_mix_2", "w_in_2", "na_rpb_2", "t5_table_2", "g_mem_2", "w_mem_kv_2", "w_out_2", "g_ffn_2", "w_r1_2", "b_r1_2",
        "w_r2_2", "b_r2_2", "w1_2", "w3_2", "w2_2"]


def kernel(**inputs):
    import numpy as _np
    import concourse.bacc as _bacc
    from concourse import mybir as _mybir
    from concourse.bass_utils import run_bass_kernel_spmd as _run

    nc = _bacc.Bacc("TRN2", target_bir_lowering=False, num_devices=1)
    arrays, args = {}, {}

    def give(name, a):
        a = _np.ascontiguousarray(a)
        arrays[f"in_{name}_dram"] = a
        args[name] = nc.dram_tensor(f"in_{name}_dram", a.shape, _mybir.dt.from_np(a.dtype), kind="ExternalInput").ap()

    for name in _INS:
        give(name, inputs[name])
    cst, hot, dmask = shape_constants()
    give("cst", cst)
    give("t5_hot", hot)
    give("t5_mask", dmask)
    qk = _np.asarray(inputs["qk_gain_2"])[0].reshape(6, 64)
    cols = [_np.asarray(inputs[k])[0] for k in ("ev_qn_g", "ev_kn_g", "od_qn_g", "od_kn_g")] + list(qk)
    col = _np.stack(cols, axis=1)
    give("gains", _np.concatenate([col, col], axis=0))
    give("conv_cols", _np.asarray(inputs["ev_conv_w"])[0].reshape(4, 8, 128).transpose(2, 1, 0))
    out = nc.dram_tensor("out_0_dram", (1, S, D), _mybir.dt.float32, kind="ExternalOutput").ap()
    program(nc, args, out)
    r = _run(nc, [arrays], core_ids=[0])
    return r.results[0]["out_0_dram"]
```
